# Optimizing a Trainium2 kernel written in Bass

```python
import math
import jax, jax.numpy as jnp
from jax import lax
import numpy as np

D_MODEL = 1024
BATCH = 1
SEQ = 512
DEPTH = 1

CHUNK = 64
EPS = 1e-6
D_MIX = D_MODEL
CONV_K = 4

SSD_HEADS = 8
SSD_HEAD_DIM = 64
SSD_DIM = SSD_HEADS * SSD_HEAD_DIM
SSD_GROUPS = 2
SSD_STATE = 128
SSD_CONV_DIM = SSD_DIM + 2 * SSD_GROUPS * SSD_STATE

ATT_HEADS = 4
ATT_KV_HEADS = 2
ATT_HEAD_DIM = 64
ATT_DIM = ATT_HEADS * ATT_HEAD_DIM
ATT_KV_DIM = ATT_KV_HEADS * ATT_HEAD_DIM
WINDOW = 128
WIN_CHUNKS = WINDOW // CHUNK

GDN_HEADS = 4
GDN_HEAD_K = 64
GDN_HEAD_V = 64
GDN_KDIM = GDN_HEADS * GDN_HEAD_K
GDN_DIM = GDN_HEADS * GDN_HEAD_V
GDN_CONV_DIM = 2 * GDN_KDIM + GDN_DIM

FF = ((8 * D_MODEL // 3 + 255) // 256) * 256

IN_SIZES = (ATT_DIM, ATT_KV_DIM, ATT_KV_DIM,
            SSD_DIM, SSD_CONV_DIM, SSD_HEADS,
            GDN_CONV_DIM, GDN_DIM, GDN_HEADS, GDN_HEADS)
IN_COLS = sum(IN_SIZES)


def _offsets(sizes):
    out, acc = [], 0
    for s in sizes[:-1]:
        acc += s
        out.append(acc)
    return out

def rmsnorm(x, w):
    xf = x.astype(jnp.float32)
    y = xf * lax.rsqrt(jnp.mean(xf * xf, axis=-1, keepdims=True) + EPS)
    return (y * w.astype(jnp.float32)).astype(x.dtype)

def l2norm(x):
    return x * lax.rsqrt(jnp.sum(x * x, axis=-1, keepdims=True) + EPS)

def causal_dwconv(x, w, b=None):
    k = w.shape[0]
    t = x.shape[1]
    xp = jnp.pad(x, ((0, 0), (k - 1, 0), (0, 0)))
    y = xp[:, 0:t] * w[0]
    for i in range(1, k):
        y = y + xp[:, i:i + t] * w[i]
    if b is not None:
        y = y + b
    return y

def alibi_slopes(n):
    return 2.0 ** (-8.0 * jnp.arange(1, n + 1, dtype=jnp.float32) / n)

def lower_exp_diff(cs):
    n = cs.shape[-1]
    tril = jnp.tril(jnp.ones((n, n), dtype=bool))
    diff = cs[..., :, None] - cs[..., None, :]
    return jnp.where(tril, jnp.exp(jnp.where(tril, diff, 0.0)), 0.0)

def swa_sink_alibi(q, k, v, sinks):
    bsz, t = q.shape[0], q.shape[1]
    nc = t // CHUNK
    grp = ATT_HEADS // ATT_KV_HEADS
    band = (WIN_CHUNKS + 1) * CHUNK
    qc = q.reshape(bsz, nc, CHUNK, ATT_KV_HEADS, grp, ATT_HEAD_DIM)
    padw = ((0, 0), (WIN_CHUNKS * CHUNK, 0), (0, 0))
    kp = jnp.pad(k, padw).reshape(bsz, nc + WIN_CHUNKS, CHUNK, ATT_KV_HEADS, ATT_HEAD_DIM)
    vp = jnp.pad(v, padw).reshape(bsz, nc + WIN_CHUNKS, CHUNK, ATT_KV_HEADS, ATT_HEAD_DIM)
    kb = jnp.concatenate([kp[:, j:j + nc] for j in range(WIN_CHUNKS + 1)], axis=2)
    vb = jnp.concatenate([vp[:, j:j + nc] for j in range(WIN_CHUNKS + 1)], axis=2)
    s = jnp.einsum('bcikgd,bcjkd->bckgij', qc, kb).astype(jnp.float32) * (ATT_HEAD_DIM ** -0.5)
    qi = jnp.arange(CHUNK)[:, None]
    kj = jnp.arange(band)[None, :]
    dist = jnp.abs(qi + WIN_CHUNKS * CHUNK - kj).astype(jnp.float32)
    slopes = alibi_slopes(ATT_HEADS).reshape(ATT_KV_HEADS, grp)
    s = s - slopes[:, :, None, None] * dist
    key_chunk = jnp.arange(nc)[:, None] - WIN_CHUNKS + (jnp.arange(band) // CHUNK)[None, :]
    valid = key_chunk >= 0
    s = jnp.where(valid[None, :, None, None, None, :], s, -jnp.inf)
    sink = jnp.broadcast_to(sinks.astype(jnp.float32).reshape(1, 1, ATT_KV_HEADS, grp, 1, 1),
                            s.shape[:-1] + (1,))
    p = jax.nn.softmax(jnp.concatenate([s, sink], axis=-1), axis=-1)[..., :band]
    o = jnp.einsum('bckgij,bcjkd->bcikgd', p.astype(v.dtype), vb)
    return o.reshape(bsz, t, ATT_DIM)

def ssd_mixer(z, xbc, dt, conv_w, conv_b, dt_bias, a_log, d_skip, norm_w):
    bsz, t = xbc.shape[0], xbc.shape[1]
    nc = t // CHUNK
    hpg = SSD_HEADS // SSD_GROUPS
    xbc = jax.nn.silu(causal_dwconv(xbc, conv_w, conv_b)).astype(jnp.float32)
    xs, bm, cm = jnp.split(xbc, [SSD_DIM, SSD_DIM + SSD_GROUPS * SSD_STATE], axis=-1)
    xs = xs.reshape(bsz, t, SSD_HEADS, SSD_HEAD_DIM)
    bm = jnp.repeat(bm.reshape(bsz, t, SSD_GROUPS, SSD_STATE), hpg, axis=2)
    cm = jnp.repeat(cm.reshape(bsz, t, SSD_GROUPS, SSD_STATE), hpg, axis=2)
    dt = jax.nn.softplus(dt.astype(jnp.float32) + dt_bias.astype(jnp.float32))
    a = -jnp.exp(a_log.astype(jnp.float32))
    xc = (xs * dt[..., None]).reshape(bsz, nc, CHUNK, SSD_HEADS, SSD_HEAD_DIM)
    bc = bm.reshape(bsz, nc, CHUNK, SSD_HEADS, SSD_STATE)
    cc = cm.reshape(bsz, nc, CHUNK, SSD_HEADS, SSD_STATE)
    da = (dt * a).reshape(bsz, nc, CHUNK, SSD_HEADS).transpose(0, 3, 1, 2)
    a_cs = jnp.cumsum(da, axis=-1)
    lmat = lower_exp_diff(a_cs)
    scores = jnp.einsum('bclhn,bcshn->bhcls', cc, bc) * lmat
    y_diag = jnp.einsum('bhcls,bcshp->bclhp', scores, xc)
    decay_states = jnp.exp(a_cs[..., -1:] - a_cs)
    chunk_states = jnp.einsum('bclhn,bhcl,bclhp->bchpn', bc, decay_states, xc)
    chunk_decay = jnp.exp(a_cs[..., -1])

    def step(state, inp):
        new, dec = inp
        return state * dec[..., None, None] + new, state

    init = jnp.zeros((bsz, SSD_HEADS, SSD_HEAD_DIM, SSD_STATE), jnp.float32)
    _, prev = lax.scan(step, init, (chunk_states.transpose(1, 0, 2, 3, 4),
                                    chunk_decay.transpose(2, 0, 1)))
    prev = prev.transpose(1, 0, 2, 3, 4)
    y_off = jnp.einsum('bclhn,bchpn,bhcl->bclhp', cc, prev, jnp.exp(a_cs))
    y = (y_diag + y_off).reshape(bsz, t, SSD_HEADS, SSD_HEAD_DIM) + xs * d_skip.astype(jnp.float32)[:, None]
    g = y.reshape(bsz, t, SSD_DIM) * jax.nn.silu(z.astype(jnp.float32))
    g = g.reshape(bsz, t, SSD_GROUPS, SSD_DIM // SSD_GROUPS)
    g = g * lax.rsqrt(jnp.mean(g * g, axis=-1, keepdims=True) + EPS)
    return (g.reshape(bsz, t, SSD_DIM) * norm_w.astype(jnp.float32)).astype(z.dtype)

def gdn_mixer(qkv, z, b, a, conv_w, dt_bias, a_log, norm_w):
    bsz, t = qkv.shape[0], qkv.shape[1]
    nc = t // CHUNK
    qkv = jax.nn.silu(causal_dwconv(qkv, conv_w)).astype(jnp.float32)
    q, k, v = jnp.split(qkv, [GDN_KDIM, 2 * GDN_KDIM], axis=-1)
    q = l2norm(q.reshape(bsz, t, GDN_HEADS, GDN_HEAD_K)) * (GDN_HEAD_K ** -0.5)
    k = l2norm(k.reshape(bsz, t, GDN_HEADS, GDN_HEAD_K))
    v = v.reshape(bsz, t, GDN_HEADS, GDN_HEAD_V)
    beta = jax.nn.sigmoid(b.astype(jnp.float32))
    g = -jnp.exp(a_log.astype(jnp.float32)) * jax.nn.softplus(a.astype(jnp.float32) + dt_bias.astype(jnp.float32))

    def chunks(u):
        return u.reshape(bsz, nc, CHUNK, GDN_HEADS, u.shape[-1]).transpose(0, 3, 1, 2, 4)

    qc, kc, vc = chunks(q), chunks(k), chunks(v)
    betac = beta.reshape(bsz, nc, CHUNK, GDN_HEADS).transpose(0, 3, 1, 2)
    gc = jnp.cumsum(g.reshape(bsz, nc, CHUNK, GDN_HEADS).transpose(0, 3, 1, 2), axis=-1)
    decay = lower_exp_diff(gc)
    kbeta = kc * betac[..., None]
    strict = jnp.tril(jnp.einsum('bhcid,bhcjd->bhcij', kbeta, kc) * decay, -1)
    rhs = jnp.concatenate([vc * betac[..., None], kbeta * jnp.exp(gc)[..., None]], axis=-1)
    sol = lax.linalg.triangular_solve(strict, rhs, left_side=True, lower=True, unit_diagonal=True)
    u, w = jnp.split(sol, [GDN_HEAD_V], axis=-1)
    qk = jnp.einsum('bhcid,bhcjd->bhcij', qc, kc) * decay

    def step(state, inp):
        q_i, k_i, u_i, w_i, qk_i, g_i = inp
        v_new = u_i - jnp.einsum('bhld,bhde->bhle', w_i, state)
        o = (jnp.einsum('bhld,bhde->bhle', q_i * jnp.exp(g_i)[..., None], state)
             + jnp.einsum('bhls,bhse->bhle', qk_i, v_new))
        g_last = g_i[..., -1]
        state = (state * jnp.exp(g_last)[..., None, None]
                 + jnp.einsum('bhld,bhle->bhde', k_i * jnp.exp(g_last[..., None] - g_i)[..., None], v_new))
        return state, o

    xs = tuple(jnp.moveaxis(u_, 2, 0) for u_ in (qc, kc, u, w, qk, gc))
    init = jnp.zeros((bsz, GDN_HEADS, GDN_HEAD_K, GDN_HEAD_V), jnp.float32)
    _, o = lax.scan(step, init, xs)
    o = o.transpose(1, 0, 3, 2, 4).reshape(bsz, t, GDN_HEADS, GDN_HEAD_V)
    o = o * lax.rsqrt(jnp.mean(o * o, axis=-1, keepdims=True) + EPS) * norm_w.astype(jnp.float32)
    o = o * jax.nn.silu(z.astype(jnp.float32).reshape(bsz, t, GDN_HEADS, GDN_HEAD_V))
    return o.reshape(bsz, t, GDN_DIM).astype(z.dtype)

def first_inputs(seed: int = 0) -> dict:
    key = jax.random.key(seed)
    ks = jax.random.split(key, 24)
    L = DEPTH

    def nrm(k, shape, scale):
        return jax.random.normal(k, shape, jnp.float32) * scale

    def gain(k, shape):
        return 1.0 + 0.05 * jax.random.normal(k, shape, jnp.float32)

    def dt_bias_init(k, shape):
        u = jax.random.uniform(k, shape, jnp.float32, math.log(1e-3), math.log(1e-1))
        dtv = jnp.exp(u)
        return dtv + jnp.log(-jnp.expm1(-dtv))

    def a_log_init(k, shape):
        return jnp.log(jax.random.uniform(k, shape, jnp.float32, 1.0, 16.0))

    return {
        "x": nrm(ks[0], (BATCH, SEQ, D_MODEL), 1.0),
        "pre_mix_norm": gain(ks[1], (L, D_MODEL)),
        "post_mix_norm": gain(ks[2], (L, D_MODEL)),
        "pre_ffn_norm": gain(ks[3], (L, D_MODEL)),
        "post_ffn_norm": gain(ks[4], (L, D_MODEL)),
        "w_in": nrm(ks[5], (L, D_MODEL, IN_COLS), D_MODEL ** -0.5),
        "w_out": nrm(ks[6], (L, D_MIX, D_MODEL), D_MIX ** -0.5),
        "attn_sinks": nrm(ks[7], (L, ATT_HEADS), 0.5),
        "ssd_conv_w": nrm(ks[8], (L, CONV_K, SSD_CONV_DIM), CONV_K ** -0.5),
        "ssd_conv_b": nrm(ks[9], (L, SSD_CONV_DIM), 0.01),
        "ssd_dt_bias": dt_bias_init(ks[10], (L, SSD_HEADS)),
        "ssd_A_log": a_log_init(ks[11], (L, SSD_HEADS)),
        "ssd_D": 1.0 + 0.1 * jax.random.normal(ks[12], (L, SSD_HEADS), jnp.float32),
        "ssd_norm_w": gain(ks[13], (L, SSD_DIM)),
        "gdn_conv_w": nrm(ks[14], (L, CONV_K, GDN_CONV_DIM), CONV_K ** -0.5),
        "gdn_dt_bias": dt_bias_init(ks[15], (L, GDN_HEADS)),
        "gdn_A_log": a_log_init(ks[16], (L, GDN_HEADS)),
        "gdn_norm_w": gain(ks[17], (L, GDN_HEAD_V)),
        "ffn_w_gate": nrm(ks[18], (L, D_MODEL, FF), D_MODEL ** -0.5),
        "ffn_w_up": nrm(ks[19], (L, D_MODEL, FF), D_MODEL ** -0.5),
        "ffn_w_down": nrm(ks[20], (L, FF, D_MODEL), FF ** -0.5),
    }

def first_block(x, pre_mix_norm, post_mix_norm, pre_ffn_norm, post_ffn_norm, w_in, w_out,
              attn_sinks, ssd_conv_w, ssd_conv_b, ssd_dt_bias, ssd_A_log, ssd_D, ssd_norm_w,
              gdn_conv_w, gdn_dt_bias, gdn_A_log, gdn_norm_w, ffn_w_gate, ffn_w_up, ffn_w_down):
    offs = _offsets(IN_SIZES)
    for l in range(DEPTH):
        h = rmsnorm(x, pre_mix_norm[l])
        proj = h @ w_in[l]
        (a_q, a_k, a_v, s_z, s_xbc, s_dt, g_qkv, g_z, g_b, g_a) = jnp.split(proj, offs, axis=-1)
        att = swa_sink_alibi(a_q, a_k, a_v, attn_sinks[l])
        ssd = ssd_mixer(s_z, s_xbc, s_dt, ssd_conv_w[l], ssd_conv_b[l], ssd_dt_bias[l],
                        ssd_A_log[l], ssd_D[l], ssd_norm_w[l])
        gdn = gdn_mixer(g_qkv, g_z, g_b, g_a, gdn_conv_w[l], gdn_dt_bias[l], gdn_A_log[l], gdn_norm_w[l])
        mix = jnp.concatenate([att, ssd, gdn], axis=-1) @ w_out[l]
        x = x + rmsnorm(mix, post_mix_norm[l])
        h = rmsnorm(x, pre_ffn_norm[l])
        f = (jax.nn.silu(h @ ffn_w_gate[l]) * (h @ ffn_w_up[l])) @ ffn_w_down[l]
        x = x + rmsnorm(f, post_ffn_norm[l])
    return x


DEPTH_2 = 2

HEAD_DIM = 64
H_A = 8
KV_RANK = 128
H_IDX = 8
D_IDX = 64
TOPK_MAX = 256
H_B = 8
Q_BLOCK = 128
N_BUCKETS = 32
T5_MAX_DIST = 128
G_C = 8
CHUNK_2 = 128
C_WIDTH = G_C * HEAD_DIM
G_D = 8
D_WIDTH = G_D * HEAD_DIM
CONV_W = 3
D_FF = 2816
N_EVEN = (DEPTH_2 + 1) // 2
N_ODD = DEPTH_2 // 2
ALPHA = (2.0 * DEPTH_2) ** 0.25
BETA = (8.0 * DEPTH_2) ** -0.25
LN_EPS = 1e-5
EVEN_WIDTHS = (H_A * HEAD_DIM, KV_RANK, H_IDX * D_IDX, D_IDX, H_IDX,
               H_B * HEAD_DIM, H_B * HEAD_DIM, H_B * HEAD_DIM, H_B)
ODD_WIDTHS = (C_WIDTH, C_WIDTH, D_WIDTH, D_WIDTH, D_WIDTH)
EVEN_PROJ = sum(EVEN_WIDTHS)
ODD_PROJ = sum(ODD_WIDTHS)
EVEN_MIX = H_A * HEAD_DIM + H_B * HEAD_DIM
ODD_MIX = C_WIDTH + D_WIDTH


def _split(h, widths):
    out, off = [], 0
    for w in widths:
        out.append(h[..., off:off + w])
        off += w
    return out

def layer_norm(x, g, b=None):
    xf = x.astype(jnp.float32)
    mu = jnp.mean(xf, axis=-1, keepdims=True)
    xc = xf - mu
    var = jnp.mean(xc * xc, axis=-1, keepdims=True)
    y = xc * lax.rsqrt(var + LN_EPS) * g.astype(jnp.float32)
    if b is not None:
        y = y + b.astype(jnp.float32)
    return y.astype(x.dtype)

def causal_dwconv_2(z, w):
    width, ch = w.shape
    return lax.conv_general_dilated(
        z, w[:, None, :].astype(z.dtype), window_strides=(1,),
        padding=[(width - 1, 0)], dimension_numbers=('NWC', 'WIO', 'NWC'),
        feature_group_count=ch)

def t5_bucket(dist):
    max_exact = N_BUCKETS // 2
    n = jnp.maximum(dist, 0)
    nf = jnp.maximum(n, 1).astype(jnp.float32)
    large = max_exact + (jnp.log(nf / max_exact) / math.log(T5_MAX_DIST / max_exact)
                         * (N_BUCKETS - max_exact)).astype(jnp.int32)
    large = jnp.minimum(large, N_BUCKETS - 1)
    return jnp.where(n < max_exact, n, large)

def to_blocks(a):
    return jnp.moveaxis(a.reshape(a.shape[0], -1, Q_BLOCK, *a.shape[2:]), 1, 0)

def from_blocks(a):
    a = jnp.moveaxis(a, 0, 1)
    return a.reshape(a.shape[0], -1, *a.shape[3:])

def even_mixer(x, w_in, w_uk, w_uv, b_f, w_o, rel_bias):
    bsz, seq, _ = x.shape
    k_sel = min(TOPK_MAX, seq // 4)
    n_blk = seq // Q_BLOCK
    h = x @ w_in
    q_a, c_kv, q_idx, k_idx, w_idx, q_b, k_b, v_b, f_in = _split(h, EVEN_WIDTHS)
    q_a = q_a.reshape(bsz, seq, H_A, HEAD_DIM)
    q_lat = jnp.einsum('bshd,hrd->bshr', q_a, w_uk) * (HEAD_DIM ** -0.5)
    q_idx = q_idx.reshape(bsz, seq, H_IDX, D_IDX) * (D_IDX ** -0.5)
    w_idx = w_idx * (H_IDX ** -0.5)
    q_b = q_b.reshape(bsz, seq, H_B, HEAD_DIM) * (HEAD_DIM ** -0.5)
    k_b = k_b.reshape(bsz, seq, H_B, HEAD_DIM)
    v_b = v_b.reshape(bsz, seq, H_B, HEAD_DIM)
    log_f = jax.nn.log_sigmoid(f_in.astype(jnp.float32) + b_f.astype(jnp.float32))
    cum_f = jnp.cumsum(log_f, axis=1)
    cum_f_keys = jnp.swapaxes(cum_f, 1, 2)

    key_pos = jnp.arange(seq)
    bidx = jnp.arange(bsz)[:, None, None]

    def block(args):
        i, ql, qi, wi, qb, fq = args
        q_pos = i * Q_BLOCK + jnp.arange(Q_BLOCK)
        causal = key_pos[None, :] <= q_pos[:, None]
        idx = jnp.einsum('bthd,bsd->bths', qi, k_idx)
        score = jnp.einsum('bth,bths->bts', wi, jax.nn.relu(idx)).astype(jnp.float32)
        score = jnp.where(causal[None], score, -jnp.inf)
        _, sel = lax.top_k(score, k_sel)
        valid = sel <= q_pos[None, :, None]
        c_sel = c_kv[bidx, sel]
        la = jnp.einsum('bthr,btkr->bhtk', ql, c_sel).astype(jnp.float32)
        bias = rel_bias[t5_bucket(q_pos[None, :, None] - sel)]
        la = la + jnp.moveaxis(bias, -1, 1).astype(jnp.float32)
        la = jnp.where(valid[:, None], la, -jnp.inf)
        pa = jax.nn.softmax(la, axis=-1).astype(c_sel.dtype)
        oa = jnp.einsum('bhtk,btkr->bthr', pa, c_sel)
        lb = jnp.einsum('bthd,bshd->bhts', qb, k_b).astype(jnp.float32)
        lb = lb + jnp.swapaxes(fq, 1, 2)[..., None] - cum_f_keys[:, :, None, :]
        lb = jnp.where(causal[None, None], lb, -jnp.inf)
        pb = jax.nn.softmax(lb, axis=-1).astype(v_b.dtype)
        ob = jnp.einsum('bhts,bshd->bthd', pb, v_b)
        return oa, ob

    oa, ob = lax.map(block, (jnp.arange(n_blk), to_blocks(q_lat), to_blocks(q_idx),
                             to_blocks(w_idx), to_blocks(q_b), to_blocks(cum_f)))
    o_a = jnp.einsum('bshr,hrd->bshd', from_blocks(oa), w_uv).reshape(bsz, seq, H_A * HEAD_DIM)
    o_b = from_blocks(ob).reshape(bsz, seq, H_B * HEAD_DIM)
    return jnp.concatenate([o_a, o_b], axis=-1) @ w_o

def odd_mixer(x, w_in, sgu_g, sgu_w, sgu_b, conv_w, w_o):
    bsz, seq, _ = x.shape
    h = x @ w_in
    u, v, g_b, g_c, z = _split(h, ODD_WIDTHS)
    u = jax.nn.gelu(u)
    v = layer_norm(jax.nn.gelu(v).reshape(bsz, seq, G_C, HEAD_DIM), sgu_g)
    v = v.reshape(bsz, seq // CHUNK_2, CHUNK_2, G_C, HEAD_DIM)
    mix = jnp.einsum('gts,bnsgd->bntgd', jnp.tril(sgu_w), v) + jnp.swapaxes(sgu_b, 0, 1)[:, :, None]
    o_c = u * mix.reshape(bsz, seq, C_WIDTH)
    o_d = g_b * causal_dwconv_2(g_c * z, conv_w)
    return jnp.concatenate([o_c, o_d], axis=-1) @ w_o

def conv_ffn(x, w_up, conv_w, w_down):
    h = causal_dwconv_2(x @ w_up, conv_w)
    g, v = jnp.split(h, 2, axis=-1)
    return (jax.nn.silu(g) * v) @ w_down

def second_inputs(seed: int = 0) -> dict:
    key = jax.random.key(seed)
    ks = jax.random.split(key, 18)

    def nrm(k, shape, scale):
        return jax.random.normal(k, shape, jnp.float32) * scale

    return {
        "x": nrm(ks[0], (BATCH, SEQ, D_MODEL), 1.0),
        "ln_g": 1.0 + nrm(ks[1], (DEPTH_2, 2, D_MODEL), 0.02),
        "ln_b": nrm(ks[2], (DEPTH_2, 2, D_MODEL), 0.02),
        "rel_bias": nrm(ks[3], (N_BUCKETS, H_A), 0.5),
        "ev_w_in": nrm(ks[4], (N_EVEN, D_MODEL, EVEN_PROJ), D_MODEL ** -0.5),
        "ev_w_uk": nrm(ks[5], (N_EVEN, H_A, KV_RANK, HEAD_DIM), KV_RANK ** -0.5),
        "ev_w_uv": nrm(ks[6], (N_EVEN, H_A, KV_RANK, HEAD_DIM), KV_RANK ** -0.5),
        "ev_b_f": jax.random.uniform(ks[7], (N_EVEN, H_B), jnp.float32, 1.0, 4.0),
        "ev_w_o": nrm(ks[8], (N_EVEN, EVEN_MIX, D_MODEL), BETA * EVEN_MIX ** -0.5),
        "od_w_in": nrm(ks[9], (N_ODD, D_MODEL, ODD_PROJ), D_MODEL ** -0.5),
        "od_sgu_g": 1.0 + nrm(ks[10], (N_ODD, G_C, HEAD_DIM), 0.02),
        "od_sgu_w": nrm(ks[11], (N_ODD, G_C, CHUNK_2, CHUNK_2), CHUNK_2 ** -0.5),
        "od_sgu_b": 1.0 + nrm(ks[12], (N_ODD, G_C, CHUNK_2), 0.1),
        "od_conv_w": nrm(ks[13], (N_ODD, CONV_W, D_WIDTH), CONV_W ** -0.5),
        "od_w_o": nrm(ks[14], (N_ODD, ODD_MIX, D_MODEL), BETA * ODD_MIX ** -0.5),
        "ffn_w_up": nrm(ks[15], (DEPTH_2, D_MODEL, 2 * D_FF), D_MODEL ** -0.5),
        "ffn_conv_w": nrm(ks[16], (DEPTH_2, CONV_W, 2 * D_FF), CONV_W ** -0.5),
        "ffn_w_down": nrm(ks[17], (DEPTH_2, D_FF, D_MODEL), BETA * D_FF ** -0.5),
    }

def second_block(x, ln_g, ln_b, rel_bias, ev_w_in, ev_w_uk, ev_w_uv, ev_b_f, ev_w_o,
              od_w_in, od_sgu_g, od_sgu_w, od_sgu_b, od_conv_w, od_w_o,
              ffn_w_up, ffn_conv_w, ffn_w_down):
    for layer in range(DEPTH_2):
        j = layer // 2
        if layer % 2 == 0:
            m = even_mixer(x, ev_w_in[j], ev_w_uk[j], ev_w_uv[j], ev_b_f[j], ev_w_o[j], rel_bias)
        else:
            m = odd_mixer(x, od_w_in[j], od_sgu_g[j], od_sgu_w[j], od_sgu_b[j], od_conv_w[j], od_w_o[j])
        x = layer_norm(ALPHA * x + m, ln_g[layer, 0], ln_b[layer, 0])
        f = conv_ffn(x, ffn_w_up[layer], ffn_conv_w[layer], ffn_w_down[layer])
        x = layer_norm(ALPHA * x + f, ln_g[layer, 1], ln_b[layer, 1])
    return x


def setup_inputs(seed=0):
    out = dict(first_inputs(seed))
    for name, value in second_inputs(seed + 1).items():
        if name != "x":
            out[name + "_2"] = value
    return out


def reference(
    x, pre_mix_norm, post_mix_norm, pre_ffn_norm, post_ffn_norm, w_in, w_out, attn_sinks,
    ssd_conv_w, ssd_conv_b, ssd_dt_bias, ssd_A_log, ssd_D, ssd_norm_w, gdn_conv_w, gdn_dt_bias,
    gdn_A_log, gdn_norm_w, ffn_w_gate, ffn_w_up, ffn_w_down, ln_g_2, ln_b_2, rel_bias_2,
    ev_w_in_2, ev_w_uk_2, ev_w_uv_2, ev_b_f_2, ev_w_o_2, od_w_in_2, od_sgu_g_2, od_sgu_w_2,
    od_sgu_b_2, od_conv_w_2, od_w_o_2, ffn_w_up_2, ffn_conv_w_2, ffn_w_down_2,
):
    x = first_block(
        x, pre_mix_norm, post_mix_norm, pre_ffn_norm, post_ffn_norm, w_in, w_out, attn_sinks,
        ssd_conv_w, ssd_conv_b, ssd_dt_bias, ssd_A_log, ssd_D, ssd_norm_w, gdn_conv_w,
        gdn_dt_bias, gdn_A_log, gdn_norm_w, ffn_w_gate, ffn_w_up, ffn_w_down,
    )
    return second_block(
        x, ln_g_2, ln_b_2, rel_bias_2, ev_w_in_2, ev_w_uk_2, ev_w_uv_2, ev_b_f_2, ev_w_o_2,
        od_w_in_2, od_sgu_g_2, od_sgu_w_2, od_sgu_b_2, od_conv_w_2, od_w_o_2, ffn_w_up_2,
        ffn_conv_w_2, ffn_w_down_2,
    )


_drawn_inputs = setup_inputs


def setup_inputs(seed=0):
    import zlib

    import numpy as np

    out = dict(_drawn_inputs(seed))
    spreads = {}
    factors = {'attn_sinks': 7.189, 'ssd_conv_b': 3.073, 'od_sgu_g_2': 8.0, 'od_sgu_b_2': 3.572}
    for name, (base, spread) in spreads.items():
        noise = np.random.default_rng([zlib.crc32(name.encode()), seed]).standard_normal(out[name].shape)
        drawn = base * np.exp(spread * noise) if base else spread * noise
        out[name] = __import__('jax').numpy.asarray(drawn.astype(out[name].dtype))
    for name, factor in factors.items():
        out[name] = (out[name] * factor).astype(out[name].dtype)
    return out
```

```python
import math
from contextlib import ExitStack

import numpy as np
import concourse.bass as bass
from concourse import mybir

ALU = mybir.AluOpType
ACT = mybir.ActivationFunctionType
F32 = mybir.dt.float32
F32R = mybir.dt.float32r
AXX = mybir.AxisListType.X
NEG = -1.0e30
TAKEN = -3.0e38
ALPHA = 4.0 ** 0.25


def rng(a, n):
    return list(range(a, a + n))


def weight_plan():
    plan = []

    def feat(name, layer, *tiles):
        cols = [c for t in tiles for c in t]
        plan.append((name, layer, 0, 8, cols))

    def tok(name, layer, cols, kt=8):
        step = min(kt, 2048 // len(cols))
        for k in range(0, kt, step):
            plan.append((name, layer, k, min(step, kt - k), cols))

    w = "w_in"
    t = [rng(0, 64) + rng(128, 64), rng(64, 64) + rng(192, 64), rng(256, 128)]
    t += [rng(1024 + 128 * j, 128) for j in range(8)]
    gq, gk, gv = 2056, 2312, 2568
    t += [rng(gq, 128), rng(gk, 128), rng(gv, 128), rng(gq + 128, 128), rng(gk + 128, 128), rng(gv + 128, 128)]
    tok(w, 0, rng(384, 128) + rng(2048, 8) + rng(3084, 4) + rng(3080, 4) + rng(2824, 256))
    for j in range(0, 17, 2):
        feat(w, 0, *t[j:j + 2])
    tok(w, 0, rng(512, 512))
    for h in range(2):
        tok("w_out", 0, rng(512 * h, 512))
    for m in range(22):
        plan.append(("gate_up", 0, 0, 8, m))
    for h in range(2):
        tok("ffn_w_down", 0, rng(512 * h, 512), 22)
    w = "ev_w_in_2"
    tok(w, 0, rng(512, 128) + rng(1216, 8) + rng(2760, 8))
    feat(w, 0, rng(640, 128), rng(768, 128))
    feat(w, 0, rng(896, 128), rng(1024, 128))
    feat(w, 0, rng(512, 128), rng(1152, 64) + rng(1152, 64))
    for j in range(2):
        feat(w, 0, rng(256 * j, 128), rng(256 * j + 128, 128))
    for j in range(2):
        feat(w, 0, rng(1224 + 256 * j, 128), rng(1224 + 256 * j + 128, 128))
    for j in range(2):
        feat(w, 0, rng(1736 + 256 * j, 128), rng(1736 + 256 * j + 128, 128))
    tok(w, 0, rng(2248, 512))
    for h in range(2):
        tok("ev_w_o_2", 0, rng(512 * h, 512))

    def conv_ffn(layer):
        for m in range(22):
            feat("ffn_w_up_2", layer, rng(128 * m, 128), rng(2816 + 128 * m, 128))
        for h in range(2):
            tok("ffn_w_down_2", layer, rng(512 * h, 512), 22)

    conv_ffn(0)
    w = "od_w_in_2"
    tok(w, 0, rng(512, 512))
    for j in range(4):
        feat(w, 0, rng(1536 + 128 * j, 128), rng(2048 + 128 * j, 128))
    for j in range(2):
        feat(w, 0, rng(1024 + 256 * j, 128), rng(1024 + 256 * j + 128, 128))
    for j in range(2):
        feat(w, 0, rng(256 * j, 128), rng(256 * j + 128, 128))
    for h in range(2):
        tok("od_w_o_2", 0, rng(512 * h, 512))
    conv_ffn(1)
    return plan


def chunk_width(c):
    return c[3] * (256 if c[0] == "gate_up" else len(c[4]))


COLS = {}
NCOLS = 0
for _n, _w in [("pre_mix", 8), ("pre_ffn", 8), ("ssd_cw", 32), ("ssd_cb", 8), ("gdn_cw", 24), ("gdn_nw", 1),
               ("ln_g", 32), ("ln_b", 32), ("od_cw", 12), ("b_f", 1), ("eps6", 1), ("eps5", 1),
               ("fcw0", 132), ("fcw1", 132)]:
    COLS[_n] = NCOLS
    NCOLS += _w


def build(nc, ins, out):
    plan = weight_plan()
    offs = [0]
    for c in plan:
        offs.append(offs[-1] + 128 * chunk_width(c))

    u_dram = nc.dram_tensor("u_scratch", (8, 384), F32, kind="Internal").ap()

    ctx = ExitStack()
    with ctx:
        names = [0]
        base = (nc.sbuf_base + 63) // 64 * 64

        def at(offset, shape, dt=F32):
            names[0] += 1
            return nc.alloc_sbuf_tensor_at(f"t{names[0]}", shape, dt, offset=base + offset)

        class Region:
            def __init__(self, start, end):
                self.at, self.end = start, end

            def __call__(self, shape, dt=F32):
                n = 4
                for s in shape[1:]:
                    n *= s
                n = (n + 63) // 64 * 64
                assert self.at + n <= self.end, (self.at, n, self.end)
                t = at(self.at, shape, dt)
                self.at += n
                return t

        TOP = nc.sbuf_usable_end - base
        R0 = Region(0, TOP)
        raw = [R0([128, 2048]) for _ in range(2)]
        wH = [R0([128, 2048], F32R) for _ in range(2)]
        wL = [R0([128, 2048], F32R) for _ in range(2)]
        x = R0([128, 4, 1024])
        hH = R0([128, 8, 512], F32R)
        hL = R0([128, 8, 512], F32R)
        ident = R0([128, 128])
        U = R0([128, 128])
        ones = R0([128, 128])
        cols = R0([128, NCOLS])
        brow = R0([128, 48])
        rows = [R0([128, 1024]) for _ in range(2)]
        st = R0([128, 80])
        BIG = R0.at

        ps = [ctx.enter_context(nc.psum_tensor(f"ps{i}", [128, 512], F32)) for i in range(8)]
        bank = [[] for _ in range(8)]

        def take(*ids):
            r = []
            for i in ids:
                r += bank[i]
                bank[i] = []
            return r

        def put(i, *toks):
            bank[i] = bank[i] + list(toks)

        sems = {}

        def sem(name):
            sems[name] = ctx.enter_context(nc.semaphore(name))
            return name

        class Queue:
            def __init__(self, name):
                self.sem, self.n, self.items = sem("s_" + name), 0, []

            def add(self, fn, after, sig=True):
                if sig:
                    self.n += 1
                self.items.append((list(after), fn, sig))
                return (self.sem, self.n) if sig else None

            def emit(self, eng):
                seen = {}
                for after, fn, sig in self.items:
                    for t in after:
                        if t is not None and seen.get(t[0], 0) < t[1]:
                            eng.wait_ge(sems[t[0]], t[1])
                            seen[t[0]] = t[1]
                    i = fn(eng)
                    if sig is True:
                        i.then_inc(sems[self.sem], 1)
                    elif sig:
                        i.then_inc(sems[sig], 16)

        PE, VE, SE, GE, SP = Queue("pe"), Queue("ve"), Queue("se"), Queue("ge"), Queue("sp")

        ndma = [0]

        def dma(dst, src, after=(), name=None, count=1, q=SP):
            if name is None:
                ndma[0] += 1
                name = sem(f"d{ndma[0]}")
            q.items.append((list(after), lambda e: e.dma_start(dst, src), name))
            return (name, 16 * count)

        def mm(o, l, r, start, stop, after=(), sig=False):
            return PE.add(lambda e: e.matmul(o, l, r, start=start, stop=stop), after, sig)

        def tr(o, i, after=(), sig=False):
            n = i.shape[0]
            return PE.add(lambda e: e.transpose(o, i, ident[0:n, 0:n]), after, sig)

        def act(o, i, f, after=(), bias=None, scale=None, accum=None):
            kw = {}
            if bias is not None:
                kw["bias"] = bias
            if scale is not None:
                kw["scale"] = scale
            if accum is not None:
                kw["accum_out"] = accum
            return SE.add(lambda e: e.activation(o, i, f, **kw), after)

        def cpa(o, i, after=()):
            return act(o, i, ACT.Copy, after)

        def tt(o, a, b, op, after=(), q=VE):
            return q.add(lambda e: e.tensor_tensor(o, a, b, op), after)

        def ts(o, a, s1, s2, op0, op1=ALU.bypass, after=(), q=VE):
            if s2 is None:
                return q.add(lambda e: e.tensor_scalar(o, a, s1, None, op0), after)
            return q.add(lambda e: e.tensor_scalar(o, a, s1, s2, op0, op1), after)

        def stt(o, a, s, b, op0, op1, after=()):
            return VE.add(lambda e: e.scalar_tensor_tensor(o, a, s, b, op0, op1), after)

        def cpv(o, i, after=(), q=VE):
            return q.add(lambda e: e.tensor_copy(o, i), after)

        def rec(o, i, after=()):
            return VE.add(lambda e: e.reciprocal(o, i), after)

        def red(o, i, op, after=(), negate=None):
            return VE.add(lambda e: e.tensor_reduce(o, i, AXX, op, negate=negate), after)

        def mset(o, v, after=(), q=VE):
            return q.add(lambda e: e.memset(o, v), after)

        def col(name, j=0):
            return cols[:, COLS[name] + j:COLS[name] + j + 1]

        d_cols = dma(cols[:, :], ins["cols"])
        d_x = [dma(x[:, i, :], ins["x"][0, 128 * i:128 * i + 128, :]) for i in range(4)]
        d_id = dma(ident[:, :], ins["ident"])
        d_U = dma(U[:, :], ins["triu"])
        d_brow = dma(brow[:, 0:48], ins["brow"].partition_broadcast(128).rearrange("p a n -> p (a n)"))
        t_ones = mset(ones[:, :], 1.0)

        raw_free = [[], []]
        hl_free = [[], []]
        landed = {}
        halves = {}
        w_sem = [sem("d_w0"), sem("d_w1")]

        def load(c):
            if c >= len(plan):
                return
            n = chunk_width(plan[c])
            r = c % 2
            src = ins["wbig"][offs[c]:offs[c + 1]].rearrange("(p n) -> p n", p=128)
            landed[c] = dma(raw[r][:, 0:n], src, raw_free[r], w_sem[r], c // 2 + 1)

        def split(c):
            if c >= len(plan) or c in halves:
                return
            n = chunk_width(plan[c])
            r = c % 2
            a = act(wH[r][:, 0:n], raw[r][:, 0:n], ACT.Copy, [landed[c]] + hl_free[r])
            b = tt(wL[r][:, 0:n], raw[r][:, 0:n], wH[r][:, 0:n].bitcast(F32), ALU.subtract, [landed[c], a] + hl_free[r])
            raw_free[r] = [b]
            halves[c] = [a, b]
            load(c + 2)

        load(0)
        load(1)
        chunk = [0]

        def weights():
            c = chunk[0]
            split(c)
            split(c + 1)
            n = chunk_width(plan[c])
            r = c % 2
            k = plan[c][3]
            return (c, wH[r][:, 0:n].rearrange("p (k c) -> p k c", k=k),
                    wL[r][:, 0:n].rearrange("p (k c) -> p k c", k=k), halves[c])

        def weights_done(tok):
            hl_free[chunk[0] % 2] = [tok]
            chunk[0] += 1

        def feat_chunk(ready, banks, use):
            c, H, L, w = weights()
            nt = plan_cols(c) // 128
            toks = []
            for t in range(nt):
                b = banks[t]
                s = slice(128 * t, 128 * t + 128)
                after = w + take(b) + ready
                for k in range(8):
                    mm(ps[b][:, :], H[:, k, s], hH[:, k, :], k == 0, False, after)
                    after = ()
                    mm(ps[b][:, :], H[:, k, s], hL[:, k, :], False, False)
                    m = mm(ps[b][:, :], L[:, k, s], hH[:, k, :], False, k == 7, (), k == 7)
                toks.append(m)
            weights_done(toks[-1])
            for t in range(nt):
                use(t, banks[t], toks[t])
            return toks[-1]

        def plan_cols(c):
            return 256 if plan[c][0] == "gate_up" else len(plan[c][4])

        def tok_group(lH, lL, kt, ready, banks, use, last=None):
            k0 = 0
            while k0 < kt:
                c, H, L, w = weights()
                nk, n = plan[c][3], len(plan[c][4])
                done = k0 + nk == kt
                toks = []
                for i in range(4):
                    b = banks[i]
                    s = slice(128 * i, 128 * i + 128)
                    after = w + ready + (take(b) if k0 == 0 else [])
                    for k in range(nk):
                        e = done and k == nk - 1
                        mm(ps[b][:, 0:n], lH[:, k0 + k, s], H[:, k, :], k0 + k == 0, False, after)
                        after = ()
                        mm(ps[b][:, 0:n], lH[:, k0 + k, s], L[:, k, :], False, False)
                        m = mm(ps[b][:, 0:n], lL[:, k0 + k, s], H[:, k, :], False, e, (), k == nk - 1)
                    toks.append(m)
                weights_done(toks[-1])
                k0 += nk
            for i in range(4):
                use(i, banks[i], toks[i])
            return toks[-1]

        def split_ht(k, src, after, free, cs=slice(0, 512), gain=None):
            if gain is None:
                a = act(hH[:, k, cs], src, ACT.Copy, after + free)
                b = tt(hL[:, k, cs], src, hH[:, k, cs].bitcast(F32), ALU.subtract, [a] + after + free)
            else:
                a = act(hH[:, k, cs], src, ACT.Identity, after + free, scale=gain)
                b = stt(hL[:, k, cs], src, gain, hH[:, k, cs].bitcast(F32), ALU.mult, ALU.subtract, [a] + after + free)
            return [a, b]

        def row(slot, j, after=()):
            return dma(rows[slot][:, :], ins["rows"][j:j + 1, :].partition_broadcast(128).rearrange("p a n -> p (a n)"), after)

        def transposed(src, toks, use, free):
            for k in range(8):
                after = take(k) + [d_id]
                for i in range(4):
                    m = tr(ps[k][:, 128 * i:128 * i + 128], src[:, i, 128 * k:128 * k + 128], after + toks[i], i == 3)
                    after = []
                use(k, k, m)

        def rms_to_ht(toks, gain, xn, free, xn_free):
            ready = []
            ntok = []
            for i in range(4):
                a = act(xn[:, i, :], x[:, i, :], ACT.Square, toks[i] + xn_free, accum=st[:, i:i + 1])
                a = act(st[:, 4 + i:5 + i], st[:, i:i + 1], ACT.Sqrt, [a, d_cols], bias=col("eps6"), scale=1.0 / 1024)
                a = rec(st[:, 8 + i:9 + i], st[:, 4 + i:5 + i], [a])
                ntok.append([ts(xn[:, i, :], x[:, i, :], st[:, 8 + i:9 + i], None, ALU.mult, after=[a])])

            def use(k, b, m):
                r = split_ht(k, ps[b][:, :], [m], free, gain=col(gain, k))
                put(b, *r)
                ready.extend(r)

            transposed(xn, ntok, use, free)
            return ready

        def ln_to_ht(toks, n, scratch, free, r_g, r_b, want_ht, store=None):
            ready, ntok, xtok = [], [], []
            stats = st[:, 32:56].rearrange("p (a b c) -> p a b c", a=2, b=2)
            last = [None, None]
            for i in range(4):
                sl = stats[:, i % 2, :, :]
                a = []
                for h in range(2):
                    a.append(VE.add(lambda e, o=sl[:, h, :], s=x[:, i, 512 * h:512 * h + 512]: e.bn_stats(o, s),
                                    toks[i] + [last[i % 2]]))
                mv = st[:, 56 + 4 * i:58 + 4 * i]
                a = VE.add(lambda e, o=mv, s=sl: e.bn_aggr(o, s), a)
                last[i % 2] = a
                a = act(st[:, 58 + 4 * i:59 + 4 * i], mv[:, 1:2], ACT.Sqrt, [a, d_cols], bias=col("eps5"))
                a = rec(st[:, 59 + 4 * i:60 + 4 * i], st[:, 58 + 4 * i:59 + 4 * i], [a])
                a = ts(x[:, i, :], x[:, i, :], mv[:, 0:1], st[:, 59 + 4 * i:60 + 4 * i], ALU.subtract, ALU.mult, [a])
                ntok.append([a])
            g_at, b_at = COLS["ln_g"] + 8 * n, COLS["ln_b"] + 8 * n
            if want_ht:
                sfree = [[], []]

                def use(k, b, m):
                    s = k % 2
                    a = act(scratch[s], ps[b][:, :], ACT.Identity, [m, d_cols] + sfree[s], bias=cols[:, b_at + k:b_at + k + 1],
                            scale=cols[:, g_at + k:g_at + k + 1])
                    put(b, a)
                    h = cpv(hH[:, k, :], scratch[s], [a] + free)
                    l = tt(hL[:, k, :], scratch[s], hH[:, k, :].bitcast(F32), ALU.subtract, [a, h] + free)
                    sfree[s] = [h, l]
                    ready.extend([h, l])

                transposed(x, ntok, use, free)
            for i in range(4):
                w = [(PE.sem, PE.n)] if want_ht else []
                a = tt(x[:, i, :], x[:, i, :], rows[0][:, :], ALU.mult, ntok[i] + [r_g] + w, q=GE)
                a = tt(x[:, i, :], x[:, i, :], rows[1][:, :], ALU.add, [a, r_b], q=GE)
                xtok.append([a])
            return ready, xtok

        PE.last = None

        def pe_mark():
            PE.last = ("s_pe", PE.n)
            return PE.last

        R = Region(BIG, TOP)
        xn = R([128, 4, 1024])
        xtok = [[t] for t in d_x]
        oneh = R([32, 384])
        rb = R([32, 8])
        uu = R([8, 384])
        d1 = dma(oneh[:, :], ins["oneh"])
        d2 = dma(rb[:, :], ins["rel_bias_2"])
        m = mm(ps[0][0:8, 0:384], rb[:, :], oneh[:, :], True, True, [d1, d2], True)
        a = cpa(uu[:, :], ps[0][0:8, 0:384], [m])
        put(0, a)
        d_u = dma(u_dram, uu[:, :], [a])

        hT = rms_to_ht(xtok, "pre_mix", xn, [], [])
        xn_done = [pe_mark_tok for pe_mark_tok in [("s_pe", PE.n)]]

        R = Region(BIG + 16384 + 64 * 60, TOP)
        qT = [R([128, 512]) for _ in range(2)]
        kT = R([128, 512])
        vtm = R([128, 4, 128])
        sm = R([128, 4, 16])
        gz = R([128, 4, 256])
        Z0 = R.at
        zs = R([128, 4, 512])
        xT = [R([128, 512]) for _ in range(8)]
        gT = [R([128, 512]) for _ in range(6)]
        mid = R.at
        y_tmp = [at(BIG + 2048 * j, [128, 512]) for j in range(4)]
        y_free = [list(xn_done) for _ in range(4)]

        tk = {}

        def small_use(i, b, m):
            a1 = cpa(vtm[:, i, :], ps[b][:, 0:128], [m])
            a2 = cpa(sm[:, i, :], ps[b][:, 128:144], [m])
            a3 = act(gz[:, i, :], ps[b][:, 144:400], ACT.Silu, [m])
            put(b, a1, a2, a3)
            tk["v", i], tk["sm", i], tk["gz", i] = a1, a2, a3

        tok_group(hH, hL, 8, hT, [0, 1, 2, 3], small_use)

        n_conv = [0]

        def conv4(b, m, o, w, bias):
            j = n_conv[0] % 4
            n_conv[0] += 1
            y = y_tmp[j]
            p = ps[b]
            a = act(y[:, :], p[:, :], ACT.Identity, [m, d_cols] + y_free[j], scale=cols[:, w + 3:w + 4])
            for d in range(1, 4):
                a = stt(y[:, d:512], p[:, 0:512 - d], cols[:, w + 3 - d:w + 4 - d], y[:, d:512], ALU.mult, ALU.add, [a])
            put(b, a)
            kw = {} if bias is None else {"bias": bias}
            a = act(o[:, :], y[:, :], ACT.Silu, [a], **kw)
            y_free[j] = [a]
            return a

        tiles = ["qA", "qB", "k"] + [("x", j) for j in range(8)] + [("g", j) for j in range(6)]

        def in_use(first):
            def use(t, b, m):
                n = tiles[first + t]
                if n == "qA" or n == "qB":
                    q = qT[0 if n == "qA" else 1]
                    a = act(q[:, :], ps[b][:, :], ACT.Copy, [m], scale=0.125)
                    put(b, a)
                elif n == "k":
                    a = cpa(kT[:, :], ps[b][:, :], [m])
                    put(b, a)
                elif n[0] == "x":
                    a = conv4(b, m, xT[n[1]], COLS["ssd_cw"] + 4 * n[1], col("ssd_cb", n[1]))
                else:
                    kind, pair = n[1] % 3, n[1] // 3
                    a = conv4(b, m, gT[n[1]], COLS["gdn_cw"] + 4 * (2 * kind + pair), None)
                tk[n] = a
            return use

        for j in range(0, 17, 2):
            feat_chunk(hT, [4 + j % 4, 5 + j % 4], in_use(j))

        def z_use(i, b, m):
            a = act(zs[:, i, :], ps[b][:, :], ACT.Silu, [m])
            put(b, a)
            tk["z", i] = a

        ht_free = [tok_group(hH, hL, 8, hT, [0, 1, 2, 3], z_use)]

        R = Region(mid, TOP)
        sp = R([128, 9, 48])

        def v3(t, n=12):
            return t.rearrange("p (i h) -> p i h", h=n)

        e0, e1, e2, e3, da = (sp[:, j, :] for j in range(5))
        csum, tot = sp[:, 5, :], sp[:, 6, :]
        eg, dl = sp[:, 7, :], sp[:, 8, :]
        dtot = R([128, 48])
        beta = R([128, 4, 4])
        an = R([128, 12])
        decS = R([128, 2, 4])

        a = tt(v3(e0), sm[:, :, 0:12], brow[:, 0:12].unsqueeze(1).broadcast_to([128, 4, 12]), ALU.add, [tk["sm", i] for i in range(4)] + [d_brow])
        b = stt(e1, e0, -1.0, e0, ALU.mult, ALU.max, [a])
        b = act(e1, e1, ACT.Exp, [b], scale=-1.0)
        c = ts(e2, e1, 1.0, None, ALU.add, after=[b])
        d = act(e3, e2, ACT.Ln, [c])
        a2 = act(an[:, :], brow[:, 12:24], ACT.Exp, [d_brow])
        a3 = act(beta[:, :, :], sm[:, :, 12:16], ACT.Exp, [tk["sm", i] for i in range(4)], scale=-1.0)
        c = ts(e2, e2, -1.0, 1e-30, ALU.add, ALU.max, [c, d])
        c = rec(da, e2, [c])
        c = tt(da, da, e3, ALU.mult, [c, d])
        c = tt(da, da, e1, ALU.mult, [c])
        f = ts(e2, e2, 1e-30, None, ALU.is_equal, after=[c])
        f = tt(e2, e2, e1, ALU.mult, [f])
        c = tt(da, da, e2, ALU.add, [c, f])
        c = stt(e0, e0, 0.0, da, ALU.max, ALU.add, [c])
        t_dt = c
        a2 = ts(an[:, :], an[:, :], -1.0, None, ALU.mult, after=[a2])
        t_da = tt(v3(da), v3(e0), an[:, :].unsqueeze(1).broadcast_to([128, 4, 12]), ALU.mult, [c, a2])
        a3 = ts(beta[:, :, :], beta[:, :, :], 1.0, None, ALU.add, after=[a3])
        t_beta = rec(beta[:, :, :], beta[:, :, :], [a3])
        m1 = mm(ps[7][:, 0:48], U[:, :], da, True, True, take(7) + [t_da, d_U], True)
        m2 = mm(ps[7][:, 64:112], ones[:, :], da, True, True, [t_ones], True)
        t_cs = cpv(csum, ps[7][:, 0:48], [m1, m2])
        t_tot = cpv(tot, ps[7][:, 64:112], [m2])
        put(7, t_cs, t_tot)
        a = tt(dl, tot, csum, ALU.subtract, [t_cs, t_tot])
        t_dl = act(dl, dl, ACT.Exp, [a])
        t_eg = act(eg, csum, ACT.Exp, [t_cs])
        t_dtot = act(dtot[:, :], tot, ACT.Exp, [t_tot])
        for p in range(2):
            for h in range(2):
                t_decS = cpv(decS[64 * h:64 * h + 64, p, :], v3(dtot[64 * h:64 * h + 64, :])[:, :, 8 + 2 * p + h], [t_dtot])

        mixed = []
        mid = R.at

        R = Region(mid, TOP)
        abias = R([128, 4, 256])
        d_ab = dma(abias[:, :, :], ins["abias"].rearrange("p (h n) -> p h n", h=4), xn_done)
        S = [R([128, 4, 256]) for _ in range(2)]
        PT = [R([128, 8, 128]) for _ in range(2)]
        sx = [R([128, 5, 4]) for _ in range(2)]
        S_free, PT_free = [[], []], [[], []]
        sink = brow[:, 24:28]
        vts = [tk["v", i] for i in range(4)]

        def att_scores(i):
            s = i % 2
            k0 = 128 * max(i - 1, 0)
            n = 128 * (i + 1) - k0
            c0 = 256 - n
            r = []
            for h in range(4):
                b = 2 * s + h // 2
                p = slice(64 * (h // 2), 64 * (h // 2) + 64)
                after = [tk["qA"], tk["qB"], tk["k"]] + (take(b) if h % 2 == 0 else [])
                m = mm(ps[b][:, 256 * (h % 2):256 * (h % 2) + n], qT[h % 2][p, 128 * i:128 * i + 128],
                       kT[p, k0:k0 + n], True, True, after, h % 2 == 1)
                if h % 2 == 1:
                    v = ps[b][:, :].rearrange("p (h n) -> p h n", h=2)[:, :, 0:n]
                    t = tt(S[s][:, h - 1:h + 1, 0:n], v, abias[:, h - 1:h + 1, c0:256], ALU.add, [m, d_ab] + S_free[s])
                    put(b, t)
                    r.append(t)
            mx, nm, sume, es, rd = (sx[s][:, j, :] for j in range(5))
            t = red(mx, S[s][:, :, 0:n], ALU.max, r + S_free[s])
            t = tt(mx, mx, sink, ALU.max, [t, d_brow])
            u = tt(es, sink, mx, ALU.subtract, [t])
            t = ts(nm, mx, -1.0, None, ALU.mult, after=[t])
            e = []
            for h in range(4):
                e.append(act(S[s][:, h, 0:n], S[s][:, h, 0:n], ACT.Exp, [t], bias=nm[:, h:h + 1], accum=sume[:, h:h + 1]))
            e.append(act(es, es, ACT.Exp, [u]))
            t = tt(rd, sume, es, ALU.add, e)
            t = rec(rd, rd, [t])
            return tt(S[s][:, :, 0:n], S[s][:, :, 0:n], rd.unsqueeze(2).broadcast_to([128, 4, n]), ALU.mult, [t])

        def att_out(i, t):
            s = i % 2
            k0 = max(i - 1, 0)
            nb = i + 1 - k0
            toks = []
            for hh in range(2):
                b = 4 + hh
                after = take(b) + [t]
                for h in range(2 * hh, 2 * hh + 2):
                    for j in range(nb):
                        c = (h % 2) * 2 + j
                        m = tr(ps[b][:, 128 * c:128 * c + 128], S[s][:, h, 128 * j:128 * j + 128], after, h % 2 == 1 and j == nb - 1)
                        after = []
                v = ps[b][:, :].rearrange("p (h j n) -> p h j n", h=2, j=2)[:, :, 0:nb, :]
                o = PT[s][:, 4 * hh:4 * hh + 4, :].rearrange("p (h j) n -> p h j n", h=2)[:, :, 0:nb, :]
                e = cpa(o, v, [m] + PT_free[s])
                put(b, e)
                toks.append(e)
            S_free[s] = [m]
            for h in range(4):
                b = 6 + h // 2
                p = slice(64 * (h % 2), 64 * (h % 2) + 64)
                for j in range(nb):
                    after = toks + vts + (take(b) if i == 0 and h % 2 == 0 and j == 0 else [])
                    m = mm(ps[b][p, 128 * i:128 * i + 128], vtm[:, k0 + j, 64 * (h // 2):64 * (h // 2) + 64],
                           PT[s][:, 2 * h + j, :], j == 0, j == nb - 1, after, j == nb - 1)
            PT_free[s] = [m]
            return m

        t = att_scores(0)
        for i in range(4):
            t2 = att_scores(i + 1) if i < 3 else None
            m = att_out(i, t)
            t = t2
        for k in range(2):
            r = split_ht(k, ps[6 + k][:, :], [m], ht_free)
            put(6 + k, *r)
            mixed += r
        att_end = r + [m] + [t for f in y_free for t in f]

        R = Region(mid, TOP)
        xs = [R([128, 512]) for _ in range(2)]
        xc = [R([128, 512]) for _ in range(2)]
        xd = R([128, 512])
        R3 = Region(BIG + 8192, BIG + 16384)
        Dm = R3([128, 8, 128])
        SM = R([128, 2, 128])
        Bt = R([128, 256])
        state = R([128, 512])
        yall = R([128, 4, 512])
        R2 = Region(BIG, BIG + 16384)
        sq = R2([128, 512])
        nwr = R2([128, 512])
        d_nwr = dma(nwr[:, :], ins["ssd_nw"].partition_broadcast(128).rearrange("p a n -> p (a n)"), att_end)
        gs = R([128, 8])
        free = {"xs": [att_end, att_end], "xc": [att_end, att_end], "xd": att_end, "Dm": att_end, "SM": att_end, "Bt": att_end}
        t_state = None
        y_toks = []

        def h64(t):
            return t.rearrange("p (h d) -> p h d", d=64)

        def bc64(t):
            return t.unsqueeze(2).broadcast_to([128, 8, 64])

        for i in range(4):
            s = i % 2
            ts_ = slice(128 * i, 128 * i + 128)
            after = take(0) + [d_id]
            for j in range(4):
                m = tr(ps[0][:, 128 * j:128 * j + 128], xT[j][:, ts_], after + [tk["x", j]], j == 3)
                after = []
            t_xs = cpa(xs[s][:, :], ps[0][:, :], [m] + free["xs"][s])
            put(0, t_xs)
            t_xc = tt(h64(xc[s][:, :]), h64(xs[s][:, :]), bc64(v3(e0)[:, i, 0:8]), ALU.mult, [t_xs, t_dt] + free["xc"][s])
            t_xd = tt(h64(xd[:, :]), h64(xc[s][:, :]), bc64(v3(dl)[:, i, 0:8]), ALU.mult, [t_xc, t_dl] + free["xd"])
            after = take(1)
            for g in range(2):
                m = tr(ps[1][:, 128 * g:128 * g + 128], xT[4 + g][:, ts_], after + [tk["x", 4 + g]], g == 1)
                after = []
            t_Bt = cpa(Bt[:, :], ps[1][:, 0:256], [m] + free["Bt"])
            put(1, t_Bt)
            after = take(2)
            for g in range(2):
                m = mm(ps[2][:, 128 * g:128 * g + 128], xT[4 + g][:, ts_], xT[6 + g][:, ts_], True, True, after + [tk["x", 6 + g]], g == 1)
                after = []
            t_SM = tt(SM[:, :, :], ps[2][:, 0:256].rearrange("p (g n) -> p g n", g=2),
                      U[:, :].unsqueeze(1).broadcast_to([128, 2, 128]), ALU.mult, [m, d_U] + free["SM"])
            put(2, t_SM)
            td = []
            for h in range(8):
                b = 3 + h // 4
                after = (take(b) if h % 4 == 0 else []) + [t_da]
                m = mm(ps[b][:, 128 * (h % 4):128 * (h % 4) + 128], v3(da)[:, i, h:h + 1].broadcast_to([128, 128]), U[:, :],
                       True, True, after, h % 4 == 3)
                if h % 4 == 3:
                    for hh in range(h - 3, h + 1):
                        t = ts(Dm[:, hh, :], ps[b][:, 128 * (hh % 4):128 * (hh % 4) + 128], v3(csum)[:, i, hh:hh + 1], 0.0,
                               ALU.subtract, ALU.min, [m, t_cs] + free["Dm"])
                    put(b, t)
                    e = act(Dm[:, h - 3:h + 1, :], Dm[:, h - 3:h + 1, :], ACT.Exp, [t])
                    td.append(tt(Dm[:, h - 3:h + 1, :], Dm[:, h - 3:h + 1, :],
                                 SM[:, h // 4, :].unsqueeze(1).broadcast_to([128, 4, 128]), ALU.mult, [e, t_SM]))
            free["SM"] = td
            after = take(5) + td + [t_xc]
            for h in range(8):
                m = mm(ps[5][:, 64 * h:64 * h + 64], Dm[:, h, :], xc[s][:, 64 * h:64 * h + 64], True, True, after, h == 7)
                after = []
            free["Dm"] = [m]
            free["xc"][s] = [m, t_xd]
            y = yall[:, i, :]
            if i > 0:
                after = take(6) + [t_state]
                for g in range(2):
                    m2 = mm(ps[6][:, 256 * g:256 * g + 256], xT[6 + g][:, ts_], state[:, 256 * g:256 * g + 256], True, True, after, g == 1)
                    after = []
                t = tt(h64(y), h64(ps[6][:, :]), bc64(v3(eg)[:, i, 0:8]), ALU.mult, [m2, t_eg])
                put(6, t)
                t = tt(y, y, ps[5][:, :], ALU.add, [t, m])
            else:
                t = cpv(y, ps[5][:, :], [m] + att_end)
            put(5, t)
            if i < 3:
                after = take(7) + [t_Bt, t_xd]
                for g in range(2):
                    m3 = mm(ps[7][:, 256 * g:256 * g + 256], Bt[:, 128 * g:128 * g + 128], xd[:, 256 * g:256 * g + 256], True, True, after, g == 1)
                    after = []
                free["Bt"] = [m3]
                free["xd"] = [m3]
                if i == 0:
                    t_state = cpv(state[:, :], ps[7][:, :], [m3] + att_end)
                else:
                    u = tt(h64(state[:, :]), h64(state[:, :]), bc64(v3(dtot[:, :])[:, i, 0:8]), ALU.mult, [t_dtot, t_state, m2])
                    t_state = tt(state[:, :], state[:, :], ps[7][:, :], ALU.add, [u, m3])
                put(7, t_state)
            u = tt(h64(xs[s][:, :]), h64(xs[s][:, :]), bc64(brow[:, 28:36]), ALU.mult, [t_xc, t_xs, d_brow])
            t = tt(y, y, xs[s][:, :], ALU.add, [t, u])
            free["xs"][s] = [t]
            t = tt(y, y, zs[:, i, :], ALU.mult, [t, tk["z", i]])
            u = tt(sq[:, :], y, y, ALU.mult, [t] + att_end + ([u_red] if i else []))
            u_red = red(gs[:, 2 * i:2 * i + 2], sq[:, :].rearrange("p (g n) -> p g n", g=2), ALU.add, [u])
            y_toks.append(t)
        a = act(gs[:, :], gs[:, :], ACT.Sqrt, [u_red, d_cols], bias=col("eps6"), scale=1.0 / 256)
        a = rec(gs[:, :], gs[:, :], [a])
        for i in range(4):
            y = yall[:, i, :]
            for g in range(2):
                t = stt(y[:, 256 * g:256 * g + 256], y[:, 256 * g:256 * g + 256], gs[:, 2 * i + g:2 * i + g + 1],
                        nwr[:, 256 * g:256 * g + 256], ALU.mult, ALU.mult, [a, y_toks[i], d_nwr])
            b = i % 2
            after = take(b) + [t]
            for j in range(4):
                m = tr(ps[b][:, 128 * j:128 * j + 128], y[:, 128 * j:128 * j + 128], after, j == 3)
                after = []
            r = split_ht(slice(2, 6), ps[b][:, :].rearrange("p (k n) -> p k n", k=4), [m], ht_free, slice(128 * i, 128 * i + 128))
            put(b, *r)
            mixed += r
        ssd_end = r + [m] + att_end

        for p in range(2):
            R = Region(mid, TOP)
            R2 = Region(BIG, BIG + 16384)
            gend = ssd_end if p == 0 else gdn_end
            qkv = R([128, 4, 3, 128])
            rsn = R([128, 4, 2, 2])
            qe = R([128, 4, 128])
            kb = R([128, 4, 128])
            rhs = R([128, 4, 2, 128])
            kd = R([128, 4, 128])
            knT = R([128, 4, 128])
            kbT = R([128, 4, 128])
            qnT = R([128, 4, 128])
            qeT = R([128, 4, 128])
            Dg = R2([128, 8, 128])
            QK = R2([128, 8, 128])
            AT = R2([128, 8, 128])
            CT = R2([128, 8, 128])
            R3 = Region(Z0, Z0 + 24576)
            X = R3([128, 8, 128])
            XT = R3([128, 8, 128])
            P1 = R3([128, 8, 128])
            lev = R3([128, 7, 128])
            d_lev = dma(lev[:, :, :], ins["levels"].rearrange("p (a n) -> p a n", a=7), gend)
            wT = R3([128, 4, 128])
            uu2 = R3([128, 2, 4, 64])
            Sg = R([128, 64])
            vn = [R([128, 2, 64]) for _ in range(2)]
            og = R3([128, 4, 128])

            tq = []
            for i in range(4):
                b = i % 2
                after = take(b) + [d_id]
                for j in range(3):
                    m = tr(ps[b][:, 128 * j:128 * j + 128], gT[3 * p + j][:, 128 * i:128 * i + 128], after + [tk["g", 3 * p + j]], j == 2)
                    after = []
                t = cpa(qkv[:, i, :, :], ps[b][:, 0:384].rearrange("p (a n) -> p a n", a=3), [m] + gend)
                put(b, t)
                tq.append(t)

            def hd(t):
                return t.rearrange("p i (h d) -> p i h d", h=2)

            def bcg(t):
                return t.unsqueeze(3).broadcast_to([128, 4, 2, 64])

            for j in range(2):
                t = tt(og[:, :, :], qkv[:, :, j, :], qkv[:, :, j, :], ALU.mult, tq + gend + ([t] if j else []))
                t = red(rsn[:, :, j, :], hd(og[:, :, :]), ALU.add, [t])
            t = act(rsn[:, :, :, :], rsn[:, :, :, :], ACT.Sqrt, [t, d_cols], bias=col("eps6"))
            t_rs = rec(rsn[:, :, :, :], rsn[:, :, :, :], [t])
            t = ts(rsn[:, :, 0, :], rsn[:, :, 0, :], 0.125, None, ALU.mult, after=[t_rs])
            qv, kv, vv = (hd(qkv[:, :, j, :]) for j in range(3))
            hs = slice(8 + 2 * p, 10 + 2 * p)
            egp, dlp, bep = v3(eg)[:, :, hs], v3(dl)[:, :, hs], beta[:, :, 2 * p:2 * p + 2]
            t_qn = tt(qv, qv, bcg(rsn[:, :, 0, :]), ALU.mult, [t])
            t_kn = tt(kv, kv, bcg(rsn[:, :, 1, :]), ALU.mult, [t_rs])
            t_qe = tt(hd(qe[:, :, :]), qv, bcg(egp), ALU.mult, [t_qn, t_eg])
            t_kb = tt(hd(kb[:, :, :]), kv, bcg(bep), ALU.mult, [t_kn, t_beta])
            t_vb = tt(rhs[:, :, :, 0:64], vv, bcg(bep), ALU.mult, [t_beta])
            t_kbe = tt(rhs[:, :, :, 64:128], hd(kb[:, :, :]), bcg(egp), ALU.mult, [t_kb, t_eg])
            t_kd = tt(hd(kd[:, :, :]), kv, bcg(dlp), ALU.mult, [t_kn, t_dl])
            ttr = []
            for n, (src, dst, w) in enumerate([(qkv[:, :, 1, :], knT, t_kn), (kb[:, :, :], kbT, t_kb),
                                               (qkv[:, :, 0, :], qnT, t_qn), (qe[:, :, :], qeT, t_qe)]):
                b = 2 + n % 2
                after = take(b) + [w]
                for i in range(4):
                    m = tr(ps[b][:, 128 * i:128 * i + 128], src[:, i, :], after, i == 3)
                    after = []
                t = cpa(dst[:, :, :], ps[b][:, :].rearrange("p (i n) -> p i n", i=4), [m] + gend)
                put(b, t)
                ttr.append(t)
            td = []
            for n in range(8):
                i, h = n % 4, 8 + 2 * p + n // 4
                b = 4 + n // 4
                after = (take(b) if n % 4 == 0 else []) + [t_da]
                m = mm(ps[b][:, 128 * (n % 4):128 * (n % 4) + 128], v3(da)[:, i, h:h + 1].broadcast_to([128, 128]), U[:, :],
                       True, True, after, n % 4 == 3)
                if n % 4 == 3:
                    for nn in range(n - 3, n + 1):
                        ii, hh = nn % 4, 8 + 2 * p + nn // 4
                        t = ts(Dg[:, nn, :], ps[b][:, 128 * (nn % 4):128 * (nn % 4) + 128], v3(csum)[:, ii, hh:hh + 1], 0.0,
                               ALU.subtract, ALU.min, [m, t_cs] + gend)
                    put(b, t)
                    e = act(Dg[:, n - 3:n + 1, :], Dg[:, n - 3:n + 1, :], ACT.Exp, [t])
                    td.append(tt(Dg[:, n - 3:n + 1, :], Dg[:, n - 3:n + 1, :],
                                 U[:, :].unsqueeze(1).broadcast_to([128, 4, 128]), ALU.mult, [e, d_U]))
            ta, tqk = [], []
            for which, (src, dst, lst) in enumerate([(kbT, AT, ta), (qnT, QK, tqk)]):
                for q4 in range(2):
                    b = 6 + q4 if which == 0 else q4
                    after = take(b) + ttr
                    for n in range(4 * q4, 4 * q4 + 4):
                        i, h = n % 4, n // 4
                        s = slice(64 * h, 64 * h + 64)
                        m = mm(ps[b][:, 128 * (n % 4):128 * (n % 4) + 128], knT[s, i, :], src[s, i, :], True, True, after, n % 4 == 3)
                        after = []
                    t = tt(dst[:, 4 * q4:4 * q4 + 4, :], ps[b][:, :].rearrange("p (n c) -> p n c", n=4), Dg[:, 4 * q4:4 * q4 + 4, :],
                           ALU.mult, [m, td[q4]] + gend)
                    put(b, t)
                    lst.append(t)
            bc8 = [128, 8, 128]
            t_ct = tt(CT[:, :, :], AT[:, :, :], lev[:, 0, :].unsqueeze(1).broadcast_to(bc8), ALU.mult, ta + [d_lev] + gend, q=GE)
            t_xt = tt(XT[:, :, :], ident[:, :].unsqueeze(1).broadcast_to(bc8), CT[:, :, :], ALU.subtract, [t_ct, d_id] + gend)
            t_x = []
            for q4 in range(2):
                b = 2 + q4
                after = take(b) + [t_ct]
                for n in range(4 * q4, 4 * q4 + 4):
                    m = tr(ps[b][:, 128 * (n % 4):128 * (n % 4) + 128], CT[:, n, :], after, n % 4 == 3)
                    after = []
                t = tt(X[:, 4 * q4:4 * q4 + 4, :], ident[:, :].unsqueeze(1).broadcast_to([128, 4, 128]),
                       ps[b][:, :].rearrange("p (n c) -> p n c", n=4), ALU.subtract, [m, d_id] + gend)
                put(b, t)
                t_x.append(t)
            t_xt = [t_xt, t_xt]
            ct_free = [m, t_xt[0]]
            for lv in range(1, 7):
                t_ct = tt(CT[:, :, :], AT[:, :, :], lev[:, lv, :].unsqueeze(1).broadcast_to(bc8), ALU.mult, ct_free + [d_lev], q=GE)
                tp = []
                for q4 in range(2):
                    b = 4 + q4
                    after = take(b) + [t_ct, t_x[q4]]
                    for n in range(4 * q4, 4 * q4 + 4):
                        m = mm(ps[b][:, 128 * (n % 4):128 * (n % 4) + 128], CT[:, n, :], X[:, n, :], True, True, after, n % 4 == 3)
                        after = []
                    t = cpa(P1[:, 4 * q4:4 * q4 + 4, :], ps[b][:, :].rearrange("p (n c) -> p n c", n=4), [m, PE.last])
                    put(b, t)
                    tp.append(t)
                ct_free = [m]
                for q4 in range(2):
                    sl = slice(4 * q4, 4 * q4 + 4)
                    if lv < 6:
                        b = 6 + q4
                        after = take(b) + [tp[q4], t_xt[q4]]
                        for n in range(4 * q4, 4 * q4 + 4):
                            mq = mm(ps[b][:, 128 * (n % 4):128 * (n % 4) + 128], XT[:, n, :], P1[:, n, :], True, True, after, n % 4 == 3)
                            after = []
                    b2 = q4
                    after = take(b2) + [tp[q4], t_xt[q4]]
                    for n in range(4 * q4, 4 * q4 + 4):
                        m = mm(ps[b2][:, 128 * (n % 4):128 * (n % 4) + 128], P1[:, n, :], XT[:, n, :], True, True, after, n % 4 == 3)
                        after = []
                    if lv < 6:
                        t = tt(X[:, sl, :], X[:, sl, :], ps[b][:, :].rearrange("p (n c) -> p n c", n=4), ALU.subtract, [mq, t_x[q4]])
                        put(b, t)
                        t_x[q4] = t
                    t = tt(XT[:, sl, :], XT[:, sl, :], ps[b2][:, :].rearrange("p (n c) -> p n c", n=4), ALU.subtract, [m, t_xt[q4]])
                    put(b2, t)
                    t_xt[q4] = t
                pe_mark()
            after = take(2, 3) + t_xt + [t_vb, t_kbe]
            for n in range(8):
                i, h = n % 4, n // 4
                m1 = mm(ps[2][:, 64 * n:64 * n + 64], XT[:, n, :], rhs[:, i, h, 0:64], True, True, after, n == 7)
                after = []
                m2 = mm(ps[3][64 * h:64 * h + 64, 128 * i:128 * i + 128], rhs[:, i, h, 64:128], XT[:, n, :], True, True, [], n == 7)
            t_u = cpv(uu2[:, :, :, :], ps[2][:, :].rearrange("p (h i d) -> p h i d", i=4, h=2), [m1] + gend)
            t_w = cpa(wT[:, :, :], ps[3][:, :].rearrange("p (i n) -> p i n", i=4), [m2] + gend)
            put(2, t_u)
            put(3, t_w)
            t_S = None
            vn_free = [gend, gend]
            t_o = []
            for i in range(4):
                s = i % 2
                t_v = []
                if i > 0:
                    after = take(4, 2) + [t_w, t_S]
                    for h in range(2):
                        r = slice(64 * h, 64 * h + 64)
                        b = 4 - 2 * h
                        m = mm(ps[b][:, 0:64], wT[r, i, :], Sg[r, :], True, True, after, True)
                        after = []
                        t = tt(vn[s][:, h, :], uu2[:, h, i, :], ps[b][:, 0:64], ALU.subtract, [m, t_u] + vn_free[s])
                        put(b, t)
                        t_v.append(t)
                else:
                    t_v.append(cpv(vn[s][:, :, :], uu2[:, :, i, :], [t_u] + vn_free[s]))
                after = take(5, 6) + tqk + t_v
                for h in range(2):
                    r = slice(64 * h, 64 * h + 64)
                    b = 5 + h
                    if i > 0:
                        mm(ps[b][:, 0:64], qeT[r, i, :], Sg[r, :], True, False, after)
                        after = []
                    mo = mm(ps[b][:, 0:64], QK[:, 4 * h + i, :], vn[s][:, h, :], i == 0, True, after, True)
                    after = []
                    t = cpa(og[:, i, 64 * h:64 * h + 64], ps[b][:, 0:64], [mo, t_kn, t_qn])
                    put(b, t)
                    t_o.append(t)
                if i < 3:
                    after = take(7) + [t_kd] + t_v
                    for h in range(2):
                        m = mm(ps[7][64 * h:64 * h + 64, 0:64], kd[:, i, 64 * h:64 * h + 64], vn[s][:, h, :], True, True, after, h == 1)
                        after = []
                    if i == 0:
                        t_S = cpv(Sg[:, :], ps[7][:, 0:64], [m] + gend)
                    else:
                        t_S = stt(Sg[:, :], Sg[:, :], decS[:, p, i:i + 1], ps[7][:, 0:64], ALU.mult, ALU.add, [m, mo, t_S, t_decS])
                    put(7, t_S)
                    vn_free[s] = [m, mo]
            t = tt(qkv[:, :, 0, :], og[:, :, :], og[:, :, :], ALU.mult, t_o + [PE_tok(PE)])
            t = red(rsn[:, :, 0, :], hd(qkv[:, :, 0, :]), ALU.add, [t])
            t = act(rsn[:, :, 0, :], rsn[:, :, 0, :], ACT.Sqrt, [t], bias=col("eps6"), scale=1.0 / 64)
            t = rec(rsn[:, :, 0, :], rsn[:, :, 0, :], [t])
            t = tt(hd(og[:, :, :]), hd(og[:, :, :]), bcg(rsn[:, :, 0, :]), ALU.mult, [t])
            t = tt(og[:, :, :], og[:, :, :], gz[:, :, 128 * p:128 * p + 128], ALU.mult, [t] + [tk["gz", i] for i in range(4)])
            after = take(2) + [t]
            for i in range(4):
                m = tr(ps[2][:, 128 * i:128 * i + 128], og[:, i, :], after, i == 3)
                after = []
            r = split_ht(6 + p, ps[2][:, :], [m], ht_free, gain=col("gdn_nw"))
            put(2, *r)
            mixed += r
            gdn_end = r + [m]

        def rms_residual(kt, lH, lL, ready, row_j, tmp, tmp_free):
            d_r = row(0, row_j, tmp_free)
            got = {}

            def use_h(h):
                def use(i, b, m):
                    got[i, h] = (b, act(tmp[i % 2][:, 512 * h:512 * h + 512], ps[b][:, :], ACT.Square, [m] + got.get(("t", i % 2, h), tmp_free),
                                        accum=st[:, 16 + 2 * i + h:17 + 2 * i + h]))
                    got["t", i % 2, h] = [got[i, h][1]]
                return use

            tok_group(lH, lL, kt, ready, [0, 1, 2, 3], use_h(0))
            last = tok_group(lH, lL, kt, ready, [4, 5, 6, 7], use_h(1))
            xt = []
            a = red(st[:, 0:4], st[:, 16:24].rearrange("p (i h) -> p i h", h=2), ALU.add, [got[i, h][1] for i in range(4) for h in range(2)])
            a = act(st[:, 4:8], st[:, 0:4], ACT.Sqrt, [a], bias=col("eps6"), scale=1.0 / 1024)
            a = rec(st[:, 8:12], st[:, 4:8], [a])
            w = [[], []]
            for i in range(4):
                o = tmp[i % 2]
                r = []
                for h in range(2):
                    b = got[i, h][0]
                    t = stt(o[:, 512 * h:512 * h + 512], ps[b][:, :], st[:, 8 + i:9 + i], rows[0][:, 512 * h:512 * h + 512],
                            ALU.mult, ALU.mult, [a, d_r] + w[i % 2])
                    put(b, t)
                    r.append(t)
                t = tt(x[:, i, :], x[:, i, :], o[:, :], ALU.add, r, q=GE)
                w[i % 2] = [t]
                xt.append([t])
            return xt, last

        R = Region(BIG, TOP)
        xn = R([128, 4, 1024])
        tmp = [R([128, 1024]) for _ in range(2)]
        xt, last = rms_residual(8, hH, hL, mixed, 0, tmp, gdn_end)
        hT = rms_to_ht(xt, "pre_ffn", xn, [last], gdn_end)
        ht_end = ("s_pe", PE.n)
        hT = hT

        R = Region(BIG, TOP)
        aH = R([128, 22, 512], F32R)
        aL = R([128, 22, 512], F32R)
        TMP = R.at
        ft = [R([128, 512]) for _ in range(6)]
        f_free = [[ht_end] for _ in range(6)]
        a_free = [ht_end]
        atoks = []

        def ffn_pair(t, b, m, m_tile, hold={}):
            if t == 0:
                s = m_tile % 2
                a = act(ft[s][:, :], ps[b][:, :], ACT.Silu, [m] + f_free[s])
                put(b, a)
                hold["g"] = a
            else:
                s = m_tile % 2
                a = tt(ft[2 + s][:, :], ft[s][:, :], ps[b][:, :], ALU.mult, [m, hold["g"]] + f_free[2 + s])
                put(b, a)
                f_free[s] = [a]
                h = act(aH[:, m_tile, :], ft[2 + s][:, :], ACT.Copy, [a] + a_free)
                l = tt(aL[:, m_tile, :], ft[2 + s][:, :], aH[:, m_tile, :].bitcast(F32), ALU.subtract, [a, h] + a_free, q=GE)
                f_free[2 + s] = [h, l]
                atoks.extend([h, l])

        for m_tile in range(22):
            feat_chunk(hT, [2 * (m_tile % 2), 2 * (m_tile % 2) + 1], lambda t, b, m, mt=m_tile: ffn_pair(t, b, m, mt))
        ft_end = [t for f in f_free for t in f]
        tmp = [at(TMP + 4096 * j, [128, 1024]) for j in range(2)]
        xt, last = rms_residual(22, aH, aL, atoks, 1, tmp, ft_end)
        x_end = [t for u in xt for t in u]

        hT = []

        def plain_ht(toks, free):
            r = []

            def use(k, b, m):
                q = split_ht(k, ps[b][:, :], [m], free)
                put(b, *q)
                r.extend(q)

            transposed(x, toks, use, free)
            return r

        hT = plain_ht(xt, [last])
        prev = [last] + x_end
        R = Region(BIG, TOP)
        ckvT = R([128, 512])
        ckv = R([128, 4, 128])
        widx = R([128, 4, 8])
        fin = R([128, 4, 8])
        Q0 = R.at
        qiT = [R([128, 512]) for _ in range(4)]
        kiT = R([128, 512])
        qaT = [R([128, 512]) for _ in range(4)]
        QB = R([66, 8, 512])
        KB = R([66, 8, 512])
        vb = R([128, 4, 512])
        near = R([128, 8, 256])
        CM = R([128, 512])
        selm = R([128, 1280])
        wuk = R([128, 4, 128])
        wuv = R([128, 8, 64])
        anti = R([128, 128])
        oh31 = R([32, 256])
        rb2 = R([32, 8])
        cf = R([8, 2, 512])
        mid = R.at
        d_CM = dma(CM[:, :], ins["causal"], prev)
        d_wuk = dma(wuk[:, :, :], ins["wuk"].rearrange("p (a r) -> p a r", a=4), prev)
        d_wuv = dma(wuv[:, :, :], ins["wuv"].rearrange("p (a r) -> p a r", a=8), prev)
        d_anti = dma(anti[:, :], ins["anti"], prev)
        d_oh = dma(oh31[:, :], ins["oh31"], prev)
        d_rb = dma(rb2[:, :], ins["rel_bias_2"], prev)
        toep = bass.AP(u_dram.tensor, 0, [[1, 128], [384, 8], [1, 256]])
        d_near = dma(near[:, :, :], toep, prev + [d_u])

        def small2(i, b, m):
            a1 = cpa(ckv[:, i, :], ps[b][:, 0:128], [m] + prev)
            a2 = act(widx[:, i, :], ps[b][:, 128:136], ACT.Copy, [m] + prev, scale=8.0 ** -0.5)
            a3 = cpa(fin[:, i, :], ps[b][:, 136:144], [m] + prev)
            put(b, a1, a2, a3)
            tk["ckv", i], tk["widx", i], tk["fin", i] = a1, a2, a3

        tok_group(hH, hL, 8, hT, [0, 1, 2, 3], small2)
        after = take(4) + [d_id]
        for i in range(4):
            m = tr(ps[4][0:8, 128 * i:128 * i + 128], fin[:, i, :], after + [tk["fin", i]], i == 3)
            after = []
        f0, f1 = cf[:, 0, :], cf[:, 1, :]
        R = Region(mid, TOP)
        w0, w1, w2 = (R([8, 512])[:, :] for _ in range(3))
        t = ts(f0, ps[4][0:8, :], cols[0:8, COLS["b_f"]:COLS["b_f"] + 1], -1.0, ALU.add, ALU.mult, [m, d_cols] + prev)
        put(4, t)
        a = stt(w0, f0, -1.0, f0, ALU.mult, ALU.max, [t] + prev)
        a = act(w0, w0, ACT.Exp, [a], scale=-1.0)
        b = ts(w1, w0, 1.0, None, ALU.add, after=[a])
        c = act(w2, w1, ACT.Ln, [b])
        b = ts(w1, w1, -1.0, 1e-30, ALU.add, ALU.max, [b, c])
        d = rec(f1, w1, [b])
        d = tt(f1, f1, w2, ALU.mult, [d, c])
        d = tt(f1, f1, w0, ALU.mult, [d])
        b = ts(w1, w1, 1e-30, None, ALU.is_equal, after=[d])
        b = tt(w1, w1, w0, ALU.mult, [b])
        d = tt(f1, f1, w1, ALU.add, [d, b])
        d = stt(f1, f0, 0.0, f1, ALU.max, ALU.add, [d])
        b = mset(w1, 1.0, [b])
        d = VE.add(lambda e: e.tensor_tensor_scan(f0, w1, f1, 0.0, ALU.mult, ALU.add), [d, b])
        d2 = ts(f1, f0, -1.0, None, ALU.mult, after=[d])
        gate_end = [d2, c]
        a = mset(QB[64:66, :, :], 1.0, prev)
        b = mset(KB[64:66, :, :], 1.0, prev)
        d_q = dma(QB[65:66, :, :], f1, [a, d2])
        d_k = dma(KB[64:65, :, :], f0, [b, d])

        def evac2(name, dst, scale=None):
            def use(b, m):
                tk[name] = act(dst[:, :], ps[b][:, :], ACT.Copy, [m] + prev, scale=scale)
                put(b, tk[name])
            return use

        def evac_heads(name, dst, j, scale=None):
            def use(b, m):
                for h in range(2):
                    o, i = dst[0:64, 2 * j + h, :], ps[b][64 * h:64 * h + 64, :]
                    if h == 0:
                        t = act(o, i, ACT.Copy, [m] + prev, scale=scale)
                    else:
                        t = ts(o, i, 1.0 if scale is None else scale, None, ALU.mult, after=[m] + prev)
                    tk[name, 2 * j + h] = t
                    put(b, t)
            return use

        uses = [evac2(("qi", 0), qiT[0], 0.125), evac2(("qi", 1), qiT[1], 0.125), evac2(("qi", 2), qiT[2], 0.125),
                evac2(("qi", 3), qiT[3], 0.125), evac2("ckvT", ckvT), evac2("ki", kiT)]
        uses += [evac2(("qa", j), qaT[j]) for j in range(4)]
        uses += [evac_heads("QB", QB, j, 0.125) for j in range(4)] + [evac_heads("KB", KB, j) for j in range(4)]
        for j in range(0, len(uses), 2):
            feat_chunk(hT, [4 + j % 4, 5 + j % 4], lambda t, b, m, j=j: uses[j + t](b, m))

        def vb_use(i, b, m):
            tk["vb", i] = cpa(vb[:, i, :], ps[b][:, :], [m] + prev)
            put(b, tk["vb", i])

        ht_free = [tok_group(hH, hL, 8, hT, [0, 1, 2, 3], vb_use)]
        mixed = []

        R = Region(mid, TOP)
        rel = [R([128, 512]) for _ in range(2)]
        sco = R([128, 512])
        m8 = R([128, 8])
        rel_free = [gate_end, gate_end]
        sel_at = [0, 128, 384, 768]
        t_sel = [cpv(selm[:, 0:128], CM[:, 384:512], [d_CM] + prev)]
        sco_end = gate_end
        n_r = 0
        for i in range(1, 4):
            n = 128 * (i + 1)
            acc = None
            for h in range(8):
                b = n_r % 2
                s = slice(64 * (h % 2), 64 * (h % 2) + 64)
                m = mm(ps[b][:, 0:n], qiT[h // 2][s, 128 * i:128 * i + 128], kiT[s, 0:n], True, True,
                       take(b) + [tk["qi", h // 2], tk["ki"]], True)
                a = act(rel[b][:, 0:n], ps[b][:, 0:n], ACT.Relu, [m] + rel_free[b])
                put(b, a)
                w = widx[:, i, h:h + 1]
                prior = CM[:, 512 - n:512] if h == 0 else sco[:, 0:n]
                acc = stt(sco[:, 0:n], rel[b][:, 0:n], w, prior, ALU.mult, ALU.add,
                          [a, tk["widx", i], d_CM] + (sco_end if h == 0 else [acc]))
                rel_free[b] = [acc]
                n_r += 1
            t = acc
            for _ in range(16):
                t = VE.add(lambda e, n=n: e.max(m8[:, :], sco[:, 0:n]), [t])
                t = VE.add(lambda e, n=n: e.match_replace(sco[:, 0:n], m8[:, :], sco[:, 0:n], TAKEN), [t])
            t = ts(selm[:, sel_at[i]:sel_at[i] + n], sco[:, 0:n], TAKEN / 2, NEG, ALU.is_gt, ALU.mult, [t] + prev)
            sco_end = [t]
            t_sel.append(t)
        idx_end = sco_end + rel_free[0] + rel_free[1]

        R = Region(mid, TOP)
        NS = 3
        Sb = [R([128, 512]) for _ in range(NS)]
        Pt = [R([128, 512]) for _ in range(2)]
        RQ = Region(Q0, Q0 + 8192)
        ql = [RQ([128, 512]) for _ in range(2)]
        oa = [RQ([128, 512]) for _ in range(2)]
        sx2 = R([128, NS, 4])
        Sb_free = [list(idx_end) for _ in range(NS)]
        Pt_free = [list(idx_end) for _ in range(2)]
        ql_free = [list(idx_end) for _ in range(2)]
        oa_free = [list(idx_end) for _ in range(2)]
        units = [(kind, h, i) for kind in "BA" for h in range(8) for i in range(4)]
        ql_tok = {}
        soft = {}

        def scores(n):
            kind, h, i = units[n]
            w = 128 * (i + 1)
            s = n % NS
            b = n % 2
            if kind == "A":
                if i == 0:
                    r = slice(64 * (h % 2), 64 * (h % 2) + 64)
                    m = mm(ps[5][:, :], wuk[r, h // 2, :], qaT[h // 2][r, :], True, True, take(5) + [d_wuk, tk["qa", h // 2]], True)
                    ql_tok[h] = act(ql[h % 2][:, :], ps[5][:, :], ACT.Copy, [m] + ql_free[h % 2], scale=0.125)
                    put(5, ql_tok[h])
                mm(ps[b][:, 0:w], ql[h % 2][:, 128 * i:128 * i + 128], ckvT[:, 0:w], True, False, take(b) + [ql_tok[h], tk["ckvT"]])
                k0 = max(i - 1, 0)
                if k0 > 0:
                    mm(ps[b][:, 0:128 * k0], rb2[:, h:h + 1].broadcast_to([32, 128]), oh31[:, 0:128 * k0], False, False, [d_rb, d_oh])
                m = mm(ps[b][:, 128 * k0:w], anti[:, :], near[:, h, (256 - w + 128 * k0):256], False, True, [d_near, d_anti], True)
                if i == 3:
                    ql_free[h % 2] = [m]
                mask = selm[:, sel_at[i]:sel_at[i] + w]
                need = [t_sel[i]]
            else:
                m = mm(ps[b][:, 0:w], QB[:, h, 128 * i:128 * i + 128], KB[:, h, 0:w], True, True,
                       take(b) + [tk["QB", h], tk["KB", h], d_q, d_k], True)
                mask = CM[:, 512 - w:512]
                need = [d_CM]
            mx, sm_, rd = (sx2[:, s, j:j + 1] for j in range(3))
            t = VE.add(lambda e, o=Sb[s][:, 0:w], a=ps[b][:, 0:w], k=mask, c=mx:
                       e.tensor_tensor_reduce(o, a, k, 1.0, 2 * NEG, ALU.add, ALU.max, c), [m] + need + Sb_free[s])
            put(b, t)
            t = ts(mx, mx, -1.0, None, ALU.mult, after=[t])
            t = act(Sb[s][:, 0:w], Sb[s][:, 0:w], ACT.Exp, [t], bias=mx, accum=sm_)
            t = rec(rd, sm_, [t])
            soft[n] = ts(Sb[s][:, 0:w], Sb[s][:, 0:w], rd, None, ALU.mult, after=[t])

        def values(n):
            kind, h, i = units[n]
            w = 128 * (i + 1)
            s = n % NS
            p = n % 2
            b = 2 + n % 2
            after = take(b) + [soft[n]]
            for j in range(i + 1):
                m = tr(ps[b][:, 128 * j:128 * j + 128], Sb[s][:, 128 * j:128 * j + 128], after, j == i)
                after = []
            Sb_free[s] = [m]
            e = cpa(Pt[p][:, 0:w], ps[b][:, 0:w], [m] + Pt_free[p])
            put(b, e)
            r = slice(64 * (h % 2), 64 * (h % 2) + 64)
            for j in range(i + 1):
                if kind == "A":
                    o, l = ps[4][:, 128 * i:128 * i + 128], ckv[:, j, :]
                    after = [e] + [tk["ckv", j]] + (take(4) if i == 0 else [])
                else:
                    ob = 6 + (h // 2) % 2
                    o, l = ps[ob][r, 128 * i:128 * i + 128], vb[:, j, 64 * h:64 * h + 64]
                    after = [e] + [tk["vb", j]] + (take(ob) if i == 0 and h % 2 == 0 else [])
                m = mm(o, l, Pt[p][:, 128 * j:128 * j + 128], j == 0, j == i, after, j == i)
            Pt_free[p] = [m]
            if i < 3:
                return
            if kind == "B":
                if h % 2 == 1:
                    q = split_ht(4 + h // 2, ps[ob][:, :], [m], ht_free)
                    put(ob, *q)
                    mixed.extend(q)
            else:
                t = cpa(oa[h % 2][:, :], ps[4][:, :], [m] + oa_free[h % 2])
                put(4, t)
                ob = 6 + (h // 2) % 2
                m = mm(ps[ob][r, :], wuv[:, h, :], oa[h % 2][:, :], True, True, [t, d_wuv] + (take(ob) if h % 2 == 0 else []), True)
                oa_free[h % 2] = [m]
                if h % 2 == 1:
                    q = split_ht(h // 2, ps[ob][:, :], [m], ht_free)
                    put(ob, *q)
                    mixed.extend(q)

        scores(0)
        scores(1)
        for n in range(len(units)):
            if n + 2 < len(units):
                scores(n + 2)
            values(n)
        att_end = [("s_pe", PE.n), ("s_ve", VE.n), ("s_se", SE.n)]

        def ln_residual(kt, lH, lL, ready):
            toks = [[] for _ in range(4)]

            def use_h(h):
                def use(i, b, m):
                    t = stt(x[:, i, 512 * h:512 * h + 512], x[:, i, 512 * h:512 * h + 512], ALPHA, ps[b][:, :], ALU.mult, ALU.add, [m] + x_end)
                    put(b, t)
                    toks[i].append(t)
                return use

            tok_group(lH, lL, kt, ready, [0, 1, 2, 3], use_h(0))
            last = tok_group(lH, lL, kt, ready, [4, 5, 6, 7], use_h(1))
            return toks, last

        def ln_stage(n, kt, lH, lL, ready, want_ht=True):
            r_g, r_b = row(0, 2 + n, x_end), row(1, 6 + n, x_end)
            toks, last = ln_residual(kt, lH, lL, ready)
            scratch = [at(TMP + 2048 * j, [128, 512])[:, :] for j in range(2)]
            hT, xt = ln_to_ht(toks, n, scratch, [last], r_g, r_b, want_ht)
            return hT, xt, last

        hT, xt, last = ln_stage(0, 8, hH, hL, mixed)
        x_end = [t for u in xt for t in u]

        def conv_ffn(layer, hT, big_free):
            R = Region(BIG, TOP)
            aH = R([128, 22, 512], F32R)
            aL = R([128, 22, 512], F32R)
            ft = [R([128, 512]) for _ in range(6)]
            f_free = [list(big_free) for _ in range(6)]
            atoks = []
            hold = {}
            cw = COLS[f"fcw{layer}"]

            def pair(t, b, m, mt):
                s = 2 * (mt % 2) + t
                w = cw + 3 * (mt + 22 * t)
                y = ft[s]
                a = act(y[:, :], ps[b][:, :], ACT.Identity, [m, d_cols] + f_free[s], scale=cols[:, w + 2:w + 3])
                for d in range(1, 3):
                    a = stt(y[:, d:512], ps[b][:, 0:512 - d], cols[:, w + 2 - d:w + 3 - d], y[:, d:512], ALU.mult, ALU.add, [a])
                put(b, a)
                if t == 0:
                    hold["g"] = act(y[:, :], y[:, :], ACT.Silu, [a])
                else:
                    g = ft[s - 1]
                    o = ft[4 + mt % 2]
                    a = tt(o[:, :], g[:, :], y[:, :], ALU.mult, [a, hold["g"]] + f_free[4 + mt % 2])
                    f_free[s - 1], f_free[s] = [a], [a]
                    h = act(aH[:, mt, :], o[:, :], ACT.Copy, [a] + big_free)
                    l = tt(aL[:, mt, :], o[:, :], aH[:, mt, :].bitcast(F32), ALU.subtract, [a, h] + big_free, q=GE)
                    f_free[4 + mt % 2] = [h, l]
                    atoks.extend([h, l])

            for mt in range(22):
                feat_chunk(hT, [2 * (mt % 2), 2 * (mt % 2) + 1], lambda t, b, m, mt=mt: pair(t, b, m, mt))
            return aH, aL, atoks

        aH, aL, atoks = conv_ffn(0, hT, att_end + hT)
        hT, xt, last = ln_stage(1, 22, aH, aL, atoks)
        x_end = [t for u in xt for t in u]

        prev = [last] + hT
        R = Region(BIG, TOP)
        v1 = R([128, 4, 512])
        vsq = R([128, 4, 512])
        sgg = R([128, 512])
        sgw = R([128, 8, 128])
        sgb = R([1, 1024])
        vst = R([128, 4, 32])
        gcT = [R([128, 516]) for _ in range(2)]
        yc = [R([128, 512]) for _ in range(4)]
        uT = [R([128, 512]) for _ in range(4)]
        od = [R([128, 512]) for _ in range(4)]
        d_sgg = dma(sgg[:, :], ins["sgg"].partition_broadcast(128).rearrange("p a n -> p (a n)"), prev)
        d_sgw = dma(sgw[:, :, :], ins["sgw"].rearrange("p (g t) -> p g t", g=8), prev)
        d_sgb = dma(sgb[:, :], ins["sgb"], prev)
        t_sgw = tt(sgw[:, :, :], sgw[:, :, :], U[:, :].unsqueeze(1).broadcast_to([128, 8, 128]), ALU.mult, [d_sgw, d_U], q=GE)

        def v_use(i, b, m):
            tk["v", i] = act(v1[:, i, :], ps[b][:, :], ACT.Gelu_apprx_tanh, [m] + prev)
            put(b, tk["v", i])

        tok_group(hH, hL, 8, hT, [0, 1, 2, 3], v_use)
        for i in range(4):
            v = h64(v1[:, i, :])
            mu, var = vst[:, i, 0:8], vst[:, i, 8:16]
            t = red(mu, v, ALU.add, [tk["v", i]] + prev)
            t = ts(mu, mu, 1.0 / 64, None, ALU.mult, after=[t])
            t = tt(v, v, bc64(mu), ALU.subtract, [t])
            u = tt(vsq[:, i, :], v1[:, i, :], v1[:, i, :], ALU.mult, [t] + prev, q=GE)
            tk["var", i] = red(var, h64(vsq[:, i, :]), ALU.add, [u])
        a = act(vst[:, :, 16:24], vst[:, :, 8:16], ACT.Sqrt, [tk["var", i] for i in range(4)], bias=col("eps5"), scale=1.0 / 64)
        a = rec(vst[:, :, 24:32], vst[:, :, 16:24], [a])
        t_v = []
        for i in range(4):
            t = tt(h64(v1[:, i, :]), h64(v1[:, i, :]), bc64(vst[:, i, 24:32]), ALU.mult, [a])
            t_v.append(tt(v1[:, i, :], v1[:, i, :], sgg[:, :], ALU.mult, [t, d_sgg]))

        gc_free = [list(prev), list(prev)]
        hold = {}

        def gcz(j):
            def use(t, b, m):
                s = j % 2
                if t == 0:
                    hold["gc"] = cpa(gcT[s][:, 0:512], ps[b][:, :], [m] + gc_free[s])
                    put(b, hold["gc"])
                else:
                    g = gcT[s]
                    a = tt(g[:, 0:512], g[:, 0:512], ps[b][:, :], ALU.mult, [m, hold["gc"]])
                    put(b, a)
                    w = COLS["od_cw"] + 3 * j
                    y = yc[j]
                    c = act(y[:, :], g[:, 0:512], ACT.Identity, [a, d_cols] + prev, scale=cols[:, w + 2:w + 3])
                    for d in range(1, 3):
                        c = stt(y[:, d:512], g[:, 0:512 - d], cols[:, w + 2 - d:w + 3 - d], y[:, d:512], ALU.mult, ALU.add, [c])
                    gc_free[s] = [c]
                    tk["yc", j] = c
            return use

        for j in range(4):
            feat_chunk(hT, [4 + 2 * (j % 2), 5 + 2 * (j % 2)], gcz(j))

        def gb_use(jj):
            def use(t, b, m):
                j = jj + t
                tk["od", j] = tt(od[j][:, :], yc[j][:, :], ps[b][:, :], ALU.mult, [m, tk["yc", j]] + prev)
                put(b, tk["od", j])
            return use

        for j in range(0, 4, 2):
            feat_chunk(hT, [4 + j, 5 + j], gb_use(j))

        def u_use(jj):
            def use(t, b, m):
                j = jj + t
                tk["u", j] = act(uT[j][:, :], ps[b][:, :], ACT.Gelu_apprx_tanh, [m] + prev)
                put(b, tk["u", j])
            return use

        for j in range(0, 4, 2):
            e = feat_chunk(hT, [4 + j, 5 + j], u_use(j))
        ht_free = [e]
        mixed = []
        for j in range(4):
            mixed += split_ht(4 + j, od[j][:, :], [tk["od", j]], ht_free)
            b = j
            after = take(b) + [t_sgw, d_sgb, t_ones] + t_v
            for n in range(4):
                for g in (2 * j, 2 * j + 1):
                    o = ps[b][64 * (g % 2):64 * (g % 2) + 64, 128 * n:128 * n + 128]
                    mm(o, v1[:, n, 64 * g:64 * g + 64], sgw[:, g, :], True, False, after)
                    after = []
                    m = mm(o, ones[0:1, 0:64], sgb[0:1, 128 * g:128 * g + 128], False, True, (), n == 3 and g % 2 == 1)
            t = tt(uT[j][:, :], uT[j][:, :], ps[b][:, :], ALU.mult, [m, tk["u", j]])
            put(b, t)
            mixed += split_ht(j, uT[j][:, :], [t], ht_free)
        odd_end = mixed + [m]

        hT, xt, last = ln_stage(2, 8, hH, hL, mixed)
        x_end = [t for u in xt for t in u]
        aH, aL, atoks = conv_ffn(1, hT, odd_end + hT)
        hT, xt, last = ln_stage(3, 22, aH, aL, atoks, want_ht=False)
        stores = [dma(out[0, 128 * i:128 * i + 128, :], x[:, i, :], xt[i]) for i in range(4)]
        SP.items.append((stores + [d_u], lambda e: None, False))

        block = ctx.enter_context(nc.Block())

        @block.sync
        def _(e):
            SP.emit(e)

        @block.gpsimd
        def _(e):
            GE.emit(e)

        @block.scalar
        def _(e):
            SE.emit(e)

        @block.vector
        def _(e):
            VE.emit(e)

        @block.tensor
        def _(e):
            PE.emit(e)


def PE_tok(q):
    return (q.sem, q.n)


def shape_constants():
    f = np.float32
    i, j = np.arange(128)[:, None], np.arange(128)[None, :]
    out = {"ident": np.eye(128, dtype=f), "anti": np.eye(128, dtype=f)[::-1], "triu": (i <= j).astype(f)}
    r, c = np.arange(128)[:, None], np.arange(256)[None, :]
    ok = ((c // 64) >= (r // 64)) & ((c // 64) <= (r // 64) + 2)
    dist = np.abs(r + 128 - c)
    out["abias"] = np.concatenate([np.where(ok, -(2.0 ** (-8.0 * h / 4)) * dist, NEG) for h in range(1, 5)], axis=1).astype(f)
    out["levels"] = np.concatenate([((i // b) % 2 == 0) & ((j // b) == (i // b) + 1) for b in (1, 2, 4, 8, 16, 32, 64)], axis=1).astype(f)
    out["causal"] = np.where(384 + i - np.arange(512)[None, :] >= 0, 0.0, NEG).astype(f)
    n = np.maximum(255 - np.arange(384), 0)
    large = 16 + (np.log(np.maximum(n, 1) / 16) / math.log(128 / 16) * 16).astype(np.int64)
    bucket = np.where(n < 16, n, np.minimum(large, 31))
    out["oneh"] = (np.arange(32)[:, None] == bucket[None, :]).astype(f)
    out["oh31"] = np.repeat((np.arange(32)[:, None] == 31).astype(f), 256, axis=1)
    return out


def kernel(**inputs):
    import concourse.bacc as bacc
    from concourse.bass_utils import run_bass_kernel_spmd

    a = {k: np.asarray(v) for k, v in inputs.items()}
    chunks = []
    for name, layer, k0, nk, cols in weight_plan():
        if name == "gate_up":
            w = np.concatenate([a[n][0][:, 128 * cols:128 * cols + 128] for n in ("ffn_w_gate", "ffn_w_up")], axis=1)
        else:
            w = a[name][layer][128 * k0:128 * (k0 + nk)]
            if cols == rng(cols[0], len(cols)):
                w = w[:, cols[0]:cols[0] + len(cols)]
            else:
                w = w[:, np.array(cols)]
        chunks.append(w.reshape(nk, 128, -1).transpose(1, 0, 2).reshape(-1))
    arrays = {"wbig": np.concatenate(chunks), "x": a["x"], "rel_bias_2": a["rel_bias_2"]}

    def tiles(v):
        return v.reshape(-1, 128).T

    def taps_(w):
        k, n = w.shape
        return w.reshape(k, n // 128, 128).transpose(2, 1, 0).reshape(128, -1)

    eps = np.full((128, 1), 1e-6, np.float32), np.full((128, 1), 1e-5, np.float32)
    bf = np.concatenate([a["ev_b_f_2"][0], np.zeros(120, np.float32)])[:, None]
    parts = [tiles(a["pre_mix_norm"][0]), tiles(a["pre_ffn_norm"][0]), taps_(a["ssd_conv_w"][0]), tiles(a["ssd_conv_b"][0]),
             taps_(a["gdn_conv_w"][0]), np.concatenate([a["gdn_norm_w"][0]] * 2)[:, None],
             tiles(a["ln_g_2"].reshape(-1)), tiles(a["ln_b_2"].reshape(-1)), taps_(a["od_conv_w_2"][0]), bf, *eps,
             taps_(a["ffn_conv_w_2"][0]), taps_(a["ffn_conv_w_2"][1])]
    arrays["cols"] = np.ascontiguousarray(np.concatenate(parts, axis=1))
    arrays["rows"] = np.concatenate([a["post_mix_norm"], a["post_ffn_norm"], a["ln_g_2"].reshape(4, 1024), a["ln_b_2"].reshape(4, 1024)], axis=0)
    arrays["brow"] = np.concatenate([a["ssd_dt_bias"][0], a["gdn_dt_bias"][0], a["ssd_A_log"][0], a["gdn_A_log"][0],
                                     a["attn_sinks"][0], a["ssd_D"][0], np.zeros(12, np.float32)])[None, :]
    arrays["ssd_nw"] = a["ssd_norm_w"]
    arrays["wuk"] = np.ascontiguousarray(a["ev_w_uk_2"][0].reshape(4, 2, 128, 64).transpose(1, 3, 0, 2).reshape(128, 512))
    arrays["wuv"] = np.ascontiguousarray(a["ev_w_uv_2"][0].transpose(1, 0, 2).reshape(128, 512))
    arrays["sgg"] = a["od_sgu_g_2"].reshape(1, 512)
    arrays["sgw"] = np.ascontiguousarray(a["od_sgu_w_2"][0].transpose(2, 0, 1).reshape(128, 1024))
    arrays["sgb"] = a["od_sgu_b_2"].reshape(1, 1024)
    arrays.update(shape_constants())
    arrays = {k: np.ascontiguousarray(v) for k, v in arrays.items()}

    nc = bacc.Bacc("TRN2", target_bir_lowering=False, num_devices=1)
    ins = {k: nc.dram_tensor("in_" + k, v.shape, mybir.dt.from_np(v.dtype), kind="ExternalInput").ap() for k, v in arrays.items()}
    out = nc.dram_tensor("out_0", (1, 512, 1024), F32, kind="ExternalOutput").ap()
    build(nc, ins, out)
    r = run_bass_kernel_spmd(nc, [{"in_" + k: v for k, v in arrays.items()}], core_ids=[0])
    return r.results[0]["out_0"]
```

```python
import math
from contextlib import ExitStack

import numpy as np
import concourse.bass as bass
from concourse import mybir

ALU = mybir.AluOpType
ACT = mybir.ActivationFunctionType
F32 = mybir.dt.float32
F32R = mybir.dt.float32r
AXX = mybir.AxisListType.X
NEG = -1.0e30
TAKEN = -3.0e38
ALPHA = 4.0 ** 0.25


def rng(a, n):
    return list(range(a, a + n))


def weight_plan():
    plan = []

    def feat(name, layer, *tiles):
        cols = [c for t in tiles for c in t]
        plan.append((name, layer, 0, 8, cols))

    def tok(name, layer, cols, kt=8):
        step = min(kt, 2048 // len(cols))
        for k in range(0, kt, step):
            plan.append((name, layer, k, min(step, kt - k), cols))

    w = "w_in"
    t = [rng(0, 64) + rng(128, 64), rng(64, 64) + rng(192, 64), rng(256, 128)]
    t += [rng(1024 + 128 * j, 128) for j in range(8)]
    g = [rng(2056 + 256 * kind + 128 * pair, 128) for pair in range(2) for kind in range(3)]
    xbc = t[3:]
    tok(w, 0, rng(384, 128) + rng(2048, 8) + rng(3084, 4) + rng(3080, 4) + rng(2824, 256))
    t = [g[0], g[1], g[2], t[0], t[1], t[2], g[3], g[4], g[5]] + xbc[4:] + xbc[:4]
    for j in range(0, 17, 2):
        feat(w, 0, *t[j:j + 2])
    tok(w, 0, rng(512, 256))
    tok(w, 0, rng(768, 256))
    for h in range(2):
        tok("w_out", 0, rng(512 * h, 512))
    for m in range(22):
        plan.append(("gate_up", 0, 0, 8, m))
    for h in range(2):
        tok("ffn_w_down", 0, rng(512 * h, 512), 22)
    w = "ev_w_in_2"
    tok(w, 0, rng(512, 128) + rng(1216, 8) + rng(2760, 8))
    feat(w, 0, rng(640, 128), rng(768, 128))
    feat(w, 0, rng(896, 128), rng(1024, 128))
    feat(w, 0, rng(512, 128), rng(1152, 64) + rng(1152, 64))
    tok(w, 0, rng(2248, 256))
    tok(w, 0, rng(2504, 256))
    for j in range(4):
        feat(w, 0, rng(1224 + 128 * j, 128), rng(1736 + 128 * j, 128))
    for j in range(2):
        feat(w, 0, rng(256 * j, 128), rng(256 * j + 128, 128))
    for h in range(2):
        tok("ev_w_o_2", 0, rng(512 * h, 512))

    def conv_ffn(layer):
        for m in range(22):
            feat("ffn_w_up_2", layer, rng(128 * m, 128), rng(2816 + 128 * m, 128))
        for h in range(2):
            tok("ffn_w_down_2", layer, rng(512 * h, 512), 22)

    conv_ffn(0)
    w = "od_w_in_2"
    tok(w, 0, rng(512, 512))
    for j in range(4):
        feat(w, 0, rng(1536 + 128 * j, 128), rng(2048 + 128 * j, 128))
    for j in range(2):
        feat(w, 0, rng(1024 + 256 * j, 128), rng(1024 + 256 * j + 128, 128))
    for j in range(2):
        feat(w, 0, rng(256 * j, 128), rng(256 * j + 128, 128))
    for h in range(2):
        tok("od_w_o_2", 0, rng(512 * h, 512))
    conv_ffn(1)
    return plan


def chunk_width(c):
    return c[3] * (256 if c[0] == "gate_up" else len(c[4]))


RATE1 = 1.5
RATE2 = 1.5

COLS = {}
NCOLS = 0
for _n, _w in [("pre_mix", 8), ("pre_ffn", 8), ("ssd_cw", 32), ("ssd_cb", 8), ("gdn_cw", 24), ("gdn_nw", 1),
               ("ln_g", 32), ("ln_b", 32), ("od_cw", 12), ("b_f", 1), ("eps6", 1), ("eps5", 1),
               ("fcw0", 132), ("fcw1", 132)]:
    COLS[_n] = NCOLS
    NCOLS += _w


def build(nc, ins, out):
    plan = weight_plan()
    offs = [0]
    for c in plan:
        offs.append(offs[-1] + 128 * chunk_width(c))

    u_dram = nc.dram_tensor("u_scratch", (8, 384), F32, kind="Internal").ap()

    ctx = ExitStack()
    with ctx:
        names = [0]
        base = (nc.sbuf_base + 63) // 64 * 64

        def at(offset, shape, dt=F32):
            names[0] += 1
            return nc.alloc_sbuf_tensor_at(f"t{names[0]}", shape, dt, offset=base + offset)

        class Region:
            def __init__(self, start, end):
                self.at, self.end = start, end

            def __call__(self, shape, dt=F32):
                n = 4
                for s in shape[1:]:
                    n *= s
                n = (n + 63) // 64 * 64
                assert self.at + n <= self.end, (self.at, n, self.end)
                t = at(self.at, shape, dt)
                self.at += n
                return t

        TOP = nc.sbuf_usable_end - base
        R0 = Region(0, TOP)
        raw = [R0([128, 2048]) for _ in range(2)]
        wH = [R0([128, 2048], F32R) for _ in range(2)]
        wL = [R0([128, 2048], F32R) for _ in range(2)]
        x = R0([128, 4, 1024])
        hH = R0([128, 8, 512], F32R)
        hL = R0([128, 8, 512], F32R)
        ident = R0([128, 128])
        U = R0([128, 128])
        ones = R0([128, 128])
        cols = R0([128, NCOLS])
        brow = R0([128, 48])
        rows = [R0([128, 1024]) for _ in range(2)]
        st = R0([128, 80])
        BIG = R0.at

        ps = [ctx.enter_context(nc.psum_tensor(f"ps{i}", [128, 512], F32)) for i in range(8)]
        bank = [[] for _ in range(8)]

        def take(*ids):
            r = []
            for i in ids:
                r += bank[i]
                bank[i] = []
            return r

        def put(i, *toks):
            bank[i] = bank[i] + list(toks)

        sems = {}

        def sem(name):
            sems[name] = ctx.enter_context(nc.semaphore(name))
            return name

        class Queue:
            def __init__(self, name):
                self.sem, self.n, self.items = sem("s_" + name), 0, []

            def add(self, fn, after, sig=True):
                if sig:
                    self.n += 1
                self.items.append((list(after), fn, sig))
                return (self.sem, self.n) if sig else None

            def emit(self, eng):
                seen = {}
                for after, fn, sig in self.items:
                    for t in after:
                        if t is not None and seen.get(t[0], 0) < t[1]:
                            eng.wait_ge(sems[t[0]], t[1])
                            seen[t[0]] = t[1]
                    i = fn(eng)
                    if sig is True:
                        i.then_inc(sems[self.sem], 1)
                    elif sig:
                        i.then_inc(sems[sig], 16)

        PE, VE, SE, GE, SP = Queue("pe"), Queue("ve"), Queue("se"), Queue("ge"), Queue("sp")

        ndma = [0]

        def dma(dst, src, after=(), name=None, count=1, q=SP):
            if name is None:
                ndma[0] += 1
                name = sem(f"d{ndma[0]}")
            q.items.append((list(after), lambda e: e.dma_start(dst, src), name))
            return (name, 16 * count)

        def mm(o, l, r, start, stop, after=(), sig=False):
            return PE.add(lambda e: e.matmul(o, l, r, start=start, stop=stop), after, sig)

        def tr(o, i, after=(), sig=False):
            n = i.shape[0]
            return PE.add(lambda e: e.transpose(o, i, ident[0:n, 0:n]), after, sig)

        def act(o, i, f, after=(), bias=None, scale=None, accum=None):
            kw = {}
            if bias is not None:
                kw["bias"] = bias
            if scale is not None:
                kw["scale"] = scale
            if accum is not None:
                kw["accum_out"] = accum
            return SE.add(lambda e: e.activation(o, i, f, **kw), after)

        def cpa(o, i, after=()):
            return act(o, i, ACT.Copy, after)

        def tt(o, a, b, op, after=(), q=VE):
            return q.add(lambda e: e.tensor_tensor(o, a, b, op), after)

        def ts(o, a, s1, s2, op0, op1=ALU.bypass, after=(), q=VE):
            if s2 is None:
                return q.add(lambda e: e.tensor_scalar(o, a, s1, None, op0), after)
            return q.add(lambda e: e.tensor_scalar(o, a, s1, s2, op0, op1), after)

        def stt(o, a, s, b, op0, op1, after=()):
            return VE.add(lambda e: e.scalar_tensor_tensor(o, a, s, b, op0, op1), after)

        def cpv(o, i, after=(), q=VE):
            return q.add(lambda e: e.tensor_copy(o, i), after)

        def rec(o, i, after=()):
            return VE.add(lambda e: e.reciprocal(o, i), after)

        def red(o, i, op, after=(), negate=None):
            return VE.add(lambda e: e.tensor_reduce(o, i, AXX, op, negate=negate), after)

        def mset(o, v, after=(), q=VE):
            return q.add(lambda e: e.memset(o, v), after)

        def col(name, j=0):
            return cols[:, COLS[name] + j:COLS[name] + j + 1]

        d_cols = dma(cols[:, :], ins["cols"])
        d_x = [dma(x[:, i, :], ins["x"][0, 128 * i:128 * i + 128, :]) for i in range(4)]
        d_id = dma(ident[:, :], ins["ident"])
        d_U = dma(U[:, :], ins["triu"])
        d_brow = dma(brow[:, 0:48], ins["brow"].partition_broadcast(128).rearrange("p a n -> p (a n)"))
        t_ones = mset(ones[:, :], 1.0)

        raw_free = [[], []]
        hl_free = [[], []]
        landed = {}
        halves = {}
        w_sem = [sem("d_w0"), sem("d_w1")]

        def load(c):
            if c >= len(plan):
                return
            n = chunk_width(plan[c])
            r = c % 2
            src = ins["wbig"][offs[c]:offs[c + 1]].rearrange("(p n) -> p n", p=128)
            landed[c] = dma(raw[r][:, 0:n], src, raw_free[r], w_sem[r], c // 2 + 1)

        def split(c):
            if c >= len(plan) or c in halves:
                return
            n = chunk_width(plan[c])
            r = c % 2
            a = act(wH[r][:, 0:n], raw[r][:, 0:n], ACT.Copy, [landed[c]] + hl_free[r])
            b = tt(wL[r][:, 0:n], raw[r][:, 0:n], wH[r][:, 0:n].bitcast(F32), ALU.subtract, [landed[c], a] + hl_free[r])
            raw_free[r] = [b]
            halves[c] = [a, b]
            load(c + 2)

        load(0)
        load(1)
        chunk = [0]

        def weights():
            c = chunk[0]
            split(c)
            split(c + 1)
            n = chunk_width(plan[c])
            r = c % 2
            k = plan[c][3]
            return (c, wH[r][:, 0:n].rearrange("p (k c) -> p k c", k=k),
                    wL[r][:, 0:n].rearrange("p (k c) -> p k c", k=k), halves[c])

        def weights_done(tok):
            hl_free[chunk[0] % 2] = [tok]
            chunk[0] += 1

        class Background:

            def __init__(self):
                self.chains, self.rate, self.credit, self.turn = [], 0.0, 0.0, 0

            def add(self, chain, rate=None):
                self.chains.append(chain)
                if rate is not None:
                    self.rate = rate

            def advance(self):
                c = self.chains[self.turn % len(self.chains)]
                for _ in c:
                    self.turn += 1
                    return
                self.chains.remove(c)

            def step(self):
                self.credit += self.rate
                while self.credit >= 1 and self.chains:
                    self.credit -= 1
                    self.advance()
                if not self.chains:
                    self.credit = 0.0

            def finish(self):
                while self.chains:
                    self.advance()

        bg = Background()

        def feat_chunk(ready, banks, use):
            c, H, L, w = weights()
            nt = plan_cols(c) // 128
            for t in range(nt):
                b = banks[t]
                s = slice(128 * t, 128 * t + 128)
                after = w + take(b)
                for k in range(8):
                    mm(ps[b][:, :], H[:, k, s], hH[:, k, :], k == 0, False, after + ready[k])
                    after = []
                    mm(ps[b][:, :], H[:, k, s], hL[:, k, :], False, False)
                    m = mm(ps[b][:, :], L[:, k, s], hH[:, k, :], False, k == 7, (), k == 7)
                    if k % 2 == 1 and k < 7:
                        bg.step()
                if t == nt - 1:
                    weights_done(m)
                use(t, b, m)
                bg.step()
            return m

        def plan_cols(c):
            return 256 if plan[c][0] == "gate_up" else len(plan[c][4])

        def tok_group(lH, lL, kt, ready, banks, use):
            k0 = 0
            while k0 < kt:
                c, H, L, w = weights()
                nk, n = plan[c][3], len(plan[c][4])
                done = k0 + nk == kt
                for i in range(4):
                    b = banks[i]
                    s = slice(128 * i, 128 * i + 128)
                    after = w + (take(b) if k0 == 0 else [])
                    for k in range(nk):
                        e = done and k == nk - 1
                        mm(ps[b][:, 0:n], lH[:, k0 + k, s], H[:, k, :], k0 + k == 0, False, after + ready[k0 + k])
                        after = []
                        mm(ps[b][:, 0:n], lH[:, k0 + k, s], L[:, k, :], False, False)
                        m = mm(ps[b][:, 0:n], lL[:, k0 + k, s], H[:, k, :], False, e, (), k == nk - 1)
                        if k % 4 == 3 and k < nk - 1:
                            bg.step()
                    if i == 3:
                        weights_done(m)
                    if done:
                        use(i, b, m)
                    bg.step()
                k0 += nk
            return m

        def split_ht(k, src, after, free, cs=slice(0, 512), gain=None):
            if gain is None:
                a = act(hH[:, k, cs], src, ACT.Copy, after + free)
                b = tt(hL[:, k, cs], src, hH[:, k, cs].bitcast(F32), ALU.subtract, [a] + after + free)
            else:
                a = act(hH[:, k, cs], src, ACT.Identity, after + free, scale=gain)
                b = stt(hL[:, k, cs], src, gain, hH[:, k, cs].bitcast(F32), ALU.mult, ALU.subtract, [a] + after + free)
            return [a, b]

        def row(slot, j, after=()):
            return dma(rows[slot][:, :], ins["rows"][j:j + 1, :].partition_broadcast(128).rearrange("p a n -> p (a n)"), after)

        def transposed(src, toks, use, free):
            for k in range(8):
                after = take(k) + [d_id]
                for i in range(4):
                    m = tr(ps[k][:, 128 * i:128 * i + 128], src[:, i, 128 * k:128 * k + 128], after + toks[i], i == 3)
                    after = []
                use(k, k, m)

        def rms_to_ht(toks, gain, xn, free, xn_free):
            ready = []
            ntok = []
            for i in range(4):
                a = act(xn[:, i, :], x[:, i, :], ACT.Square, toks[i] + xn_free, accum=st[:, i:i + 1])
                a = act(st[:, 4 + i:5 + i], st[:, i:i + 1], ACT.Sqrt, [a, d_cols], bias=col("eps6"), scale=1.0 / 1024)
                a = rec(st[:, 8 + i:9 + i], st[:, 4 + i:5 + i], [a])
                ntok.append([ts(xn[:, i, :], x[:, i, :], st[:, 8 + i:9 + i], None, ALU.mult, after=[a])])

            def use(k, b, m):
                r = split_ht(k, ps[b][:, :], [m], free, gain=col(gain, k))
                put(b, *r)
                ready.append(r)

            transposed(xn, ntok, use, free)
            return ready

        def ln_to_ht(toks, n, scratch, free, r_g, r_b, want_ht, store=None):
            ready, ntok, xtok = [], [], []
            stats = st[:, 32:56].rearrange("p (a b c) -> p a b c", a=2, b=2)
            last = [None, None]
            for i in range(4):
                sl = stats[:, i % 2, :, :]
                a = []
                for h in range(2):
                    a.append(VE.add(lambda e, o=sl[:, h, :], s=x[:, i, 512 * h:512 * h + 512]: e.bn_stats(o, s),
                                    toks[i] + [last[i % 2]]))
                mv = st[:, 56 + 4 * i:58 + 4 * i]
                a = VE.add(lambda e, o=mv, s=sl: e.bn_aggr(o, s), a)
                last[i % 2] = a
                a = act(st[:, 58 + 4 * i:59 + 4 * i], mv[:, 1:2], ACT.Sqrt, [a, d_cols], bias=col("eps5"))
                a = rec(st[:, 59 + 4 * i:60 + 4 * i], st[:, 58 + 4 * i:59 + 4 * i], [a])
                a = ts(x[:, i, :], x[:, i, :], mv[:, 0:1], st[:, 59 + 4 * i:60 + 4 * i], ALU.subtract, ALU.mult, [a])
                ntok.append([a])
            g_at, b_at = COLS["ln_g"] + 8 * n, COLS["ln_b"] + 8 * n
            if want_ht:
                sfree = [[], []]

                def use(k, b, m):
                    s = k % 2
                    a = act(scratch[s], ps[b][:, :], ACT.Identity, [m, d_cols] + sfree[s], bias=cols[:, b_at + k:b_at + k + 1],
                            scale=cols[:, g_at + k:g_at + k + 1])
                    put(b, a)
                    h = cpv(hH[:, k, :], scratch[s], [a] + free)
                    l = tt(hL[:, k, :], scratch[s], hH[:, k, :].bitcast(F32), ALU.subtract, [a, h] + free)
                    sfree[s] = [h, l]
                    ready.append([h, l])

                transposed(x, ntok, use, free)
            for i in range(4):
                w = [(PE.sem, PE.n)] if want_ht else []
                a = tt(x[:, i, :], x[:, i, :], rows[0][:, :], ALU.mult, ntok[i] + [r_g] + w, q=GE)
                a = tt(x[:, i, :], x[:, i, :], rows[1][:, :], ALU.add, [a, r_b], q=GE)
                xtok.append([a])
            return ready, xtok

        PE.last = None

        def pe_mark():
            PE.last = ("s_pe", PE.n)
            return PE.last

        R = Region(BIG, TOP)
        GD = R.at
        xn = R([128, 4, 1024])
        R = Region(GD + 30720, TOP)
        gT = [R([128, 512]) for _ in range(6)]
        xT = [R([128, 512]) for _ in range(8)]
        zs = R([128, 4, 512])
        gz = R([128, 4, 256])
        og0 = R([128, 4, 128])
        lev = R([128, 7, 128])
        sm = R([128, 4, 16])
        sp = R([128, 9, 48])
        dtot = R([128, 48])
        beta = R([128, 4, 4])
        an = R([128, 12])
        decS = R([128, 2, 4])
        gs = R([128, 8])
        rsn = R([128, 4, 2, 2])
        AS = R.at
        R = Region(AS, TOP)
        qT = [R([128, 512]) for _ in range(2)]
        kT = R([128, 512])
        vtm = R([128, 4, 128])
        abias = R([128, 4, 256])
        S = R([128, 4, 256])
        PT = R([128, 8, 128])
        sx = R([128, 5, 4])
        R = Region(GD, GD + 6144)
        attT = at(GD + 30720, [128, 2, 512])
        og1 = at(GD + 30720 + 4096, [128, 4, 128])
        d_lev = dma(lev[:, :, :], ins["levels"].rearrange("p (a n) -> p a n", a=7))
        d_ab = dma(abias[:, :, :], ins["abias"].rearrange("p (h n) -> p h n", h=4))

        xtok = [[t] for t in d_x]
        hT = rms_to_ht(xtok, "pre_mix", xn, [], [])
        xn_done = [(PE.sem, PE.n)]

        R = Region(AS, TOP)
        oneh = R([32, 384])
        rb = R([32, 8])
        uu = R([8, 384])
        d1 = dma(oneh[:, :], ins["oneh"])
        d2 = dma(rb[:, :], ins["rel_bias_2"])
        m = mm(ps[7][0:8, 0:384], rb[:, :], oneh[:, :], True, True, take(7) + [d1, d2], True)
        a = cpa(uu[:, :], ps[7][0:8, 0:384], [m])
        put(7, a)
        d_u = dma(u_dram, uu[:, :], [a])
        as_free = [m, d_u]

        y_tmp = [rows[j // 2][:, 512 * (j % 2):512 * (j % 2) + 512] for j in range(4)]
        y_free = [[] for _ in range(4)]
        tk = {}

        def small_use(i, b, m):
            a1 = cpa(vtm[:, i, :], ps[b][:, 0:128], [m] + as_free)
            a2 = cpa(sm[:, i, :], ps[b][:, 128:144], [m])
            a3 = act(gz[:, i, :], ps[b][:, 144:400], ACT.Silu, [m])
            put(b, a1, a2, a3)
            tk["v", i], tk["sm", i], tk["gz", i] = a1, a2, a3

        tok_group(hH, hL, 8, hT, [0, 1, 2, 3], small_use)

        n_conv = [0]

        def conv4(b, m, o, w, bias):
            j = n_conv[0] % 4
            n_conv[0] += 1
            y = y_tmp[j]
            p = ps[b]
            a = act(y, p[:, :], ACT.Identity, [m, d_cols] + y_free[j], scale=cols[:, w + 3:w + 4])
            for d in range(1, 4):
                a = stt(y[:, d:512], p[:, 0:512 - d], cols[:, w + 3 - d:w + 4 - d], y[:, d:512], ALU.mult, ALU.add, [a])
            put(b, a)
            kw = {} if bias is None else {"bias": bias}
            a = act(o[:, :], y, ACT.Silu, [a], **kw)
            y_free[j] = [a]
            return a

        def v3(t, n=12):
            return t.rearrange("p (i h) -> p i h", h=n)

        e0, e1, e2, e3, da = (sp[:, j, :] for j in range(5))
        csum, tot = sp[:, 5, :], sp[:, 6, :]
        eg, dl = sp[:, 7, :], sp[:, 8, :]

        def steps():
            t_sm = [tk["sm", i] for i in range(4)]
            a = tt(v3(e0), sm[:, :, 0:12], brow[:, 0:12].unsqueeze(1).broadcast_to([128, 4, 12]), ALU.add, t_sm + [d_brow])
            b = stt(e1, e0, -1.0, e0, ALU.mult, ALU.max, [a])
            b = act(e1, e1, ACT.Exp, [b], scale=-1.0)
            c = ts(e2, e1, 1.0, None, ALU.add, after=[b])
            d = act(e3, e2, ACT.Ln, [c])
            a2 = act(an[:, :], brow[:, 12:24], ACT.Exp, [d_brow])
            a3 = act(beta[:, :, :], sm[:, :, 12:16], ACT.Exp, t_sm, scale=-1.0)
            c = ts(e2, e2, -1.0, 1e-30, ALU.add, ALU.max, [c, d])
            c = rec(da, e2, [c])
            c = tt(da, da, e3, ALU.mult, [c, d])
            c = tt(da, da, e1, ALU.mult, [c])
            f = ts(e2, e2, 1e-30, None, ALU.is_equal, after=[c])
            f = tt(e2, e2, e1, ALU.mult, [f])
            c = tt(da, da, e2, ALU.add, [c, f])
            c = stt(e0, e0, 0.0, da, ALU.max, ALU.add, [c])
            tk["dt"] = c
            a2 = ts(an[:, :], an[:, :], -1.0, None, ALU.mult, after=[a2])
            tk["da"] = tt(v3(da), v3(e0), an[:, :].unsqueeze(1).broadcast_to([128, 4, 12]), ALU.mult, [c, a2])
            a3 = ts(beta[:, :, :], beta[:, :, :], 1.0, None, ALU.add, after=[a3])
            tk["beta"] = rec(beta[:, :, :], beta[:, :, :], [a3])
            yield
            yield
            m1 = mm(ps[7][:, 0:48], U[:, :], da, True, True, take(7) + [tk["da"], d_U], True)
            m2 = mm(ps[7][:, 64:112], ones[:, :], da, True, True, [t_ones], True)
            t_cs = cpv(csum, ps[7][:, 0:48], [m1, m2])
            t_tot = cpv(tot, ps[7][:, 64:112], [m2])
            put(7, t_cs, t_tot)
            a = tt(dl, tot, csum, ALU.subtract, [t_cs, t_tot])
            tk["dl"] = act(dl, dl, ACT.Exp, [a])
            tk["eg"] = act(eg, csum, ACT.Exp, [t_cs])
            tk["dtot"] = act(dtot[:, :], tot, ACT.Exp, [t_tot])
            for p in range(2):
                for h in range(2):
                    tk["decS"] = cpv(decS[64 * h:64 * h + 64, p, :], v3(dtot[64 * h:64 * h + 64, :])[:, :, 8 + 2 * p + h], [tk["dtot"]])
            tk["cs"] = t_cs
            yield

        sink = brow[:, 24:28]

        def attention(bA, bB):
            vts = [tk["v", i] for i in range(4)]
            S_free, PT_free = [], []
            for i in range(4):
                k0 = 128 * max(i - 1, 0)
                n = 128 * (i + 1) - k0
                nb = n // 128
                r = []
                for h in range(4):
                    b = (bA, bB)[h // 2]
                    p = slice(64 * (h // 2), 64 * (h // 2) + 64)
                    after = [tk["qA"], tk["qB"], tk["k"]] + (take(b) if h % 2 == 0 else [])
                    m = mm(ps[b][:, 256 * (h % 2):256 * (h % 2) + n], qT[h % 2][p, 128 * i:128 * i + 128],
                           kT[p, k0:k0 + n], True, True, after, h % 2 == 1)
                    if h % 2 == 1:
                        v = ps[b][:, :].rearrange("p (h n) -> p h n", h=2)[:, :, 0:n]
                        t = tt(S[:, h - 1:h + 1, 0:n], v, abias[:, h - 1:h + 1, 256 - n:256], ALU.add, [m, d_ab] + S_free + as_free)
                        put(b, t)
                        r.append(t)
                yield
                mx, nm, sume, es, rd = (sx[:, j, :] for j in range(5))
                t = red(mx, S[:, :, 0:n], ALU.max, r + S_free)
                t = tt(mx, mx, sink, ALU.max, [t, d_brow])
                u = tt(es, sink, mx, ALU.subtract, [t])
                t = ts(nm, mx, -1.0, None, ALU.mult, after=[t])
                e = []
                for h in range(4):
                    e.append(act(S[:, h, 0:n], S[:, h, 0:n], ACT.Exp, [t], bias=nm[:, h:h + 1], accum=sume[:, h:h + 1]))
                e.append(act(es, es, ACT.Exp, [u]))
                t = tt(rd, sume, es, ALU.add, e)
                t = rec(rd, rd, [t])
                t = tt(S[:, :, 0:n], S[:, :, 0:n], rd.unsqueeze(2).broadcast_to([128, 4, n]), ALU.mult, [t])
                yield
                yield
                toks = []
                for hh in range(2):
                    b = (bA, bB)[hh]
                    after = take(b) + [t, d_id]
                    for h in range(2 * hh, 2 * hh + 2):
                        for j in range(nb):
                            c = (h % 2) * 2 + j
                            m = tr(ps[b][:, 128 * c:128 * c + 128], S[:, h, 128 * j:128 * j + 128], after, h % 2 == 1 and j == nb - 1)
                            after = []
                    v = ps[b][:, :].rearrange("p (h j n) -> p h j n", h=2, j=2)[:, :, 0:nb, :]
                    o = PT[:, 4 * hh:4 * hh + 4, :].rearrange("p (h j) n -> p h j n", h=2)[:, :, 0:nb, :]
                    e = cpa(o, v, [m] + PT_free + as_free)
                    put(b, e)
                    toks.append(e)
                S_free = [m]
                yield
                after = toks + vts + take(bA)
                for h in range(4):
                    p = slice(64 * (h % 2), 64 * (h % 2) + 64)
                    for j in range(nb):
                        m = mm(ps[bA][p, 128 * (h // 2):128 * (h // 2) + 128], vtm[:, k0 // 128 + j, 64 * (h // 2):64 * (h // 2) + 64],
                               PT[:, 2 * h + j, :], j == 0, j == nb - 1, after, h == 3 and j == nb - 1)
                        after = []
                PT_free = [m]
                t = cpa(attT[:, :, 128 * i:128 * i + 128], ps[bA][:, 0:256].rearrange("p (a n) -> p a n", a=2), [m] + tk["g0 read"])
                put(bA, t)
                yield
            tk["att"] = [t]
            tk["as"] = [t, m]

        def h64(t):
            return t.rearrange("p (h d) -> p h d", d=64)

        def bc64(t):
            return t.unsqueeze(2).broadcast_to([128, 8, 64])

        R = Region(AS, TOP)
        xs = R([128, 512])
        xc = R([128, 512])
        xd = R([128, 512])
        Dm = R([128, 8, 128])
        SM = R([128, 2, 128])
        Bt = R([128, 256])
        state = R([128, 512])
        yall = R([128, 4, 512])

        def state_space(bA, bB):
            start = tk["as"]
            free = {n: start for n in ("xs", "xc", "xd", "Dm", "SM", "Bt")}
            t_state = None
            y_toks = []
            while ("x", 3) not in tk:
                yield
            for i in range(4):
                ts_ = slice(128 * i, 128 * i + 128)
                after = take(bA) + [d_id]
                for j in range(4):
                    m = tr(ps[bA][:, 128 * j:128 * j + 128], xT[j][:, ts_], after + [tk["x", j]], j == 3)
                    after = []
                t_xs = cpa(xs[:, :], ps[bA][:, :], [m] + free["xs"])
                put(bA, t_xs)
                after = take(bB)
                for g in range(2):
                    tr(ps[bB][:, 128 * g:128 * g + 128], xT[4 + g][:, ts_], after + [tk["x", 4 + g]])
                    after = []
                for g in range(2):
                    m = mm(ps[bB][:, 256 + 128 * g:384 + 128 * g], xT[4 + g][:, ts_], xT[6 + g][:, ts_], True, True, [tk["x", 6 + g]], g == 1)
                t_Bt = cpa(Bt[:, :], ps[bB][:, 0:256], [m] + free["Bt"])
                t_SM = tt(SM[:, :, :], ps[bB][:, 256:512].rearrange("p (g n) -> p g n", g=2),
                          U[:, :].unsqueeze(1).broadcast_to([128, 2, 128]), ALU.mult, [m, t_Bt, d_U] + free["SM"])
                put(bB, t_Bt, t_SM)
                t_xc = tt(h64(xc[:, :]), h64(xs[:, :]), bc64(v3(e0)[:, i, 0:8]), ALU.mult, [t_xs, tk["dt"]] + free["xc"], q=GE)
                t_xd = tt(h64(xd[:, :]), h64(xc[:, :]), bc64(v3(dl)[:, i, 0:8]), ALU.mult, [t_xc, tk["dl"]] + free["xd"], q=GE)
                yield
                td = []
                for q in range(2):
                    b = (bA, bB)[q]
                    after = take(b) + [tk["da"]]
                    for h in range(4 * q, 4 * q + 4):
                        m = mm(ps[b][:, 128 * (h % 4):128 * (h % 4) + 128], v3(da)[:, i, h:h + 1].broadcast_to([128, 128]), U[:, :],
                               True, True, after, h % 4 == 3)
                        after = []
                    for h in range(4 * q, 4 * q + 4):
                        t = ts(Dm[:, h, :], ps[b][:, 128 * (h % 4):128 * (h % 4) + 128], v3(csum)[:, i, h:h + 1], 0.0,
                               ALU.subtract, ALU.min, [m, tk["cs"]] + free["Dm"])
                    put(b, t)
                    e = act(Dm[:, 4 * q:4 * q + 4, :], Dm[:, 4 * q:4 * q + 4, :], ACT.Exp, [t])
                    td.append(tt(Dm[:, 4 * q:4 * q + 4, :], Dm[:, 4 * q:4 * q + 4, :],
                                 SM[:, q, :].unsqueeze(1).broadcast_to([128, 4, 128]), ALU.mult, [e, t_SM], q=GE))
                    yield
                free["SM"] = td
                y = yall[:, i, :]
                if i > 0:
                    after = take(bB) + [t_state]
                    for g in range(2):
                        m2 = mm(ps[bB][:, 256 * g:256 * g + 256], xT[6 + g][:, ts_], state[:, 256 * g:256 * g + 256], True, True, after, g == 1)
                        after = []
                    t_off = tt(h64(y), h64(ps[bB][:, :]), bc64(v3(eg)[:, i, 0:8]), ALU.mult, [m2, tk["eg"]] + start)
                    put(bB, t_off)
                    yield
                if i < 3:
                    after = take(bB) + [t_Bt, t_xd]
                    for g in range(2):
                        m3 = mm(ps[bB][:, 256 * g:256 * g + 256], Bt[:, 128 * g:128 * g + 128], xd[:, 256 * g:256 * g + 256], True, True, after, g == 1)
                        after = []
                    free["Bt"] = [m3]
                    free["xd"] = [m3]
                    if i == 0:
                        t_state = cpv(state[:, :], ps[bB][:, :], [m3] + start)
                    else:
                        u = tt(h64(state[:, :]), h64(state[:, :]), bc64(v3(dtot[:, :])[:, i, 0:8]), ALU.mult, [tk["dtot"], t_state, m2], q=GE)
                        t_state = tt(state[:, :], state[:, :], ps[bB][:, :], ALU.add, [u, m3])
                    put(bB, t_state)
                yield
                after = take(bA) + td + [t_xc]
                for h in range(8):
                    m = mm(ps[bA][:, 64 * h:64 * h + 64], Dm[:, h, :], xc[:, 64 * h:64 * h + 64], True, True, after, h == 7)
                    after = []
                free["Dm"] = [m]
                free["xc"] = [m, t_xd]
                if i > 0:
                    t = tt(y, y, ps[bA][:, :], ALU.add, [t_off, m])
                else:
                    t = cpv(y, ps[bA][:, :], [m] + start)
                put(bA, t)
                u = tt(h64(xs[:, :]), h64(xs[:, :]), bc64(brow[:, 28:36]), ALU.mult, [t_xc, t_xs, d_brow], q=GE)
                t = tt(y, y, xs[:, :], ALU.add, [t, u], q=GE)
                free["xs"] = [t]
                y_toks.append(t)
                yield
            tk["y"] = y_toks

        def hd(t):
            return t.rearrange("p i (h d) -> p i h d", h=2)

        def bcg(t):
            return t.unsqueeze(3).broadcast_to([128, 4, 2, 64])

        def q4v(t):
            return t.rearrange("p (n c) -> p n c", n=4)

        def delta(p, og, start, b0, b1, b2, b3):
            R = Region(GD, GD + 30720)
            rhs = R([128, 4, 2, 128])
            kd = R([128, 4, 128])
            qeT = R([128, 4, 128])
            QK = R([128, 8, 128])
            two = R.at
            qkv = R([128, 4, 3, 128])
            kb = R([128, 4, 128])
            qe = R([128, 4, 128])
            three = R.at
            knT = R([128, 4, 128])
            kbT = R([128, 4, 128])
            qnT = R([128, 4, 128])
            R = Region(two, three)
            AT = R([128, 8, 128])
            XT = R([128, 8, 128])
            Dg = at(two + 4096, [128, 8, 128])
            Sg = R([128, 64])
            vn = [R([128, 2, 64]) for _ in range(2)]
            uu2 = at(two, [128, 2, 4, 64])
            wT = at(two + 2048, [128, 4, 128])
            R = Region(three, GD + 30720)
            X = R([128, 8, 128])
            P1 = R([128, 8, 128])
            while ("g", 3 * p + 2) not in tk or "cs" not in tk:
                yield
            tq = []
            for i in range(4):
                b = (b0, b1)[i % 2]
                after = take(b) + [d_id]
                for j in range(3):
                    m = tr(ps[b][:, 128 * j:128 * j + 128], gT[3 * p + j][:, 128 * i:128 * i + 128], after + [tk["g", 3 * p + j]], j == 2)
                    after = []
                t = cpa(qkv[:, i, :, :], ps[b][:, 0:384].rearrange("p (a n) -> p a n", a=3), [m] + start)
                put(b, t)
                tq.append(t)
                if i % 2 == 1:
                    yield
            if p == 0:
                tk["g0 read"] = [m]
            s_og = start + tk["g0 read"]
            for j in range(2):
                t = tt(og[:, :, :], qkv[:, :, j, :], qkv[:, :, j, :], ALU.mult, tq + s_og + ([t] if j else []))
                t = red(rsn[:, :, j, :], hd(og[:, :, :]), ALU.add, [t] + start)
            t = act(rsn[:, :, :, :], rsn[:, :, :, :], ACT.Sqrt, [t, d_cols], bias=col("eps6"))
            t_rs = rec(rsn[:, :, :, :], rsn[:, :, :, :], [t])
            t = ts(rsn[:, :, 0, :], rsn[:, :, 0, :], 0.125, None, ALU.mult, after=[t_rs])
            qv, kv, vv = (hd(qkv[:, :, j, :]) for j in range(3))
            hs = slice(8 + 2 * p, 10 + 2 * p)
            egp, dlp, bep = v3(eg)[:, :, hs], v3(dl)[:, :, hs], beta[:, :, 2 * p:2 * p + 2]
            t_kn = tt(kv, kv, bcg(rsn[:, :, 1, :]), ALU.mult, [t_rs])
            t_kb = tt(hd(kb[:, :, :]), kv, bcg(bep), ALU.mult, [t_kn, tk["beta"]] + start)
            t_qn = tt(qv, qv, bcg(rsn[:, :, 0, :]), ALU.mult, [t])
            t_qe = tt(hd(qe[:, :, :]), qv, bcg(egp), ALU.mult, [t_qn, tk["eg"]] + start)
            t_vb = tt(rhs[:, :, :, 0:64], vv, bcg(bep), ALU.mult, tq + [tk["beta"]] + start, q=GE)
            t_kbe = tt(rhs[:, :, :, 64:128], hd(kb[:, :, :]), bcg(egp), ALU.mult, [t_kb, tk["eg"]] + start, q=GE)
            t_kd = tt(hd(kd[:, :, :]), kv, bcg(dlp), ALU.mult, [t_kn, tk["dl"]] + start, q=GE)
            yield
            yield
            ttr = []
            for n, (src, dst, w) in enumerate([(qkv[:, :, 1, :], knT, t_kn), (kb[:, :, :], kbT, t_kb),
                                               (qkv[:, :, 0, :], qnT, t_qn), (qe[:, :, :], qeT, t_qe)]):
                b = (b0, b1)[n % 2]
                after = take(b) + [w]
                for i in range(4):
                    m = tr(ps[b][:, 128 * i:128 * i + 128], src[:, i, :], after, i == 3)
                    after = []
                t = cpa(dst[:, :, :], ps[b][:, :].rearrange("p (i n) -> p i n", i=4), [m] + start)
                put(b, t)
                ttr.append(t)
                if n % 2 == 1:
                    yield
            two_free = [m, t_vb, t_kbe, t_kd]
            td = []
            for q in range(2):
                b = (b2, b3)[q]
                h = 8 + 2 * p + q
                after = take(b) + [tk["da"]]
                for i in range(4):
                    m = mm(ps[b][:, 128 * i:128 * i + 128], v3(da)[:, i, h:h + 1].broadcast_to([128, 128]), U[:, :], True, True, after, i == 3)
                    after = []
                for i in range(4):
                    t = ts(Dg[:, 4 * q + i, :], ps[b][:, 128 * i:128 * i + 128], v3(csum)[:, i, h:h + 1], 0.0,
                           ALU.subtract, ALU.min, [m, tk["cs"]] + two_free)
                put(b, t)
                e = act(Dg[:, 4 * q:4 * q + 4, :], Dg[:, 4 * q:4 * q + 4, :], ACT.Exp, [t])
                td.append(tt(Dg[:, 4 * q:4 * q + 4, :], Dg[:, 4 * q:4 * q + 4, :],
                             U[:, :].unsqueeze(1).broadcast_to([128, 4, 128]), ALU.mult, [e, d_U], q=GE))
                yield
            ta, tqk = [], []
            for src, dst, lst, bb in ((kbT, AT, ta, (b0, b1)), (qnT, QK, tqk, (b2, b3))):
                for q in range(2):
                    b = bb[q]
                    s = slice(64 * q, 64 * q + 64)
                    after = take(b) + ttr
                    for i in range(4):
                        m = mm(ps[b][:, 128 * i:128 * i + 128], knT[s, i, :], src[s, i, :], True, True, after, i == 3)
                        after = []
                    t = tt(dst[:, 4 * q:4 * q + 4, :], q4v(ps[b][:, :]), Dg[:, 4 * q:4 * q + 4, :], ALU.mult, [m, td[q]] + two_free + start)
                    put(b, t)
                    lst.append(t)
                yield
            three_free = [m] + ta + tqk
            bc4 = [128, 4, 128]
            I4 = ident[:, :].unsqueeze(1).broadcast_to(bc4)
            t_x, t_xt = [None, None], [None, None]
            for q in range(2):
                sl = slice(4 * q, 4 * q + 4)
                t = tt(XT[:, sl, :], AT[:, sl, :], lev[:, 0, :].unsqueeze(1).broadcast_to(bc4), ALU.mult, [ta[q], d_lev] + tqk, q=GE)
                b = (b0, b1)[q]
                after = take(b) + [t]
                for n in range(4 * q, 4 * q + 4):
                    m = tr(ps[b][:, 128 * (n % 4):128 * (n % 4) + 128], XT[:, n, :], after, n % 4 == 3)
                    after = []
                t_x[q] = tt(X[:, sl, :], I4, q4v(ps[b][:, :]), ALU.subtract, [m, d_id] + three_free)
                put(b, t_x[q])
                t_xt[q] = tt(XT[:, sl, :], I4, XT[:, sl, :], ALU.subtract, [t, m, d_id], q=GE)
                yield
            p1_free = [three_free, three_free]
            for lv in range(1, 7):
                tp = [None, None]
                for q in range(2):
                    sl = slice(4 * q, 4 * q + 4)
                    b = (b0, b1)[q]
                    after = take(b) + [ta[q], t_x[q]]
                    for n in range(4 * q, 4 * q + 4):
                        m = mm(ps[b][:, 128 * (n % 4):128 * (n % 4) + 128], AT[:, n, :], X[:, n, :], True, True, after, n % 4 == 3)
                        after = []
                    tp[q] = tt(P1[:, sl, :], q4v(ps[b][:, :]), lev[:, lv, :].unsqueeze(1).broadcast_to(bc4), ALU.mult, [m, d_lev] + p1_free[q])
                    put(b, tp[q])
                    yield
                for q in range(2):
                    sl = slice(4 * q, 4 * q + 4)
                    b, bt = (b2, b3)[q], (b0, b1)[q]
                    after = take(bt) + [tp[q], t_xt[q]]
                    for n in range(4 * q, 4 * q + 4):
                        m = mm(ps[bt][:, 128 * (n % 4):128 * (n % 4) + 128], P1[:, n, :], XT[:, n, :], True, True, after, n % 4 == 3)
                        after = []
                    if lv < 6:
                        after = take(b)
                        for n in range(4 * q, 4 * q + 4):
                            mq = mm(ps[b][:, 128 * (n % 4):128 * (n % 4) + 128], XT[:, n, :], P1[:, n, :], True, True, after, n % 4 == 3)
                            after = []
                        t_x[q] = tt(X[:, sl, :], X[:, sl, :], q4v(ps[b][:, :]), ALU.subtract, [mq, t_x[q]])
                        put(b, t_x[q])
                        m2 = mq
                    else:
                        m2 = m
                    t_xt[q] = tt(XT[:, sl, :], XT[:, sl, :], q4v(ps[bt][:, :]), ALU.subtract, [m, m2, t_xt[q]])
                    put(bt, t_xt[q])
                    p1_free[q] = [m2]
                    yield
            after = take(b2, b3) + t_xt + [t_vb, t_kbe]
            for n in range(8):
                i, h = n % 4, n // 4
                m1 = mm(ps[b2][:, 64 * n:64 * n + 64], XT[:, n, :], rhs[:, i, h, 0:64], True, True, after, n == 7)
                after = []
                m2 = mm(ps[b3][64 * h:64 * h + 64, 128 * i:128 * i + 128], rhs[:, i, h, 64:128], XT[:, n, :], True, True, [], n == 7)
            t_u = cpv(uu2[:, :, :, :], ps[b2][:, :].rearrange("p (h i d) -> p h i d", i=4, h=2), [m1] + p1_free[0] + p1_free[1])
            t_w = cpa(wT[:, :, :], ps[b3][:, :].rearrange("p (i n) -> p i n", i=4), [m2] + p1_free[0] + p1_free[1])
            put(b2, t_u)
            put(b3, t_w)
            yield
            t_S = None
            vn_free = [two_free, two_free]
            t_o = []
            for i in range(4):
                s = i % 2
                t_v = []
                if i > 0:
                    after = take(b0, b1) + [t_w, t_S]
                    for h in range(2):
                        r = slice(64 * h, 64 * h + 64)
                        b = (b0, b1)[h]
                        m = mm(ps[b][:, 0:64], wT[r, i, :], Sg[r, :], True, True, after, True)
                        after = []
                        t = tt(vn[s][:, h, :], uu2[:, h, i, :], ps[b][:, 0:64], ALU.subtract, [m, t_u] + vn_free[s])
                        put(b, t)
                        t_v.append(t)
                else:
                    t_v.append(cpv(vn[s][:, :, :], uu2[:, :, i, :], [t_u] + vn_free[s]))
                yield
                if i < 3:
                    after = take(b0) + [t_kd] + t_v
                    for h in range(2):
                        m = mm(ps[b0][64 * h:64 * h + 64, 0:64], kd[:, i, 64 * h:64 * h + 64], vn[s][:, h, :], True, True, after, h == 1)
                        after = []
                after = take(b2, b3) + tqk + t_v
                for h in range(2):
                    r = slice(64 * h, 64 * h + 64)
                    b = (b2, b3)[h]
                    if i > 0:
                        mm(ps[b][:, 0:64], qeT[r, i, :], Sg[r, :], True, False, after)
                        after = []
                    mo = mm(ps[b][:, 0:64], QK[:, 4 * h + i, :], vn[s][:, h, :], i == 0, True, after, True)
                    after = []
                    t = cpa(og[:, i, 64 * h:64 * h + 64], ps[b][:, 0:64], [mo, t_kn, t_qn])
                    put(b, t)
                    t_o.append(t)
                if i < 3:
                    if i == 0:
                        t_S = cpv(Sg[:, :], ps[b0][:, 0:64], [m] + two_free)
                    else:
                        t_S = stt(Sg[:, :], Sg[:, :], decS[:, p, i:i + 1], ps[b0][:, 0:64], ALU.mult, ALU.add, [m, mo, t_S, tk["decS"]])
                    put(b0, t_S)
                    vn_free[s] = [m, mo]
                yield
            sq_ = qeT[:, :, :]
            t = tt(sq_, og[:, :, :], og[:, :, :], ALU.mult, t_o + [mo, t_S], q=GE)
            t = red(rsn[:, :, 0, :], hd(sq_), ALU.add, [t])
            t = act(rsn[:, :, 0, :], rsn[:, :, 0, :], ACT.Sqrt, [t], bias=col("eps6"), scale=1.0 / 64)
            t = rec(rsn[:, :, 0, :], rsn[:, :, 0, :], [t])
            t = tt(hd(og[:, :, :]), hd(og[:, :, :]), bcg(rsn[:, :, 0, :]), ALU.mult, [t])
            t = tt(og[:, :, :], og[:, :, :], gz[:, :, 128 * p:128 * p + 128], ALU.mult, [t] + [tk["gz", i] for i in range(4)], q=GE)
            tk["og", p] = [t]
            tk["gd", p] = [t, mo]
            yield

        def delta_chain():
            yield from delta(0, og0, xn_done, 2, 3, 4, 5)
            yield from delta(1, og1, tk["gd", 0], 2, 3, 4, 5)

        def short_chain():
            yield from steps()
            while "k" not in tk or "g0 read" not in tk:
                yield
            yield from attention(6, 7)
            yield from state_space(6, 7)

        tiles = [("g", 0), ("g", 1), ("g", 2), "qA", "qB", "k", ("g", 3), ("g", 4), ("g", 5)]
        tiles += [("x", j) for j in (4, 5, 6, 7, 0, 1, 2, 3)]

        def in_use(first):
            def use(t, b, m):
                n = tiles[first + t]
                if n == "qA" or n == "qB":
                    q = qT[0 if n == "qA" else 1]
                    a = act(q[:, :], ps[b][:, :], ACT.Copy, [m] + as_free, scale=0.125)
                    put(b, a)
                elif n == "k":
                    a = cpa(kT[:, :], ps[b][:, :], [m] + as_free)
                    put(b, a)
                elif n[0] == "x":
                    a = conv4(b, m, xT[n[1]], COLS["ssd_cw"] + 4 * n[1], col("ssd_cb", n[1]))
                else:
                    kind, pair = n[1] % 3, n[1] // 3
                    a = conv4(b, m, gT[n[1]], COLS["gdn_cw"] + 4 * (2 * kind + pair), None)
                tk[n] = a
            return use

        bg.add(short_chain(), RATE1)
        bg.add(delta_chain())
        for j in range(0, 17, 2):
            feat_chunk(hT, [0, 1], in_use(j))

        def z_use(half):
            def use(i, b, m):
                a = act(zs[:, i, 256 * half:256 * half + 256], ps[b][:, 0:256], ACT.Silu, [m])
                put(b, a)
                tk["z", i, half] = a
            return use

        for half in range(2):
            e = tok_group(hH, hL, 8, hT, [0, 1, 0, 1], z_use(half))
        ht_free = [e]
        bg.finish()

        mixed = [[] for _ in range(8)]
        R = Region(GD, GD + 30720)
        nwr = R([128, 512])
        sq = R([128, 512])
        gend = tk["gd", 1]
        d_nwr = dma(nwr[:, :], ins["ssd_nw"].partition_broadcast(128).rearrange("p a n -> p (a n)"), gend)
        u = None
        y_toks = []
        for i in range(4):
            y = yall[:, i, :]
            t = tt(y, y, zs[:, i, :], ALU.mult, [tk["y"][i], tk["z", i, 0], tk["z", i, 1]])
            y_toks.append(t)
            for g in range(2):
                u = act(sq[:, 0:256], y[:, 256 * g:256 * g + 256], ACT.Square, [t, u] + gend, accum=gs[:, 2 * i + g:2 * i + g + 1])
        a = act(gs[:, :], gs[:, :], ACT.Sqrt, [u, d_cols], bias=col("eps6"), scale=1.0 / 256)
        a = rec(gs[:, :], gs[:, :], [a])
        r = split_ht(slice(0, 2), attT[:, :, :], tk["att"], ht_free)
        mixed[0], mixed[1] = r, r
        for p in range(2):
            b = 2 + p
            after = take(b) + tk["og", p]
            for i in range(4):
                m = tr(ps[b][:, 128 * i:128 * i + 128], (og0, og1)[p][:, i, :], after, i == 3)
                after = []
            r = split_ht(6 + p, ps[b][:, :], [m], ht_free, gain=col("gdn_nw"))
            put(b, *r)
            mixed[6 + p] = r
        for i in range(4):
            y = yall[:, i, :]
            for g in range(2):
                t = stt(y[:, 256 * g:256 * g + 256], y[:, 256 * g:256 * g + 256], gs[:, 2 * i + g:2 * i + g + 1],
                        nwr[:, 256 * g:256 * g + 256], ALU.mult, ALU.mult, [a, y_toks[i], d_nwr])
            b = 4 + i
            after = take(b) + [t]
            for j in range(4):
                m = tr(ps[b][:, 128 * j:128 * j + 128], y[:, 128 * j:128 * j + 128], after, j == 3)
                after = []
            r = split_ht(slice(2, 6), ps[b][:, :].rearrange("p (k n) -> p k n", k=4), [m], ht_free, slice(128 * i, 128 * i + 128))
            put(b, *r)
            for k in range(2, 6):
                mixed[k] = mixed[k] + r
        gdn_end = [t for q in mixed for t in q] + [m] + tk["og", 0] + tk["og", 1] + [f for q in y_free for f in q]

        def rms_residual(kt, lH, lL, ready, row_j, tmp, tmp_free):
            d_r = row(0, row_j, tmp_free)
            got = {}

            def use_h(h):
                def use(i, b, m):
                    got[i, h] = (b, act(tmp[i % 2][:, 512 * h:512 * h + 512], ps[b][:, :], ACT.Square, [m] + got.get(("t", i % 2, h), tmp_free),
                                        accum=st[:, 16 + 2 * i + h:17 + 2 * i + h]))
                    got["t", i % 2, h] = [got[i, h][1]]
                return use

            tok_group(lH, lL, kt, ready, [0, 1, 2, 3], use_h(0))
            last = tok_group(lH, lL, kt, ready, [4, 5, 6, 7], use_h(1))
            xt = []
            a = red(st[:, 0:4], st[:, 16:24].rearrange("p (i h) -> p i h", h=2), ALU.add, [got[i, h][1] for i in range(4) for h in range(2)])
            a = act(st[:, 4:8], st[:, 0:4], ACT.Sqrt, [a], bias=col("eps6"), scale=1.0 / 1024)
            a = rec(st[:, 8:12], st[:, 4:8], [a])
            w = [[], []]
            for i in range(4):
                o = tmp[i % 2]
                r = []
                for h in range(2):
                    b = got[i, h][0]
                    t = stt(o[:, 512 * h:512 * h + 512], ps[b][:, :], st[:, 8 + i:9 + i], rows[0][:, 512 * h:512 * h + 512],
                            ALU.mult, ALU.mult, [a, d_r] + w[i % 2])
                    put(b, t)
                    r.append(t)
                t = tt(x[:, i, :], x[:, i, :], o[:, :], ALU.add, r, q=GE)
                w[i % 2] = [t]
                xt.append([t])
            return xt, last

        R = Region(BIG, TOP)
        xn = R([128, 4, 1024])
        tmp = [R([128, 1024]) for _ in range(2)]
        xt, last = rms_residual(8, hH, hL, mixed, 0, tmp, gdn_end)
        hT = rms_to_ht(xt, "pre_ffn", xn, [last], gdn_end)
        ht_end = ("s_pe", PE.n)
        hT = hT

        R = Region(BIG, TOP)
        aH = R([128, 22, 512], F32R)
        aL = R([128, 22, 512], F32R)
        TMP = R.at
        ft = [R([128, 512]) for _ in range(6)]
        f_free = [[ht_end] for _ in range(6)]
        a_free = [ht_end]
        atoks = []

        def ffn_pair(t, b, m, m_tile, hold={}):
            if t == 0:
                s = m_tile % 2
                a = act(ft[s][:, :], ps[b][:, :], ACT.Silu, [m] + f_free[s])
                put(b, a)
                hold["g"] = a
            else:
                s = m_tile % 2
                a = tt(ft[2 + s][:, :], ft[s][:, :], ps[b][:, :], ALU.mult, [m, hold["g"]] + f_free[2 + s])
                put(b, a)
                f_free[s] = [a]
                h = act(aH[:, m_tile, :], ft[2 + s][:, :], ACT.Copy, [a] + a_free)
                l = tt(aL[:, m_tile, :], ft[2 + s][:, :], aH[:, m_tile, :].bitcast(F32), ALU.subtract, [a, h] + a_free, q=GE)
                f_free[2 + s] = [h, l]
                atoks.append([h, l])

        for m_tile in range(22):
            feat_chunk(hT, [2 * (m_tile % 2), 2 * (m_tile % 2) + 1], lambda t, b, m, mt=m_tile: ffn_pair(t, b, m, mt))
        ft_end = [t for f in f_free for t in f]
        tmp = [at(TMP + 4096 * j, [128, 1024]) for j in range(2)]
        xt, last = rms_residual(22, aH, aL, atoks, 1, tmp, ft_end)
        x_end = [t for u in xt for t in u]

        hT = []

        def plain_ht(toks, free):
            r = []

            def use(k, b, m):
                q = split_ht(k, ps[b][:, :], [m], free)
                put(b, *q)
                r.append(q)

            transposed(x, toks, use, free)
            return r

        hT = plain_ht(xt, [last])
        prev = [last] + x_end
        R = Region(BIG, TOP)
        ckvT = R([128, 512])
        ckv = R([128, 4, 128])
        widx = R([128, 4, 8])
        fin = R([128, 4, 8])
        Q0 = R.at
        qiT = [R([128, 512]) for _ in range(4)]
        kiT = R([128, 512])
        qaT = [R([128, 512]) for _ in range(4)]
        QB = R([66, 8, 512])
        KB = R([66, 8, 512])
        vb = R([128, 4, 512])
        near = R([128, 8, 256])
        CM = R([128, 512])
        selm = R([128, 1152])
        wuk = R([128, 4, 128])
        wuv = R([128, 8, 64])
        anti = R([128, 128])
        oh31 = R([32, 4])
        rb2 = R([32, 8])
        C0 = R.at
        cf = R([8, 2, 512])
        obT = R([128, 4, 512])
        sco = R([128, 512])
        Pt = [R([128, 512]) for _ in range(2)]
        m8 = R([128, 8])
        sx2 = R([128, 6, 4])
        d_CM = dma(CM[:, :], ins["causal"], prev)
        d_wuk = dma(wuk[:, :, :], ins["wuk"].rearrange("p (a r) -> p a r", a=4), prev)
        d_wuv = dma(wuv[:, :, :], ins["wuv"].rearrange("p (a r) -> p a r", a=8), prev)
        d_anti = dma(anti[:, :], ins["anti"], prev)
        d_oh = dma(oh31[:, 0:1], ins["oh31"], prev)
        d_rb = dma(rb2[:, :], ins["rel_bias_2"], prev)
        toep = bass.AP(u_dram.tensor, 0, [[1, 128], [384, 8], [1, 256]])
        d_near = dma(near[:, :, :], toep, prev + [d_u])

        def small2(i, b, m):
            a1 = cpa(ckv[:, i, :], ps[b][:, 0:128], [m] + prev)
            a2 = act(widx[:, i, :], ps[b][:, 128:136], ACT.Copy, [m] + prev, scale=8.0 ** -0.5)
            a3 = cpa(fin[:, i, :], ps[b][:, 136:144], [m] + prev)
            put(b, a1, a2, a3)
            tk["ckv", i], tk["widx", i], tk["fin", i] = a1, a2, a3

        tok_group(hH, hL, 8, hT, [0, 1, 0, 1], small2)

        def gates():
            after = take(7) + [d_id]
            for i in range(4):
                m = tr(ps[7][0:8, 128 * i:128 * i + 128], fin[:, i, :], after + [tk["fin", i]], i == 3)
                after = []
            f0, f1 = cf[:, 0, :], cf[:, 1, :]
            w0, w1, w2 = (rows[j // 2][0:8, 512 * (j % 2):512 * (j % 2) + 512] for j in range(3))
            t = ts(f0, ps[7][0:8, :], cols[0:8, COLS["b_f"]:COLS["b_f"] + 1], -1.0, ALU.add, ALU.mult, [m, d_cols] + prev)
            put(7, t)
            a = stt(w0, f0, -1.0, f0, ALU.mult, ALU.max, [t] + prev)
            a = act(w0, w0, ACT.Exp, [a], scale=-1.0)
            b = ts(w1, w0, 1.0, None, ALU.add, after=[a])
            c = act(w2, w1, ACT.Ln, [b])
            yield
            b = ts(w1, w1, -1.0, 1e-30, ALU.add, ALU.max, [b, c])
            d = rec(f1, w1, [b])
            d = tt(f1, f1, w2, ALU.mult, [d, c])
            d = tt(f1, f1, w0, ALU.mult, [d])
            b = ts(w1, w1, 1e-30, None, ALU.is_equal, after=[d])
            b = tt(w1, w1, w0, ALU.mult, [b])
            d = tt(f1, f1, w1, ALU.add, [d, b])
            d = stt(f1, f0, 0.0, f1, ALU.max, ALU.add, [d])
            yield
            b = mset(w1, 1.0, [b])
            d = VE.add(lambda e: e.tensor_tensor_scan(f0, w1, f1, 0.0, ALU.mult, ALU.add), [d, b])
            d2 = ts(f1, f0, -1.0, None, ALU.mult, after=[d])
            tk["gates"] = [d2, c]
            a = mset(QB[64:66, :, :], 1.0, prev, q=GE)
            b = mset(KB[64:66, :, :], 1.0, prev, q=GE)
            tk["dq"] = dma(QB[65:66, :, :], f1, [a, d2])
            tk["dk"] = dma(KB[64:65, :, :], f0, [b, d])
            yield

        sel_at = [0, 0, 256, 640]
        t_sel = [d_CM, None, None, None]

        def index():
            while ("ki" not in tk) or ("dk" not in tk):
                yield
            rel = [at(C0 + 2048 * j, [128, 512]) for j in range(2)]
            rel_free = [[tk["dq"], tk["dk"]], [tk["dq"], tk["dk"]]]
            done = []
            n_r = 0
            for i in range(1, 4):
                n = 128 * (i + 1)
                acc = None
                for h in range(8):
                    r = n_r % 2
                    s = slice(64 * (h % 2), 64 * (h % 2) + 64)
                    m = mm(ps[7][:, 0:n], qiT[h // 2][s, 128 * i:128 * i + 128], kiT[s, 0:n], True, True,
                           take(7) + [tk["qi", h // 2], tk["ki"]], True)
                    a = act(rel[r][:, 0:n], ps[7][:, 0:n], ACT.Relu, [m] + rel_free[r])
                    put(7, a)
                    prior = CM[:, 512 - n:512] if h == 0 else sco[:, 0:n]
                    acc = stt(sco[:, 0:n], rel[r][:, 0:n], widx[:, i, h:h + 1], prior, ALU.mult, ALU.add,
                              [a, tk["widx", i], d_CM] + (prev + done if h == 0 else [acc]))
                    rel_free[r] = [acc]
                    n_r += 1
                    yield
                t = acc
                for q in range(16):
                    t = VE.add(lambda e, n=n: e.max(m8[:, :], sco[:, 0:n]), [t])
                    t = VE.add(lambda e, n=n: e.match_replace(sco[:, 0:n], m8[:, :], sco[:, 0:n], TAKEN), [t])
                    yield
                t = ts(selm[:, sel_at[i]:sel_at[i] + n], sco[:, 0:n], TAKEN / 2, NEG, ALU.is_gt, ALU.mult, [t] + prev)
                done = [t]
                t_sel[i] = t
            tk["index"] = [t]
            yield

        Pt_free = [list(prev), list(prev)]

        def units(todo, slots, slot_free, look, scores, product, out, there=lambda h: True):
            NS = len(slots)
            soft, turned = {}, {}

            def first(n):
                h, i = todo[n]
                w = 128 * (i + 1)
                s, b = n % NS, 2 + n % 2
                m, mask, need = scores(h, i, b)
                mx, sm_, rd = (sx2[:, s, j:j + 1] for j in range(3))
                t = VE.add(lambda e, o=slots[s][:, 0:w], a=ps[b][:, 0:w], k=mask, c=mx:
                           e.tensor_tensor_reduce(o, a, k, 1.0, 2 * NEG, ALU.add, ALU.max, c), [m] + need + slot_free[s])
                put(b, t)
                t = ts(mx, mx, -1.0, None, ALU.mult, after=[t])
                t = act(slots[s][:, 0:w], slots[s][:, 0:w], ACT.Exp, [t], bias=mx, accum=sm_)
                t = rec(rd, sm_, [t])
                soft[n] = ts(slots[s][:, 0:w], slots[s][:, 0:w], rd, None, ALU.mult, after=[t])

            def second(n):
                h, i = todo[n]
                w = 128 * (i + 1)
                s, p, b = n % NS, n % 2, 4 + n % 2
                after = take(b) + [soft[n]]
                for j in range(i + 1):
                    m = tr(ps[b][:, 128 * j:128 * j + 128], slots[s][:, 128 * j:128 * j + 128], after, j == i)
                    after = []
                slot_free[s] = [m]
                turned[n] = cpa(Pt[p][:, 0:w], ps[b][:, 0:w], [m] + Pt_free[p])
                put(b, turned[n])

            def third(n):
                h, i = todo[n]
                p = n % 2
                after = [turned[n]]
                for j in range(i + 1):
                    o, l, more = product(h, i, j)
                    m = mm(o, l, Pt[p][:, 128 * j:128 * j + 128], j == 0, j == i, after + more, j == i)
                    after = []
                Pt_free[p] = [m]
                if i == 3:
                    out(h, m)

            N = len(todo)
            for n in range(-look, N):
                if n + look < N:
                    while not there(todo[n + look][0]):
                        yield
                    first(n + look)
                    yield
                if 0 <= n + 1 < N:
                    second(n + 1)
                    yield
                if n >= 0:
                    third(n)
                    yield

        def scores_b(h, i, b):
            w = 128 * (i + 1)
            m = mm(ps[b][:, 0:w], QB[:, h, 128 * i:128 * i + 128], KB[:, h, 0:w], True, True,
                   take(b) + [tk["QB", h], tk["KB", h], tk["dq"], tk["dk"]], True)
            return m, CM[:, 512 - w:512], [d_CM]

        def product_b(h, i, j):
            r = slice(64 * (h % 2), 64 * (h % 2) + 64)
            return (ps[6][r, 128 * i:128 * i + 128], vb[:, j, 64 * h:64 * h + 64],
                    [tk["vb", j, h // 4]] + (take(6) if i == 0 and j == 0 and h % 2 == 0 else []))

        def out_b(h, m):
            if h % 2 == 1:
                tk["ob", h // 2] = cpa(obT[:, h // 2, :], ps[6][:, :], [m] + prev)
                put(6, tk["ob", h // 2])

        rows4 = [rows[j // 2][:, 512 * (j % 2):512 * (j % 2) + 512] for j in range(4)]
        rows_free = [None] * 4

        def forget_attention():
            while "dk" not in tk:
                yield
            for j in range(4):
                rows_free[j] = prev + tk["gates"]
            todo = [(h, i) for h in range(8) for i in range(4)]
            for _ in units(todo, rows4, rows_free, 3, scores_b, product_b, out_b,
                           lambda h: ("QB", h) in tk and ("KB", h) in tk and "dk" in tk):
                yield

        def evac2(name, dst, scale=None):
            def use(b, m):
                tk[name] = act(dst[:, :], ps[b][:, :], ACT.Copy, [m] + prev, scale=scale)
                put(b, tk[name])
            return use

        def evac_heads(name, dst, j, scale=None):
            def use(b, m):
                for h in range(2):
                    o, i = dst[0:64, 2 * j + h, :], ps[b][64 * h:64 * h + 64, :]
                    if h == 0:
                        t = act(o, i, ACT.Copy, [m] + prev, scale=scale)
                    else:
                        t = ts(o, i, 1.0 if scale is None else scale, None, ALU.mult, after=[m] + prev)
                    tk[name, 2 * j + h] = t
                    put(b, t)
            return use

        def two(a, b):
            feat_chunk(hT, [0, 1], lambda t, bk, m: (a, b)[t](bk, m))

        bg.add(gates(), RATE2)
        bg.add(index())
        for j in range(2):
            two(evac2(("qi", 2 * j), qiT[2 * j], 0.125), evac2(("qi", 2 * j + 1), qiT[2 * j + 1], 0.125))
        two(evac2("ckvT", ckvT), evac2("ki", kiT))
        for half in range(2):
            def vb_use(i, b, m, half=half):
                tk["vb", i, half] = cpa(vb[:, i, 256 * half:256 * half + 256], ps[b][:, 0:256], [m] + prev)
                put(b, tk["vb", i, half])

            tok_group(hH, hL, 8, hT, [0, 1, 0, 1], vb_use)
        bg.add(forget_attention())
        for j in range(4):
            two(evac_heads("QB", QB, j, 0.125), evac_heads("KB", KB, j))
        for j in range(2):
            two(evac2(("qa", 2 * j), qaT[2 * j]), evac2(("qa", 2 * j + 1), qaT[2 * j + 1]))
        ht_free = [(PE.sem, PE.n)]
        bg.finish()
        mixed = [[] for _ in range(8)]
        for j in range(4):
            mixed[4 + j] = split_ht(4 + j, obT[:, j, :], [tk["ob", j]], ht_free)

        RQ = Region(Q0, Q0 + 8192)
        ql = [RQ([128, 512]) for _ in range(2)]
        oa = [RQ([128, 512]) for _ in range(2)]
        ql_free = [list(tk["index"]) for _ in range(2)]
        oa_free = [list(tk["index"]) for _ in range(2)]
        ql_tok = {}

        def latent(h):
            r = slice(64 * (h % 2), 64 * (h % 2) + 64)
            m = mm(ps[0][:, :], wuk[r, h // 2, :], qaT[h // 2][r, :], True, True, take(0) + [d_wuk, tk["qa", h // 2]], True)
            ql_tok[h] = act(ql[h % 2][:, :], ps[0][:, :], ACT.Copy, [m] + ql_free[h % 2], scale=0.125)
            put(0, ql_tok[h])

        def scores_a(h, i, b):
            w = 128 * (i + 1)
            if i == 0 and h == 0:
                latent(0)
            if i == 3 and h < 7:
                latent(h + 1)
            mm(ps[b][:, 0:w], ql[h % 2][:, 128 * i:128 * i + 128], ckvT[:, 0:w], True, False, take(b) + [ql_tok[h], tk["ckvT"]])
            k0 = max(i - 1, 0)
            if k0 > 0:
                mm(ps[b][:, 0:128 * k0], rb2[:, h:h + 1].broadcast_to([32, 128]), oh31[:, 0:1].broadcast_to([32, 128 * k0]),
                   False, False, [d_rb, d_oh])
            m = mm(ps[b][:, 128 * k0:w], anti[:, :], near[:, h, (256 - w + 128 * k0):256], False, True, [d_near, d_anti], True)
            if i == 3:
                ql_free[h % 2] = [m]
            if i == 0:
                return m, CM[:, 384:512], [d_CM]
            return m, selm[:, sel_at[i]:sel_at[i] + w], [t_sel[i]]

        def product_a(h, i, j):
            return ps[6][:, 128 * i:128 * i + 128], ckv[:, j, :], [tk["ckv", j]] + (take(6) if i == 0 and j == 0 else [])

        def out_a(h, m):
            r = slice(64 * (h % 2), 64 * (h % 2) + 64)
            t = cpa(oa[h % 2][:, :], ps[6][:, :], [m] + oa_free[h % 2])
            put(6, t)
            ob = 7 if (h // 2) % 2 else 1
            m = mm(ps[ob][r, :], wuv[:, h, :], oa[h % 2][:, :], True, True, [t, d_wuv] + (take(ob) if h % 2 == 0 else []), True)
            oa_free[h % 2] = [m]
            if h % 2 == 1:
                mixed[h // 2] = split_ht(h // 2, ps[ob][:, :], [m], ht_free)
                put(ob, *mixed[h // 2])

        todo = [(h, i) for h in range(8) for i in range(4)]
        slots = rows4 + [at(C0 + 2048 * j, [128, 512])[:, :] for j in range(2)]
        for _ in units(todo, slots, rows_free + [tk["index"], tk["index"]], 4, scores_a, product_a, out_a):
            pass
        att_end = [(PE.sem, PE.n), (VE.sem, VE.n), (SE.sem, SE.n)]
        x_end = x_end + att_end

        def ln_residual(kt, lH, lL, ready):
            toks = [[] for _ in range(4)]

            def use_h(h):
                def use(i, b, m):
                    t = stt(x[:, i, 512 * h:512 * h + 512], x[:, i, 512 * h:512 * h + 512], ALPHA, ps[b][:, :], ALU.mult, ALU.add, [m] + x_end)
                    put(b, t)
                    toks[i].append(t)
                return use

            tok_group(lH, lL, kt, ready, [0, 1, 2, 3], use_h(0))
            last = tok_group(lH, lL, kt, ready, [4, 5, 6, 7], use_h(1))
            return toks, last

        def ln_stage(n, kt, lH, lL, ready, want_ht=True):
            r_g, r_b = row(0, 2 + n, x_end), row(1, 6 + n, x_end)
            toks, last = ln_residual(kt, lH, lL, ready)
            scratch = [at(TMP + 2048 * j, [128, 512])[:, :] for j in range(2)]
            hT, xt = ln_to_ht(toks, n, scratch, [last], r_g, r_b, want_ht)
            return hT, xt, last

        hT, xt, last = ln_stage(0, 8, hH, hL, mixed)
        x_end = [t for u in xt for t in u]

        def conv_ffn(layer, hT, big_free):
            R = Region(BIG, TOP)
            aH = R([128, 22, 512], F32R)
            aL = R([128, 22, 512], F32R)
            ft = [R([128, 512]) for _ in range(6)]
            f_free = [list(big_free) for _ in range(6)]
            atoks = []
            hold = {}
            cw = COLS[f"fcw{layer}"]

            def pair(t, b, m, mt):
                s = 2 * (mt % 2) + t
                w = cw + 3 * (mt + 22 * t)
                y = ft[s]
                a = act(y[:, :], ps[b][:, :], ACT.Identity, [m, d_cols] + f_free[s], scale=cols[:, w + 2:w + 3])
                for d in range(1, 3):
                    a = stt(y[:, d:512], ps[b][:, 0:512 - d], cols[:, w + 2 - d:w + 3 - d], y[:, d:512], ALU.mult, ALU.add, [a])
                put(b, a)
                if t == 0:
                    hold["g"] = act(y[:, :], y[:, :], ACT.Silu, [a])
                else:
                    g = ft[s - 1]
                    o = ft[4 + mt % 2]
                    a = tt(o[:, :], g[:, :], y[:, :], ALU.mult, [a, hold["g"]] + f_free[4 + mt % 2])
                    f_free[s - 1], f_free[s] = [a], [a]
                    h = act(aH[:, mt, :], o[:, :], ACT.Copy, [a] + big_free)
                    l = tt(aL[:, mt, :], o[:, :], aH[:, mt, :].bitcast(F32), ALU.subtract, [a, h] + big_free, q=GE)
                    f_free[4 + mt % 2] = [h, l]
                    atoks.append([h, l])

            for mt in range(22):
                feat_chunk(hT, [2 * (mt % 2), 2 * (mt % 2) + 1], lambda t, b, m, mt=mt: pair(t, b, m, mt))
            return aH, aL, atoks

        aH, aL, atoks = conv_ffn(0, hT, att_end + [t for q in hT for t in q])
        hT, xt, last = ln_stage(1, 22, aH, aL, atoks)
        x_end = [t for u in xt for t in u]

        prev = [last] + [t for q in hT for t in q]
        R = Region(BIG, TOP)
        v1 = R([128, 4, 512])
        vsq = R([128, 4, 512])
        sgg = R([128, 512])
        sgw = R([128, 8, 128])
        sgb = R([1, 1024])
        vst = R([128, 4, 32])
        gcT = [R([128, 516]) for _ in range(2)]
        yc = [R([128, 512]) for _ in range(4)]
        uT = [R([128, 512]) for _ in range(4)]
        od = [R([128, 512]) for _ in range(4)]
        d_sgg = dma(sgg[:, :], ins["sgg"].partition_broadcast(128).rearrange("p a n -> p (a n)"), prev)
        d_sgw = dma(sgw[:, :, :], ins["sgw"].rearrange("p (g t) -> p g t", g=8), prev)
        d_sgb = dma(sgb[:, :], ins["sgb"], prev)
        t_sgw = tt(sgw[:, :, :], sgw[:, :, :], U[:, :].unsqueeze(1).broadcast_to([128, 8, 128]), ALU.mult, [d_sgw, d_U], q=GE)

        def v_use(i, b, m):
            tk["v", i] = act(v1[:, i, :], ps[b][:, :], ACT.Gelu_apprx_tanh, [m] + prev)
            put(b, tk["v", i])

        tok_group(hH, hL, 8, hT, [0, 1, 2, 3], v_use)
        for i in range(4):
            v = h64(v1[:, i, :])
            mu, var = vst[:, i, 0:8], vst[:, i, 8:16]
            t = red(mu, v, ALU.add, [tk["v", i]] + prev)
            t = ts(mu, mu, 1.0 / 64, None, ALU.mult, after=[t])
            t = tt(v, v, bc64(mu), ALU.subtract, [t])
            u = tt(vsq[:, i, :], v1[:, i, :], v1[:, i, :], ALU.mult, [t] + prev, q=GE)
            tk["var", i] = red(var, h64(vsq[:, i, :]), ALU.add, [u])
        a = act(vst[:, :, 16:24], vst[:, :, 8:16], ACT.Sqrt, [tk["var", i] for i in range(4)], bias=col("eps5"), scale=1.0 / 64)
        a = rec(vst[:, :, 24:32], vst[:, :, 16:24], [a])
        t_v = []
        for i in range(4):
            t = tt(h64(v1[:, i, :]), h64(v1[:, i, :]), bc64(vst[:, i, 24:32]), ALU.mult, [a])
            t_v.append(tt(v1[:, i, :], v1[:, i, :], sgg[:, :], ALU.mult, [t, d_sgg]))

        gc_free = [list(prev), list(prev)]
        hold = {}

        def gcz(j):
            def use(t, b, m):
                s = j % 2
                if t == 0:
                    hold["gc"] = cpa(gcT[s][:, 0:512], ps[b][:, :], [m] + gc_free[s])
                    put(b, hold["gc"])
                else:
                    g = gcT[s]
                    a = tt(g[:, 0:512], g[:, 0:512], ps[b][:, :], ALU.mult, [m, hold["gc"]])
                    put(b, a)
                    w = COLS["od_cw"] + 3 * j
                    y = yc[j]
                    c = act(y[:, :], g[:, 0:512], ACT.Identity, [a, d_cols] + prev, scale=cols[:, w + 2:w + 3])
                    for d in range(1, 3):
                        c = stt(y[:, d:512], g[:, 0:512 - d], cols[:, w + 2 - d:w + 3 - d], y[:, d:512], ALU.mult, ALU.add, [c])
                    gc_free[s] = [c]
                    tk["yc", j] = c
            return use

        for j in range(4):
            feat_chunk(hT, [4 + 2 * (j % 2), 5 + 2 * (j % 2)], gcz(j))

        def gb_use(jj):
            def use(t, b, m):
                j = jj + t
                tk["od", j] = tt(od[j][:, :], yc[j][:, :], ps[b][:, :], ALU.mult, [m, tk["yc", j]] + prev)
                put(b, tk["od", j])
            return use

        for j in range(0, 4, 2):
            feat_chunk(hT, [4 + j, 5 + j], gb_use(j))

        def u_use(jj):
            def use(t, b, m):
                j = jj + t
                tk["u", j] = act(uT[j][:, :], ps[b][:, :], ACT.Gelu_apprx_tanh, [m] + prev)
                put(b, tk["u", j])
            return use

        for j in range(0, 4, 2):
            e = feat_chunk(hT, [4 + j, 5 + j], u_use(j))
        ht_free = [e]
        mixed = [None] * 8
        for j in range(4):
            mixed[4 + j] = split_ht(4 + j, od[j][:, :], [tk["od", j]], ht_free)
            b = j
            after = take(b) + [t_sgw, d_sgb, t_ones] + t_v
            for n in range(4):
                for g in (2 * j, 2 * j + 1):
                    o = ps[b][64 * (g % 2):64 * (g % 2) + 64, 128 * n:128 * n + 128]
                    mm(o, v1[:, n, 64 * g:64 * g + 64], sgw[:, g, :], True, False, after)
                    after = []
                    m = mm(o, ones[0:1, 0:64], sgb[0:1, 128 * g:128 * g + 128], False, True, (), n == 3 and g % 2 == 1)
            t = tt(uT[j][:, :], uT[j][:, :], ps[b][:, :], ALU.mult, [m, tk["u", j]])
            put(b, t)
            mixed[j] = split_ht(j, uT[j][:, :], [t], ht_free)
        odd_end = [t for q in mixed for t in q] + [m]

        hT, xt, last = ln_stage(2, 8, hH, hL, mixed)
        x_end = [t for u in xt for t in u]
        aH, aL, atoks = conv_ffn(1, hT, odd_end + [t for q in hT for t in q])
        hT, xt, last = ln_stage(3, 22, aH, aL, atoks, want_ht=False)
        stores = [dma(out[0, 128 * i:128 * i + 128, :], x[:, i, :], xt[i]) for i in range(4)]
        SP.items.append((stores + [d_u], lambda e: None, False))

        block = ctx.enter_context(nc.Block())

        @block.sync
        def _(e):
            SP.emit(e)

        @block.gpsimd
        def _(e):
            GE.emit(e)

        @block.scalar
        def _(e):
            SE.emit(e)

        @block.vector
        def _(e):
            VE.emit(e)

        @block.tensor
        def _(e):
            PE.emit(e)


def PE_tok(q):
    return (q.sem, q.n)


def shape_constants():
    f = np.float32
    i, j = np.arange(128)[:, None], np.arange(128)[None, :]
    out = {"ident": np.eye(128, dtype=f), "anti": np.eye(128, dtype=f)[::-1], "triu": (i <= j).astype(f)}
    r, c = np.arange(128)[:, None], np.arange(256)[None, :]
    ok = ((c // 64) >= (r // 64)) & ((c // 64) <= (r // 64) + 2)
    dist = np.abs(r + 128 - c)
    out["abias"] = np.concatenate([np.where(ok, -(2.0 ** (-8.0 * h / 4)) * dist, NEG) for h in range(1, 5)], axis=1).astype(f)
    levels = [((i // b) % 2 == 1) & ((j // b) == (i // b) - 1) for b in (1, 2, 4, 8, 16, 32, 64)]
    out["levels"] = np.concatenate([levels[0].T] + levels[1:], axis=1).astype(f)
    out["causal"] = np.where(384 + i - np.arange(512)[None, :] >= 0, 0.0, NEG).astype(f)
    n = np.maximum(255 - np.arange(384), 0)
    large = 16 + (np.log(np.maximum(n, 1) / 16) / math.log(128 / 16) * 16).astype(np.int64)
    bucket = np.where(n < 16, n, np.minimum(large, 31))
    out["oneh"] = (np.arange(32)[:, None] == bucket[None, :]).astype(f)
    out["oh31"] = (np.arange(32)[:, None] == 31).astype(f)
    return out


def kernel(**inputs):
    import concourse.bacc as bacc
    from concourse.bass_utils import run_bass_kernel_spmd

    a = {k: np.asarray(v) for k, v in inputs.items()}
    chunks = []
    for name, layer, k0, nk, cols in weight_plan():
        if name == "gate_up":
            w = np.concatenate([a[n][0][:, 128 * cols:128 * cols + 128] for n in ("ffn_w_gate", "ffn_w_up")], axis=1)
        else:
            w = a[name][layer][128 * k0:128 * (k0 + nk)]
            if cols == rng(cols[0], len(cols)):
                w = w[:, cols[0]:cols[0] + len(cols)]
            else:
                w = w[:, np.array(cols)]
        chunks.append(w.reshape(nk, 128, -1).transpose(1, 0, 2).reshape(-1))
    arrays = {"wbig": np.concatenate(chunks), "x": a["x"], "rel_bias_2": a["rel_bias_2"]}

    def tiles(v):
        return v.reshape(-1, 128).T

    def taps_(w):
        k, n = w.shape
        return w.reshape(k, n // 128, 128).transpose(2, 1, 0).reshape(128, -1)

    eps = np.full((128, 1), 1e-6, np.float32), np.full((128, 1), 1e-5, np.float32)
    bf = np.concatenate([a["ev_b_f_2"][0], np.zeros(120, np.float32)])[:, None]
    parts = [tiles(a["pre_mix_norm"][0]), tiles(a["pre_ffn_norm"][0]), taps_(a["ssd_conv_w"][0]), tiles(a["ssd_conv_b"][0]),
             taps_(a["gdn_conv_w"][0]), np.concatenate([a["gdn_norm_w"][0]] * 2)[:, None],
             tiles(a["ln_g_2"].reshape(-1)), tiles(a["ln_b_2"].reshape(-1)), taps_(a["od_conv_w_2"][0]), bf, *eps,
             taps_(a["ffn_conv_w_2"][0]), taps_(a["ffn_conv_w_2"][1])]
    arrays["cols"] = np.ascontiguousarray(np.concatenate(parts, axis=1))
    arrays["rows"] = np.concatenate([a["post_mix_norm"], a["post_ffn_norm"], a["ln_g_2"].reshape(4, 1024), a["ln_b_2"].reshape(4, 1024)], axis=0)
    arrays["brow"] = np.concatenate([a["ssd_dt_bias"][0], a["gdn_dt_bias"][0], a["ssd_A_log"][0], a["gdn_A_log"][0],
                                     a["attn_sinks"][0], a["ssd_D"][0], np.zeros(12, np.float32)])[None, :]
    arrays["ssd_nw"] = a["ssd_norm_w"]
    arrays["wuk"] = np.ascontiguousarray(a["ev_w_uk_2"][0].reshape(4, 2, 128, 64).transpose(1, 3, 0, 2).reshape(128, 512))
    arrays["wuv"] = np.ascontiguousarray(a["ev_w_uv_2"][0].transpose(1, 0, 2).reshape(128, 512))
    arrays["sgg"] = a["od_sgu_g_2"].reshape(1, 512)
    arrays["sgw"] = np.ascontiguousarray(a["od_sgu_w_2"][0].transpose(2, 0, 1).reshape(128, 1024))
    arrays["sgb"] = a["od_sgu_b_2"].reshape(1, 1024)
    arrays.update(shape_constants())
    arrays = {k: np.ascontiguousarray(v) for k, v in arrays.items()}

    nc = bacc.Bacc("TRN2", target_bir_lowering=False, num_devices=1)
    ins = {k: nc.dram_tensor("in_" + k, v.shape, mybir.dt.from_np(v.dtype), kind="ExternalInput").ap() for k, v in arrays.items()}
    out = nc.dram_tensor("out_0", (1, 512, 1024), F32, kind="ExternalOutput").ap()
    build(nc, ins, out)
    r = run_bass_kernel_spmd(nc, [{"in_" + k: v for k, v in arrays.items()}], core_ids=[0])
    return r.results[0]["out_0"]
```

```python
import math
from contextlib import ExitStack

import numpy as np
import concourse.bass as bass
from concourse import mybir

ALU = mybir.AluOpType
ACT = mybir.ActivationFunctionType
F32 = mybir.dt.float32
F32R = mybir.dt.float32r
AXX = mybir.AxisListType.X
NEG = -1.0e30
TAKEN = -3.0e38
ALPHA = 4.0 ** 0.25


def rng(a, n):
    return list(range(a, a + n))


def weight_plan():
    plan = []

    def feat(name, layer, *tiles):
        cols = [c for t in tiles for c in t]
        plan.append((name, layer, 0, 8, cols))

    def tok(name, layer, cols, kt=8):
        step = min(kt, 2048 // len(cols))
        sizes = [step] * (kt // step)
        if kt % step:
            sizes.insert(max(len(sizes) - 2, 1), kt % step)
        k = 0
        for n in sizes:
            plan.append((name, layer, k, n, cols))
            k += n

    w = "w_in"
    t = [rng(0, 64) + rng(128, 64), rng(64, 64) + rng(192, 64), rng(256, 128)]
    t += [rng(1024 + 128 * j, 128) for j in range(8)]
    g = [rng(2056 + 256 * kind + 128 * pair, 128) for pair in range(2) for kind in range(3)]
    xbc = t[3:]
    tok(w, 0, rng(384, 128) + rng(2048, 8) + rng(3084, 4) + rng(3080, 4) + rng(2824, 256))
    t = [g[0], g[1], g[2], t[0], t[1], t[2], g[3], g[4], g[5]] + xbc[4:] + xbc[:4]
    for j in range(0, 17, 2):
        feat(w, 0, *t[j:j + 2])
    tok(w, 0, rng(512, 256))
    tok(w, 0, rng(768, 256))
    for h in range(2):
        tok("w_out", 0, rng(512 * h, 512))
    for m in range(22):
        plan.append(("gate_up", 0, 0, 8, m))
    for h in range(2):
        tok("ffn_w_down", 0, rng(512 * h, 512), 22)
    w = "ev_w_in_2"
    tok(w, 0, rng(2248, 256))
    tok(w, 0, rng(2504, 256))
    feat(w, 0, rng(2760, 8) + rng(512, 24) + rng(1216, 8) + rng(512, 88))
    feat(w, 0, rng(640, 128), rng(768, 128))
    feat(w, 0, rng(896, 128), rng(1024, 128))
    feat(w, 0, rng(512, 128), rng(1152, 64) + rng(1152, 64))
    for j in range(4):
        feat(w, 0, rng(1224 + 128 * j, 128), rng(1736 + 128 * j, 128))
    for j in range(2):
        feat(w, 0, rng(256 * j, 128), rng(256 * j + 128, 128))
    for h in range(2):
        for k in (4, 0):
            plan.append(("ev_w_o_2", 0, k, 4, rng(512 * h, 512)))

    def conv_ffn(layer):
        for m in range(22):
            feat("ffn_w_up_2", layer, rng(128 * m, 128), rng(2816 + 128 * m, 128))
        for h in range(2):
            tok("ffn_w_down_2", layer, rng(512 * h, 512), 22)

    conv_ffn(0)
    w = "od_w_in_2"
    tok(w, 0, rng(512, 512))
    for j in range(4):
        feat(w, 0, rng(1536 + 128 * j, 128), rng(2048 + 128 * j, 128))
    for j in range(2):
        feat(w, 0, rng(1024 + 256 * j, 128), rng(1024 + 256 * j + 128, 128))
    for j in range(2):
        feat(w, 0, rng(256 * j, 128), rng(256 * j + 128, 128))
    for h in range(2):
        tok("od_w_o_2", 0, rng(512 * h, 512))
    conv_ffn(1)
    return plan


def chunk_width(c):
    return c[3] * (256 if c[0] == "gate_up" else len(c[4]))


TAIL = None
NORM_YIELDS = 1
MOST = 3
SLACK = 1200

COLS = {}
NCOLS = 0
for _n, _w in [("ssd_cw", 32), ("ssd_cb", 8), ("gdn_cw", 24), ("gdn_nw", 1),
               ("od_cw", 12), ("b_f", 1), ("eps6", 1), ("eps5", 1),
               ("fcw0", 132), ("fcw1", 132)]:
    COLS[_n] = NCOLS
    NCOLS += _w


def build(nc, ins, out):
    plan = weight_plan()
    offs = [0]
    for c in plan:
        offs.append(offs[-1] + 128 * chunk_width(c))

    u_dram = nc.dram_tensor("u_scratch", (8, 384), F32, kind="Internal").ap()

    ctx = ExitStack()
    with ctx:
        names = [0]
        base = (nc.sbuf_base + 63) // 64 * 64

        def at(offset, shape, dt=F32):
            names[0] += 1
            return nc.alloc_sbuf_tensor_at(f"t{names[0]}", shape, dt, offset=base + offset)

        class Region:
            def __init__(self, start, end):
                self.at, self.end = start, end

            def __call__(self, shape, dt=F32):
                n = 4
                for s in shape[1:]:
                    n *= s
                n = (n + 63) // 64 * 64
                assert self.at + n <= self.end, (self.at, n, self.end)
                t = at(self.at, shape, dt)
                self.at += n
                return t

        TOP = nc.sbuf_usable_end - base
        R0 = Region(0, TOP)
        raw = [R0([128, 2048]) for _ in range(2)]
        wH = [R0([128, 2048], F32R) for _ in range(2)]
        wL = [R0([128, 2048], F32R) for _ in range(2)]
        x = R0([128, 4, 1024])
        hH = R0([128, 8, 512], F32R)
        hL = R0([128, 8, 512], F32R)
        ident = R0([128, 128])
        U = R0([128, 128])
        ones = R0([128, 128])
        cols = R0([128, NCOLS])
        brow = R0([128, 48])
        rows = [R0([128, 1024]) for _ in range(2)]
        st = R0([128, 64])
        after_end = R0([128, 128])
        BIG = R0.at

        ps = [ctx.enter_context(nc.psum_tensor(f"ps{i}", [128, 512], F32)) for i in range(8)]
        bank = [[] for _ in range(8)]

        def take(*ids):
            r = []
            for i in ids:
                r += bank[i]
                bank[i] = []
            return r

        def put(i, *toks):
            bank[i] = bank[i] + list(toks)

        sems = {}

        def sem(name):
            sems[name] = ctx.enter_context(nc.semaphore(name))
            return name

        eta = {}

        class Queue:
            def __init__(self, name):
                self.sem, self.n, self.items, self.time = sem("s_" + name), 0, [], 0.0

            def add(self, fn, after, sig=True, cost=0.0):
                if sig:
                    self.n += 1
                self.items.append((list(after), fn, sig))
                self.time = max([self.time] + [eta[t] for t in after if t is not None]) + cost
                if not sig:
                    return None
                eta[self.sem, self.n] = self.time + 100
                return (self.sem, self.n)

            def emit(self, eng):
                seen = {}
                for after, fn, sig in self.items:
                    for t in after:
                        if t is not None and seen.get(t[0], 0) < t[1]:
                            eng.wait_ge(sems[t[0]], t[1])
                            seen[t[0]] = t[1]
                    i = fn(eng)
                    if sig is True:
                        i.then_inc(sems[self.sem], 1)
                    elif sig:
                        i.then_inc(sems[sig], 16)

        PE, VE, SE, GE, SP = Queue("pe"), Queue("ve"), Queue("se"), Queue("ge"), Queue("sp")

        ndma = [0]

        def dma(dst, src, after=(), name=None, count=1, q=SP):
            if name is None:
                ndma[0] += 1
                name = sem(f"d{ndma[0]}")
            q.items.append((list(after), lambda e: e.dma_start(dst, src), name))
            eta[name, 16 * count] = max([0.0] + [eta[t] for t in after if t is not None]) + 3000
            return (name, 16 * count)

        def size(o):
            n = 1
            for d in o.shape[1:]:
                n *= d
            return n

        def mm(o, l, r, start, stop, after=(), sig=False):
            return PE.add(lambda e: e.matmul(o, l, r, start=start, stop=stop), after, sig, size(o) * (0.42 if l.dtype == F32R else 1.68))

        def tr(o, i, after=(), sig=False):
            n = i.shape[0]
            return PE.add(lambda e: e.transpose(o, i, ident[0:n, 0:n]), after, sig, 107)

        table = [None]

        def act(o, i, f, after=(), bias=None, scale=None, accum=None):
            kw = {}
            if bias is not None:
                kw["bias"] = bias
            if scale is not None:
                kw["scale"] = scale
            if accum is not None:
                kw["accum_out"] = accum
            t = 60 + 0.87 * size(o)
            if f not in (ACT.Copy, ACT.Identity, ACT.Square, ACT.Relu) and f != table[0]:
                table[0] = f
                t += 1300
            return SE.add(lambda e: e.activation(o, i, f, **kw), after, True, t)

        def cpa(o, i, after=()):
            return act(o, i, ACT.Copy, after)

        def cost(q, o):
            return 70 + size(o) * (2.2 if q is GE else 1.05)

        def tt(o, a, b, op, after=(), q=VE):
            return q.add(lambda e: e.tensor_tensor(o, a, b, op), after, True, cost(q, o))

        def ts(o, a, s1, s2, op0, op1=ALU.bypass, after=(), q=VE):
            if s2 is None:
                return q.add(lambda e: e.tensor_scalar(o, a, s1, None, op0), after, True, cost(q, o))
            return q.add(lambda e: e.tensor_scalar(o, a, s1, s2, op0, op1), after, True, cost(q, o))

        def stt(o, a, s, b, op0, op1, after=()):
            return VE.add(lambda e: e.scalar_tensor_tensor(o, a, s, b, op0, op1), after, True, cost(VE, o))

        def cpv(o, i, after=(), q=VE):
            return q.add(lambda e: e.tensor_copy(o, i), after, True, cost(q, o))

        def rec(o, i, after=()):
            return VE.add(lambda e: e.reciprocal(o, i), after, True, cost(VE, o))

        def red(o, i, op, after=(), negate=None):
            return VE.add(lambda e: e.tensor_reduce(o, i, AXX, op, negate=negate), after, True, cost(VE, i))

        def mset(o, v, after=(), q=VE):
            return q.add(lambda e: e.memset(o, v), after)

        def col(name, j=0):
            return cols[:, COLS[name] + j:COLS[name] + j + 1]

        def load_x(i):
            return dma(x[:, i, :], ins["x"][0, 128 * i:128 * i + 128, :])

        d_x = [load_x(0)]
        d_cols = dma(cols[:, :], ins["cols"])
        d_pm = dma(rows[0][:, :], ins["rows"][10:11, :].partition_broadcast(128).rearrange("p a n -> p (a n)"))
        d_id = dma(ident[:, :], ins["ident"])
        t_ones = mset(ones[:, :], 1.0)

        raw_free = [[], []]
        hl_free = [[], []]
        landed = {}
        halves = {}
        w_sem = [sem("d_w0"), sem("d_w1")]

        def load(c):
            if c >= len(plan):
                return
            n = chunk_width(plan[c])
            r = c % 2
            src = ins["wbig"][offs[c]:offs[c + 1]].rearrange("(p n) -> p n", p=128)
            landed[c] = dma(raw[r][:, 0:n], src, raw_free[r], w_sem[r], c // 2 + 1)

        split_by = [VE]

        def split(c, q=None):
            if c >= len(plan) or c in halves:
                return
            n = chunk_width(plan[c])
            r = c % 2
            cut = n // plan[c][3] * ((plan[c][3] + 1) // 2)
            halves[c] = []
            for cs in (slice(0, cut), slice(cut, n)):
                a = act(wH[r][:, cs], raw[r][:, cs], ACT.Copy, [landed[c]] + hl_free[r])
                b = tt(wL[r][:, cs], raw[r][:, cs], wH[r][:, cs].bitcast(F32), ALU.subtract, [landed[c], a] + hl_free[r], q=q or split_by[0])
                halves[c].append([a, b])
            raw_free[r] = [a, b]
            load(c + 2)

        load(0)
        d_x += [load_x(1), load_x(2), load_x(3)]
        load(1)
        d_U = dma(U[:, :], ins["triu"])
        t_mask = ts(after_end[:, :], U[:, :], -1.0, -NEG, ALU.add, ALU.mult, [d_U])
        d_brow = dma(brow[:, 0:48], ins["brow"].partition_broadcast(128).rearrange("p a n -> p (a n)"))
        chunk = [0]

        def weights(j=0):
            split(chunk[0])
            split(chunk[0] + 1)
            c = chunk[0] + j
            n = chunk_width(plan[c])
            r = c % 2
            k = plan[c][3]
            return (c, wH[r][:, 0:n].rearrange("p (k c) -> p k c", k=k),
                    wL[r][:, 0:n].rearrange("p (k c) -> p k c", k=k), halves[c])

        def weights_done(tok):
            hl_free[chunk[0] % 2] = [tok]
            chunk[0] += 1

        def need(ready, k, tiles):
            if isinstance(ready, dict):
                return [t for i in tiles for t in ready[i, k // 4]]
            return ready[k]

        class Background:

            def __init__(self):
                self.chains = []

            def add(self, chain):
                self.chains.append([chain, 0.0])

            def advance(self, c):
                before = [q.time for q in (VE, SE, GE)]
                for _ in c[0]:
                    c[1] = max([PE.time] + [q.time for q, t in zip((VE, SE, GE), before) if q.time > t])
                    return
                self.chains.remove(c)

            def step(self, most=MOST):
                for _ in range(most):
                    ready = [c for c in self.chains if c[1] <= PE.time + SLACK]
                    if ready:
                        self.advance(min(ready, key=lambda c: c[1]))

            def finish(self):
                while self.chains:
                    self.advance(min(self.chains, key=lambda c: c[1]))

        bg = Background()

        def feat_chunk(ready, banks, use):
            c, H, L, w = weights()
            nt = plan_cols(c) // 128
            for t in range(nt):
                b = banks[t]
                s = slice(128 * t, 128 * t + 128)
                after = w[0] + take(b)
                for k in range(8):
                    if k == 4:
                        after = w[1]
                    mm(ps[b][:, :], H[:, k, s], hH[:, k, :], k == 0, False, after + need(ready, k, range(4)))
                    after = []
                    mm(ps[b][:, :], H[:, k, s], hL[:, k, :], False, False)
                    m = mm(ps[b][:, :], L[:, k, s], hH[:, k, :], False, k == 7, (), k == 7)
                    if k < 7:
                        bg.step()
                if t == nt - 1:
                    weights_done(m)
                use(t, b, m)
                bg.step()
            return m

        def plan_cols(c):
            return 256 if plan[c][0] == "gate_up" else len(plan[c][4])

        def feat_lead(ready, banks, use, between):
            parts = [weights(0), weights(1)]
            for pair in range(2):
                cs = slice(256 * pair, 256 * pair + 256)
                for n, (c, H, L, w) in enumerate(parts):
                    for t in range(2):
                        b = banks[2 * n + t]
                        s = slice(128 * t, 128 * t + 128)
                        after = w[0] + (take(b) if pair == 0 else [])
                        for k in range(8):
                            if k == 4:
                                after = w[1]
                            mm(ps[b][:, cs], H[:, k, s], hH[:, k, cs], k == 0, False, after + need(ready, k, (2 * pair, 2 * pair + 1)))
                            after = []
                            mm(ps[b][:, cs], H[:, k, s], hL[:, k, cs], False, False)
                            m = mm(ps[b][:, cs], L[:, k, s], hH[:, k, cs], False, k == 7, (), k == 7)
                        if pair == 1:
                            if t == 1:
                                weights_done(m)
                                if n == 0:
                                    split(c + 2)
                            use(n, t, b, m)
                    if pair == 0 and n == 0:
                        between()

        def tok_group(lH, lL, kt, ready, banks, use, tail=False, between={}):
            k0 = 0
            while k0 < kt:
                parts = [weights()]
                nk, n = plan[chunk[0]][3], len(plan[chunk[0]][4])
                at_k = [p[2] for p in plan[chunk[0]:chunk[0] + 2]]
                two = tail and k0 + nk < kt and k0 + nk + plan[chunk[0] + 1][3] == kt
                if two:
                    parts.append(weights(1))
                k_end = k0 + sum(plan[p[0]][3] for p in parts)
                order = [(i, 0) for i in range(4)]
                if two:
                    order = [(0, 0), (1, 0), (0, 1), (1, 1), (2, 0), (2, 1), (3, 0), (3, 1)]
                for i, j in order:
                    b = banks[i]
                    s = slice(128 * i, 128 * i + 128)
                    c, H, L, w = parts[j]
                    first, end = k0 == 0 and j == 0, k_end == kt and j == len(parts) - 1
                    after = w[0] + (take(b) if first else [])
                    nk = plan[c][3]
                    for k in range(nk):
                        if k == (nk + 1) // 2:
                            after = w[1]
                        kk = at_k[j] + k
                        mm(ps[b][:, 0:n], lH[:, kk, s], H[:, k, :], first and k == 0, False, after + need(ready, kk, (i,)))
                        after = []
                        mm(ps[b][:, 0:n], lH[:, kk, s], L[:, k, :], False, False)
                        m = mm(ps[b][:, 0:n], lL[:, kk, s], H[:, k, :], False, end and k == nk - 1, (), k == nk - 1)
                        if k % 4 == 3 and k < nk - 1:
                            bg.step()
                    if i == 3:
                        weights_done(m)
                        if two and j == 0:
                            split(c + 2, TAIL)
                    if j == len(parts) - 1 and k_end == kt:
                        use(i, b, m)
                    if k_end == kt and (i, j) in between:
                        between[i, j]()
                    bg.step()
                k0 = k_end
            return m

        def split_ht(k, src, after, free, cs=slice(0, 512), gain=None):
            if gain is None:
                a = act(hH[:, k, cs], src, ACT.Copy, after + free)
                b = tt(hL[:, k, cs], src, hH[:, k, cs].bitcast(F32), ALU.subtract, [a] + after + free)
            else:
                a = act(hH[:, k, cs], src, ACT.Identity, after + free, scale=gain)
                b = stt(hL[:, k, cs], src, gain, hH[:, k, cs].bitcast(F32), ALU.mult, ALU.subtract, [a] + after + free)
            return [a, b]

        def row(slot, j, after=()):
            return dma(rows[slot][:, :], ins["rows"][j:j + 1, :].partition_broadcast(128).rearrange("p a n -> p (a n)"), after)

        def turn(i, src, toks, free, ready, halves=(0, 1)):
            for j in halves:
                b = ((0, 1), (2, 4), (5, 6), (3, 7))[i][j]
                after = take(b) + toks + [d_id]
                for k in range(4):
                    m = tr(ps[b][:, 128 * k:128 * k + 128], src[:, 128 * (k + 4 * (j - halves[0])):128 * (k + 4 * (j - halves[0])) + 128], after, k == 3)
                    after = []
                ready[i, j] = split_ht(slice(4 * j, 4 * j + 4), ps[b][:, :].rearrange("p (k n) -> p k n", k=4), [m], free,
                                       slice(128 * i, 128 * i + 128))
                put(b, *ready[i, j])

        def rms_scale(i, o, src, toks, gain, free, junk, at_, done):
            a = act(junk, src, ACT.Square, toks + free, accum=st[:, at_ + i:at_ + 1 + i])
            yield
            a = act(st[:, at_ + 4 + i:at_ + 5 + i], st[:, at_ + i:at_ + 1 + i], ACT.Sqrt, [a, d_cols], bias=col("eps6"), scale=1.0 / 1024)
            yield
            a = rec(st[:, at_ + 8 + i:at_ + 9 + i], st[:, at_ + 4 + i:at_ + 5 + i], [a])
            yield
            done[i] = stt(o, src, st[:, at_ + 8 + i:at_ + 9 + i], rows[gain[0]][:, :], ALU.mult, ALU.mult, [a, gain[1]])

        def go(steps):
            if steps is not None:
                for _ in steps:
                    return

        def go_all(steps):
            if steps is not None:
                for _ in steps:
                    pass

        R = Region(BIG, TOP)
        GD = R.at
        xn = R([128, 4, 1024])
        R = Region(GD + 30720, TOP)
        gT = [R([128, 512]) for _ in range(6)]
        xT = [R([128, 512]) for _ in range(8)]
        zs = R([128, 4, 512])
        gz = R([128, 4, 256])
        og0 = R([128, 4, 128])
        lev = R([128, 7, 128])
        sm = R([128, 4, 16])
        sp = R([128, 9, 48])
        dtot = R([128, 48])
        beta = R([128, 4, 4])
        an = R([128, 12])
        decS = R([128, 2, 4])
        gs = R([128, 8])
        rsn = R([128, 4, 2, 2])
        AS = R.at
        R = Region(AS, TOP)
        qT = [R([128, 512]) for _ in range(2)]
        kT = R([128, 512])
        vtm = R([128, 4, 128])
        abias = R([128, 4, 256])
        S = R([128, 4, 256])
        PT = R([128, 8, 128])
        sx = R([128, 5, 4])
        R = Region(GD, GD + 6144)
        attT = at(GD + 30720, [128, 2, 512])
        og1 = at(GD + 30720 + 4096, [128, 4, 128])
        d_lev = dma(lev[:, :, :], ins["levels"].rearrange("p (a n) -> p a n", a=7))
        d_ab = dma(abias[:, :, :], ins["abias"].rearrange("p (h n) -> p h n", h=4))

        xtok = [[t] for t in d_x]
        hT = {}
        t_rms = {}
        for i in range(4):
            go_all(rms_scale(i, xn[:, i, :], x[:, i, :], xtok[i], (0, d_pm), [], xn[:, i, :], 0, t_rms))
            if i == 1:
                split(0)
        turn(0, xn[:, 0, :], [t_rms[0]], [], hT)
        turn(1, xn[:, 1, :], [t_rms[1]], [], hT)

        y_tmp = [rows[j // 2][:, 512 * (j % 2):512 * (j % 2) + 512] for j in range(4)]
        y_free = [[t_rms[3]] for _ in range(4)]
        tk = {}

        def small_use(i, b, m):
            a1 = cpa(vtm[:, i, :], ps[b][:, 0:128], [m])
            a2 = cpa(sm[:, i, :], ps[b][:, 128:144], [m])
            a3 = act(gz[:, i, :], ps[b][:, 144:400], ACT.Silu, [m])
            put(b, a1, a2, a3)
            tk["v", i], tk["sm", i], tk["gz", i] = a1, a2, a3

        tok_group(hH, hL, 8, hT, [0, 1, 2, 3], small_use, True,
                  {(0, 1): lambda: turn(2, xn[:, 2, :], [t_rms[2]], [], hT), (1, 1): lambda: turn(3, xn[:, 3, :], [t_rms[3]], [], hT)})
        xn_done = [(PE.sem, PE.n)]

        n_conv = [0]

        def conv4(b, m, o, w, bias):
            j = n_conv[0] % 4
            n_conv[0] += 1
            y = y_tmp[j]
            p = ps[b]
            a = act(y, p[:, :], ACT.Identity, [m, d_cols] + y_free[j], scale=cols[:, w + 3:w + 4])
            for d in range(1, 4):
                a = stt(y[:, d:512], p[:, 0:512 - d], cols[:, w + 3 - d:w + 4 - d], y[:, d:512], ALU.mult, ALU.add, [a])
            put(b, a)
            kw = {} if bias is None else {"bias": bias}
            a = act(o[:, :], y, ACT.Silu, [a], **kw)
            y_free[j] = [a]
            return a

        def v3(t, n=12):
            return t.rearrange("p (i h) -> p i h", h=n)

        e0, e1, e2, e3, da = (sp[:, j, :] for j in range(5))
        csum, tot = sp[:, 5, :], sp[:, 6, :]
        eg, dl = sp[:, 7, :], sp[:, 8, :]

        def steps():
            t_sm = [tk["sm", i] for i in range(4)]
            a = tt(v3(e0), sm[:, :, 0:12], brow[:, 0:12].unsqueeze(1).broadcast_to([128, 4, 12]), ALU.add, t_sm + [d_brow])
            b = stt(e1, e0, -1.0, e0, ALU.mult, ALU.max, [a])
            b = act(e1, e1, ACT.Exp, [b], scale=-1.0)
            c = ts(e2, e1, 1.0, None, ALU.add, after=[b])
            d = act(e3, e2, ACT.Ln, [c])
            a2 = act(an[:, :], brow[:, 12:24], ACT.Exp, [d_brow])
            a3 = act(beta[:, :, :], sm[:, :, 12:16], ACT.Exp, t_sm, scale=-1.0)
            c = ts(e2, e2, -1.0, 1e-30, ALU.add, ALU.max, [c, d])
            c = rec(da, e2, [c])
            c = tt(da, da, e3, ALU.mult, [c, d])
            c = tt(da, da, e1, ALU.mult, [c])
            f = ts(e2, e2, 1e-30, None, ALU.is_equal, after=[c])
            f = tt(e2, e2, e1, ALU.mult, [f])
            c = tt(da, da, e2, ALU.add, [c, f])
            c = stt(e0, e0, 0.0, da, ALU.max, ALU.add, [c])
            tk["dt"] = c
            a2 = ts(an[:, :], an[:, :], -1.0, None, ALU.mult, after=[a2])
            tk["da"] = tt(v3(da), v3(e0), an[:, :].unsqueeze(1).broadcast_to([128, 4, 12]), ALU.mult, [c, a2])
            a3 = ts(beta[:, :, :], beta[:, :, :], 1.0, None, ALU.add, after=[a3])
            tk["beta"] = rec(beta[:, :, :], beta[:, :, :], [a3])
            yield
            yield
            m1 = mm(ps[7][:, 0:48], U[:, :], da, True, True, take(7) + [tk["da"], d_U], True)
            m2 = mm(ps[7][:, 64:112], ones[:, :], da, True, True, [t_ones], True)
            t_cs = cpv(csum, ps[7][:, 0:48], [m1, m2])
            t_tot = cpv(tot, ps[7][:, 64:112], [m2])
            put(7, t_cs, t_tot)
            a = tt(dl, tot, csum, ALU.subtract, [t_cs, t_tot])
            tk["dl"] = act(dl, dl, ACT.Exp, [a])
            tk["eg"] = act(eg, csum, ACT.Exp, [t_cs])
            tk["dtot"] = act(dtot[:, :], tot, ACT.Exp, [t_tot])
            for p in range(2):
                for h in range(2):
                    tk["decS"] = cpv(decS[64 * h:64 * h + 64, p, :], v3(dtot[64 * h:64 * h + 64, :])[:, :, 8 + 2 * p + h], [tk["dtot"]])
            tk["cs"] = t_cs
            yield

        sink = brow[:, 24:28]

        def attention(bA, bB):
            vts = [tk["v", i] for i in range(4)]
            S_free, PT_free = [], []
            for i in range(4):
                k0 = 128 * max(i - 1, 0)
                n = 128 * (i + 1) - k0
                nb = n // 128
                r = []
                for h in range(4):
                    b = (bA, bB)[h // 2]
                    p = slice(64 * (h // 2), 64 * (h // 2) + 64)
                    after = [tk["qA"], tk["qB"], tk["k"]] + (take(b) if h % 2 == 0 else [])
                    m = mm(ps[b][:, 256 * (h % 2):256 * (h % 2) + n], qT[h % 2][p, 128 * i:128 * i + 128],
                           kT[p, k0:k0 + n], True, True, after, h % 2 == 1)
                    if h % 2 == 1:
                        v = ps[b][:, :].rearrange("p (h n) -> p h n", h=2)[:, :, 0:n]
                        t = tt(S[:, h - 1:h + 1, 0:n], v, abias[:, h - 1:h + 1, 256 - n:256], ALU.add, [m, d_ab] + S_free)
                        put(b, t)
                        r.append(t)
                yield
                mx, nm, sume, es, rd = (sx[:, j, :] for j in range(5))
                t = red(mx, S[:, :, 0:n], ALU.max, r + S_free)
                t = tt(mx, mx, sink, ALU.max, [t, d_brow])
                u = tt(es, sink, mx, ALU.subtract, [t])
                t = ts(nm, mx, -1.0, None, ALU.mult, after=[t])
                e = []
                for h in range(4):
                    e.append(act(S[:, h, 0:n], S[:, h, 0:n], ACT.Exp, [t], bias=nm[:, h:h + 1], accum=sume[:, h:h + 1]))
                e.append(act(es, es, ACT.Exp, [u]))
                t = tt(rd, sume, es, ALU.add, e)
                t = rec(rd, rd, [t])
                t = tt(S[:, :, 0:n], S[:, :, 0:n], rd.unsqueeze(2).broadcast_to([128, 4, n]), ALU.mult, [t])
                yield
                yield
                toks = []
                for hh in range(2):
                    b = (bA, bB)[hh]
                    after = take(b) + [t, d_id]
                    for h in range(2 * hh, 2 * hh + 2):
                        for j in range(nb):
                            c = (h % 2) * 2 + j
                            m = tr(ps[b][:, 128 * c:128 * c + 128], S[:, h, 128 * j:128 * j + 128], after, h % 2 == 1 and j == nb - 1)
                            after = []
                    v = ps[b][:, :].rearrange("p (h j n) -> p h j n", h=2, j=2)[:, :, 0:nb, :]
                    o = PT[:, 4 * hh:4 * hh + 4, :].rearrange("p (h j) n -> p h j n", h=2)[:, :, 0:nb, :]
                    e = cpa(o, v, [m] + PT_free)
                    put(b, e)
                    toks.append(e)
                S_free = [m]
                yield
                after = toks + vts + take(bA)
                for h in range(4):
                    p = slice(64 * (h % 2), 64 * (h % 2) + 64)
                    for j in range(nb):
                        m = mm(ps[bA][p, 128 * (h // 2):128 * (h // 2) + 128], vtm[:, k0 // 128 + j, 64 * (h // 2):64 * (h // 2) + 64],
                               PT[:, 2 * h + j, :], j == 0, j == nb - 1, after, h == 3 and j == nb - 1)
                        after = []
                PT_free = [m]
                t = cpa(attT[:, :, 128 * i:128 * i + 128], ps[bA][:, 0:256].rearrange("p (a n) -> p a n", a=2), [m] + tk["g0 read"])
                put(bA, t)
                yield
            tk["att"] = [t]
            tk["as"] = [t, m]

        def h64(t):
            return t.rearrange("p (h d) -> p h d", d=64)

        def bc64(t):
            return t.unsqueeze(2).broadcast_to([128, 8, 64])

        R = Region(AS, TOP)
        xs = R([128, 512])
        xc = R([128, 512])
        xd = R([128, 512])
        Dm = R([128, 8, 128])
        SM = R([128, 2, 128])
        Bt = R([128, 256])
        state = R([128, 512])
        yall = R([128, 4, 512])

        def state_space(bA, bB):
            start = tk["as"]
            free = {n: start for n in ("xs", "xc", "xd", "Dm", "SM", "Bt")}
            t_state = None
            y_toks = []
            while ("x", 3) not in tk:
                yield
            for i in range(4):
                ts_ = slice(128 * i, 128 * i + 128)
                after = take(bA) + [d_id]
                for j in range(4):
                    m = tr(ps[bA][:, 128 * j:128 * j + 128], xT[j][:, ts_], after + [tk["x", j]], j == 3)
                    after = []
                t_xs = cpa(xs[:, :], ps[bA][:, :], [m] + free["xs"])
                put(bA, t_xs)
                after = take(bB)
                for g in range(2):
                    tr(ps[bB][:, 128 * g:128 * g + 128], xT[4 + g][:, ts_], after + [tk["x", 4 + g]])
                    after = []
                for g in range(2):
                    m = mm(ps[bB][:, 256 + 128 * g:384 + 128 * g], xT[4 + g][:, ts_], xT[6 + g][:, ts_], True, True, [tk["x", 6 + g]], g == 1)
                t_Bt = cpa(Bt[:, :], ps[bB][:, 0:256], [m] + free["Bt"])
                t_SM = tt(SM[:, :, :], ps[bB][:, 256:512].rearrange("p (g n) -> p g n", g=2),
                          U[:, :].unsqueeze(1).broadcast_to([128, 2, 128]), ALU.mult, [m, t_Bt, d_U] + free["SM"])
                put(bB, t_Bt, t_SM)
                t_xc = tt(h64(xc[:, :]), h64(xs[:, :]), bc64(v3(e0)[:, i, 0:8]), ALU.mult, [t_xs, tk["dt"]] + free["xc"], q=GE)
                if i < 3:
                    t_xd = tt(h64(xd[:, :]), h64(xc[:, :]), bc64(v3(dl)[:, i, 0:8]), ALU.mult, [t_xc, tk["dl"]] + free["xd"], q=GE)
                else:
                    tk["nwr"] = dma(xd[:, :], ins["ssd_nw"].partition_broadcast(128).rearrange("p a n -> p (a n)"), free["xd"])
                yield
                td = []
                for q in range(2):
                    b = (bA, bB)[q]
                    after = take(b) + [tk["da"]]
                    for h in range(4 * q, 4 * q + 4):
                        m = mm(ps[b][:, 128 * (h % 4):128 * (h % 4) + 128], v3(da)[:, i, h:h + 1].broadcast_to([128, 128]), U[:, :],
                               True, True, after, h % 4 == 3)
                        after = []
                    for h in range(4 * q, 4 * q + 4):
                        t = ts(Dm[:, h, :], ps[b][:, 128 * (h % 4):128 * (h % 4) + 128], v3(csum)[:, i, h:h + 1], 0.0,
                               ALU.subtract, ALU.min, [m, tk["cs"]] + free["Dm"])
                    put(b, t)
                    e = act(Dm[:, 4 * q:4 * q + 4, :], Dm[:, 4 * q:4 * q + 4, :], ACT.Exp, [t])
                    td.append(tt(Dm[:, 4 * q:4 * q + 4, :], Dm[:, 4 * q:4 * q + 4, :],
                                 SM[:, q, :].unsqueeze(1).broadcast_to([128, 4, 128]), ALU.mult, [e, t_SM], q=GE))
                    yield
                free["SM"] = td
                y = yall[:, i, :]
                if i > 0:
                    after = take(bB) + [t_state]
                    for g in range(2):
                        m2 = mm(ps[bB][:, 256 * g:256 * g + 256], xT[6 + g][:, ts_], state[:, 256 * g:256 * g + 256], True, True, after, g == 1)
                        after = []
                    t_off = tt(h64(y), h64(ps[bB][:, :]), bc64(v3(eg)[:, i, 0:8]), ALU.mult, [m2, tk["eg"]] + start)
                    put(bB, t_off)
                    yield
                if i < 3:
                    after = take(bB) + [t_Bt, t_xd]
                    for g in range(2):
                        m3 = mm(ps[bB][:, 256 * g:256 * g + 256], Bt[:, 128 * g:128 * g + 128], xd[:, 256 * g:256 * g + 256], True, True, after, g == 1)
                        after = []
                    free["Bt"] = [m3]
                    free["xd"] = [m3]
                    if i == 0:
                        t_state = cpv(state[:, :], ps[bB][:, :], [m3] + start)
                    else:
                        u = tt(h64(state[:, :]), h64(state[:, :]), bc64(v3(dtot[:, :])[:, i, 0:8]), ALU.mult, [tk["dtot"], t_state, m2], q=GE)
                        t_state = tt(state[:, :], state[:, :], ps[bB][:, :], ALU.add, [u, m3])
                    put(bB, t_state)
                yield
                after = take(bA) + td + [t_xc]
                for h in range(8):
                    m = mm(ps[bA][:, 64 * h:64 * h + 64], Dm[:, h, :], xc[:, 64 * h:64 * h + 64], True, True, after, h == 7)
                    after = []
                free["Dm"] = [m]
                free["xc"] = [m, t_xd]
                if i > 0:
                    t = tt(y, y, ps[bA][:, :], ALU.add, [t_off, m])
                else:
                    t = cpv(y, ps[bA][:, :], [m] + start)
                put(bA, t)
                u = tt(h64(xs[:, :]), h64(xs[:, :]), bc64(brow[:, 28:36]), ALU.mult, [t_xc, t_xs, d_brow], q=GE)
                t = tt(y, y, xs[:, :], ALU.add, [t, u], q=GE)
                free["xs"] = [t]
                y_toks.append(t)
                yield
            tk["y"] = y_toks

        def hd(t):
            return t.rearrange("p i (h d) -> p i h d", h=2)

        def bcg(t):
            return t.unsqueeze(3).broadcast_to([128, 4, 2, 64])

        def q4v(t):
            return t.rearrange("p (n c) -> p n c", n=4)

        def delta(p, og, start, b0, b1, b2, b3):
            R = Region(GD, GD + 30720)
            rhs = R([128, 4, 2, 128])
            kd = R([128, 4, 128])
            qeT = R([128, 4, 128])
            QK = R([128, 8, 128])
            two = R.at
            qkv = R([128, 4, 3, 128])
            kb = R([128, 4, 128])
            qe = R([128, 4, 128])
            three = R.at
            knT = R([128, 4, 128])
            kbT = R([128, 4, 128])
            qnT = R([128, 4, 128])
            R = Region(two, three)
            AT = R([128, 8, 128])
            XT = R([128, 8, 128])
            Dg = at(two + 4096, [128, 8, 128])
            Sg = R([128, 64])
            vn = [R([128, 2, 64]) for _ in range(2)]
            uu2 = at(two, [128, 2, 4, 64])
            wT = at(two + 2048, [128, 4, 128])
            R = Region(three, GD + 30720)
            X = R([128, 8, 128])
            P1 = R([128, 8, 128])
            while ("g", 3 * p + 2) not in tk or "cs" not in tk:
                yield
            tq = []
            for i in range(4):
                b = (b0, b1)[i % 2]
                after = take(b) + [d_id]
                for j in range(3):
                    m = tr(ps[b][:, 128 * j:128 * j + 128], gT[3 * p + j][:, 128 * i:128 * i + 128], after + [tk["g", 3 * p + j]], j == 2)
                    after = []
                t = cpa(qkv[:, i, :, :], ps[b][:, 0:384].rearrange("p (a n) -> p a n", a=3), [m] + start)
                put(b, t)
                tq.append(t)
                if i % 2 == 1:
                    yield
            if p == 0:
                tk["g0 read"] = [m]
            s_og = start + tk["g0 read"]
            for j in range(2):
                t = tt(og[:, :, :], qkv[:, :, j, :], qkv[:, :, j, :], ALU.mult, tq + s_og + ([t] if j else []))
                t = red(rsn[:, :, j, :], hd(og[:, :, :]), ALU.add, [t] + start)
            t = act(rsn[:, :, :, :], rsn[:, :, :, :], ACT.Sqrt, [t, d_cols], bias=col("eps6"))
            t_rs = rec(rsn[:, :, :, :], rsn[:, :, :, :], [t])
            t = ts(rsn[:, :, 0, :], rsn[:, :, 0, :], 0.125, None, ALU.mult, after=[t_rs])
            qv, kv, vv = (hd(qkv[:, :, j, :]) for j in range(3))
            hs = slice(8 + 2 * p, 10 + 2 * p)
            egp, dlp, bep = v3(eg)[:, :, hs], v3(dl)[:, :, hs], beta[:, :, 2 * p:2 * p + 2]
            t_kn = tt(kv, kv, bcg(rsn[:, :, 1, :]), ALU.mult, [t_rs])
            t_kb = tt(hd(kb[:, :, :]), kv, bcg(bep), ALU.mult, [t_kn, tk["beta"]] + start)
            t_qn = tt(qv, qv, bcg(rsn[:, :, 0, :]), ALU.mult, [t])
            t_qe = tt(hd(qe[:, :, :]), qv, bcg(egp), ALU.mult, [t_qn, tk["eg"]] + start)
            t_vb = tt(rhs[:, :, :, 0:64], vv, bcg(bep), ALU.mult, tq + [tk["beta"]] + start, q=GE)
            t_kbe = tt(rhs[:, :, :, 64:128], hd(kb[:, :, :]), bcg(egp), ALU.mult, [t_kb, tk["eg"]] + start, q=GE)
            t_kd = tt(hd(kd[:, :, :]), kv, bcg(dlp), ALU.mult, [t_kn, tk["dl"]] + start, q=GE)
            for _ in range(NORM_YIELDS):
                yield
            ttr = []
            for n, (src, dst, w) in enumerate([(qkv[:, :, 1, :], knT, t_kn), (kb[:, :, :], kbT, t_kb),
                                               (qkv[:, :, 0, :], qnT, t_qn), (qe[:, :, :], qeT, t_qe)]):
                b = (b0, b1)[n % 2]
                after = take(b) + [w]
                for i in range(4):
                    m = tr(ps[b][:, 128 * i:128 * i + 128], src[:, i, :], after, i == 3)
                    after = []
                t = cpa(dst[:, :, :], ps[b][:, :].rearrange("p (i n) -> p i n", i=4), [m] + start)
                put(b, t)
                ttr.append(t)
                if n % 2 == 1:
                    yield
            two_free = [m, t_vb, t_kbe, t_kd]
            td = []
            for q in range(2):
                b = (b2, b3)[q]
                h = 8 + 2 * p + q
                after = take(b) + [tk["da"]]
                for i in range(4):
                    m = mm(ps[b][:, 128 * i:128 * i + 128], v3(da)[:, i, h:h + 1].broadcast_to([128, 128]), U[:, :], True, True, after, i == 3)
                    after = []
                for i in range(4):
                    t = stt(Dg[:, 4 * q + i, :], ps[b][:, 128 * i:128 * i + 128], v3(csum)[:, i, h:h + 1], after_end[:, :],
                            ALU.subtract, ALU.add, [m, tk["cs"], t_mask] + two_free)
                put(b, t)
                td.append(act(Dg[:, 4 * q:4 * q + 4, :], Dg[:, 4 * q:4 * q + 4, :], ACT.Exp, [t]))
                yield
            ta, tqk = [], []
            for src, dst, lst, bb in ((kbT, AT, ta, (b0, b1)), (qnT, QK, tqk, (b2, b3))):
                for q in range(2):
                    b = bb[q]
                    s = slice(64 * q, 64 * q + 64)
                    after = take(b) + ttr
                    for i in range(4):
                        m = mm(ps[b][:, 128 * i:128 * i + 128], knT[s, i, :], src[s, i, :], True, True, after, i == 3)
                        after = []
                    t = tt(dst[:, 4 * q:4 * q + 4, :], q4v(ps[b][:, :]), Dg[:, 4 * q:4 * q + 4, :], ALU.mult, [m, td[q]] + two_free + start)
                    put(b, t)
                    lst.append(t)
                yield
            three_free = [m] + ta + tqk
            bc4 = [128, 4, 128]
            I4 = ident[:, :].unsqueeze(1).broadcast_to(bc4)
            t_x, t_xt = [None, None], [None, None]
            for q in range(2):
                sl = slice(4 * q, 4 * q + 4)
                t = tt(XT[:, sl, :], AT[:, sl, :], lev[:, 0, :].unsqueeze(1).broadcast_to(bc4), ALU.mult, [ta[q], d_lev] + tqk)
                b = (b0, b1)[q]
                after = take(b) + [t]
                for n in range(4 * q, 4 * q + 4):
                    m = tr(ps[b][:, 128 * (n % 4):128 * (n % 4) + 128], XT[:, n, :], after, n % 4 == 3)
                    after = []
                t_x[q] = tt(X[:, sl, :], I4, q4v(ps[b][:, :]), ALU.subtract, [m, d_id] + three_free)
                put(b, t_x[q])
                t_xt[q] = tt(XT[:, sl, :], I4, XT[:, sl, :], ALU.subtract, [t, m, d_id], q=GE)
                yield
            p1_free = [three_free, three_free]
            for lv in range(1, 7):
                tp = [None, None]
                for q in range(2):
                    sl = slice(4 * q, 4 * q + 4)
                    b = (b0, b1)[q]
                    after = take(b) + [ta[q], t_x[q]]
                    for n in range(4 * q, 4 * q + 4):
                        m = mm(ps[b][:, 128 * (n % 4):128 * (n % 4) + 128], AT[:, n, :], X[:, n, :], True, True, after, n % 4 == 3)
                        after = []
                    tp[q] = tt(P1[:, sl, :], q4v(ps[b][:, :]), lev[:, lv, :].unsqueeze(1).broadcast_to(bc4), ALU.mult, [m, d_lev] + p1_free[q])
                    put(b, tp[q])
                    yield
                for q in range(2):
                    sl = slice(4 * q, 4 * q + 4)
                    b, bt = (b2, b3)[q], (b0, b1)[q]
                    after = take(bt) + [tp[q], t_xt[q]]
                    for n in range(4 * q, 4 * q + 4):
                        m = mm(ps[bt][:, 128 * (n % 4):128 * (n % 4) + 128], P1[:, n, :], XT[:, n, :], True, True, after, n % 4 == 3)
                        after = []
                    if lv < 6:
                        after = take(b)
                        for n in range(4 * q, 4 * q + 4):
                            mq = mm(ps[b][:, 128 * (n % 4):128 * (n % 4) + 128], XT[:, n, :], P1[:, n, :], True, True, after, n % 4 == 3)
                            after = []
                        t_x[q] = tt(X[:, sl, :], X[:, sl, :], q4v(ps[b][:, :]), ALU.subtract, [mq, t_x[q]])
                        put(b, t_x[q])
                        m2 = mq
                    else:
                        m2 = m
                    t_xt[q] = tt(XT[:, sl, :], XT[:, sl, :], q4v(ps[bt][:, :]), ALU.subtract, [m, m2, t_xt[q]])
                    put(bt, t_xt[q])
                    p1_free[q] = [m2]
                    yield
            after = take(b2, b3) + t_xt + [t_vb, t_kbe]
            for n in range(8):
                i, h = n % 4, n // 4
                m1 = mm(ps[b2][:, 64 * n:64 * n + 64], XT[:, n, :], rhs[:, i, h, 0:64], True, True, after, n == 7)
                after = []
                m2 = mm(ps[b3][64 * h:64 * h + 64, 128 * i:128 * i + 128], rhs[:, i, h, 64:128], XT[:, n, :], True, True, [], n == 7)
            t_u = cpv(uu2[:, :, :, :], ps[b2][:, :].rearrange("p (h i d) -> p h i d", i=4, h=2), [m1] + p1_free[0] + p1_free[1])
            t_w = cpa(wT[:, :, :], ps[b3][:, :].rearrange("p (i n) -> p i n", i=4), [m2] + p1_free[0] + p1_free[1])
            put(b2, t_u)
            put(b3, t_w)
            yield
            t_S = None
            vn_free = [two_free, two_free]
            t_o = []
            for i in range(4):
                s = i % 2
                t_v = []
                if i > 0:
                    after = take(b0, b1) + [t_w, t_S]
                    for h in range(2):
                        r = slice(64 * h, 64 * h + 64)
                        b = (b0, b1)[h]
                        m = mm(ps[b][:, 0:64], wT[r, i, :], Sg[r, :], True, True, after, True)
                        after = []
                        t = tt(vn[s][:, h, :], uu2[:, h, i, :], ps[b][:, 0:64], ALU.subtract, [m, t_u] + vn_free[s])
                        put(b, t)
                        t_v.append(t)
                else:
                    t_v.append(cpv(vn[s][:, :, :], uu2[:, :, i, :], [t_u] + vn_free[s]))
                yield
                if i < 3:
                    after = take(b0) + [t_kd] + t_v
                    for h in range(2):
                        m = mm(ps[b0][64 * h:64 * h + 64, 0:64], kd[:, i, 64 * h:64 * h + 64], vn[s][:, h, :], True, True, after, h == 1)
                        after = []
                after = take(b2, b3) + tqk + t_v
                for h in range(2):
                    r = slice(64 * h, 64 * h + 64)
                    b = (b2, b3)[h]
                    if i > 0:
                        mm(ps[b][:, 0:64], qeT[r, i, :], Sg[r, :], True, False, after)
                        after = []
                    mo = mm(ps[b][:, 0:64], QK[:, 4 * h + i, :], vn[s][:, h, :], i == 0, True, after, True)
                    after = []
                    t = cpa(og[:, i, 64 * h:64 * h + 64], ps[b][:, 0:64], [mo, t_kn, t_qn])
                    put(b, t)
                    t_o.append(t)
                if i < 3:
                    if i == 0:
                        t_S = cpv(Sg[:, :], ps[b0][:, 0:64], [m] + two_free)
                    else:
                        t_S = stt(Sg[:, :], Sg[:, :], decS[:, p, i:i + 1], ps[b0][:, 0:64], ALU.mult, ALU.add, [m, mo, t_S, tk["decS"]])
                    put(b0, t_S)
                    vn_free[s] = [m, mo]
                yield
            sq_ = qeT[:, :, :]
            t = act(sq_, og[:, :, :], ACT.Square, t_o + [mo, t_S])
            t = red(rsn[:, :, 0, :], hd(sq_), ALU.add, [t])
            t = act(rsn[:, :, 0, :], rsn[:, :, 0, :], ACT.Sqrt, [t], bias=col("eps6"), scale=1.0 / 64)
            t = rec(rsn[:, :, 0, :], rsn[:, :, 0, :], [t])
            t = tt(hd(og[:, :, :]), hd(og[:, :, :]), bcg(rsn[:, :, 0, :]), ALU.mult, [t])
            t = tt(og[:, :, :], og[:, :, :], gz[:, :, 128 * p:128 * p + 128], ALU.mult, [t] + [tk["gz", i] for i in range(4)])
            tk["og", p] = [t]
            tk["gd", p] = [t, mo]
            yield

        mixed = [[] for _ in range(8)]

        def state_space_out(banks):
            while "proj" not in tk:
                yield
            ht_free = tk["proj"]
            r = split_ht(slice(0, 2), attT[:, :, :], tk["att"], ht_free)
            mixed[0], mixed[1] = r, r
            u = None
            y_toks = []
            for i in range(4):
                y = yall[:, i, :]
                t = tt(y, y, zs[:, i, :], ALU.mult, [tk["y"][i], tk["z", i, 0], tk["z", i, 1]])
                y_toks.append(t)
                for g in range(2):
                    u = act(xs[:, 0:256], y[:, 256 * g:256 * g + 256], ACT.Square, [t, u, tk["y"][3]], accum=gs[:, 2 * i + g:2 * i + g + 1])
            a = act(gs[:, :], gs[:, :], ACT.Sqrt, [u, d_cols], bias=col("eps6"), scale=1.0 / 256)
            a = rec(gs[:, :], gs[:, :], [a])
            yield
            for i in range(4):
                y = yall[:, i, :]
                for g in range(2):
                    t = stt(y[:, 256 * g:256 * g + 256], y[:, 256 * g:256 * g + 256], gs[:, 2 * i + g:2 * i + g + 1],
                            xd[:, 256 * g:256 * g + 256], ALU.mult, ALU.mult, [a, y_toks[i], tk["nwr"]])
                yield
                b = banks[i % len(banks)]
                after = take(b) + [t, d_id]
                for j in range(4):
                    m = tr(ps[b][:, 128 * j:128 * j + 128], y[:, 128 * j:128 * j + 128], after, j == 3)
                    after = []
                r = split_ht(slice(2, 6), ps[b][:, :].rearrange("p (k n) -> p k n", k=4), [m], ht_free, slice(128 * i, 128 * i + 128))
                put(b, *r)
                for k in range(2, 6):
                    mixed[k] = mixed[k] + r
                yield
            tk["ssd out"] = m

        def delta_out(p, b):
            while "proj" not in tk:
                yield
            after = take(b) + tk["og", p]
            for i in range(4):
                m = tr(ps[b][:, 128 * i:128 * i + 128], (og0, og1)[p][:, i, :], after, i == 3)
                after = []
            r = split_ht(6 + p, ps[b][:, :], [m], tk["proj"], gain=col("gdn_nw"))
            put(b, *r)
            mixed[6 + p] = r
            tk["gd out", p] = m
            yield

        def delta_chain():
            yield from delta(0, og0, xn_done, 2, 3, 4, 5)
            yield from delta(1, og1, tk["gd", 0], 2, 3, 4, 5)
            for p in range(2):
                yield from delta_out(p, 2 + p)

        def short_chain():
            yield from steps()
            while "k" not in tk or "g0 read" not in tk:
                yield
            yield from attention(6, 7)
            yield from state_space(6, 7)
            yield from state_space_out((6, 7))

        tiles = [("g", 0), ("g", 1), ("g", 2), "qA", "qB", "k", ("g", 3), ("g", 4), ("g", 5)]
        tiles += [("x", j) for j in (4, 5, 6, 7, 0, 1, 2, 3)]

        def in_use(first):
            def use(t, b, m):
                n = tiles[first + t]
                if n == "qA" or n == "qB":
                    q = qT[0 if n == "qA" else 1]
                    a = act(q[:, :], ps[b][:, :], ACT.Copy, [m], scale=0.125)
                    put(b, a)
                elif n == "k":
                    a = cpa(kT[:, :], ps[b][:, :], [m])
                    put(b, a)
                elif n[0] == "x":
                    a = conv4(b, m, xT[n[1]], COLS["ssd_cw"] + 4 * n[1], col("ssd_cb", n[1]))
                else:
                    kind, pair = n[1] % 3, n[1] // 3
                    a = conv4(b, m, gT[n[1]], COLS["gdn_cw"] + 4 * (2 * kind + pair), None)
                tk[n] = a
            return use

        split_by[0] = GE
        bg.add(short_chain())
        bg.add(delta_chain())
        for j in range(0, 17, 2):
            feat_chunk(hT, [0, 1], in_use(j))

        def z_use(half):
            def use(i, b, m):
                a = act(zs[:, i, 256 * half:256 * half + 256], ps[b][:, 0:256], ACT.Silu, [m])
                put(b, a)
                tk["z", i, half] = a
            return use

        for half in range(2):
            e = tok_group(hH, hL, 8, hT, [0, 1, 0, 1], z_use(half))
        tk["proj"] = [e]
        bg.finish()
        split_by[0] = VE

        gdn_end = [t for q in mixed for t in q] + [tk["ssd out"], tk["gd out", 0], tk["gd out", 1]] + tk["og", 0] + tk["og", 1] + [f for q in y_free for f in q]

        def rms_residual(kt, lH, lL, ready, row_j, tmp, junk, free, then, between, middle=None, early=None):
            d_r = row(0, row_j, free)
            sq_, xt = {}, [None] * 4
            last_sq = [None]

            def square(i, h, b, m):
                at_ = 16 + 2 * i + h
                sq_[i, h] = (b, act(junk, ps[b][:, :], ACT.Square, [m, last_sq[0]] + free, accum=st[:, at_:at_ + 1]))
                last_sq[0] = sq_[i, h][1]

            more = [None]

            def use(i, b, m):
                g = more[0]
                if i == 3 and early is not None:
                    early()
                square(i, 1, b, m)
                go(g)
                a = tt(st[:, 24 + i:25 + i], st[:, 16 + 2 * i:17 + 2 * i], st[:, 17 + 2 * i:18 + 2 * i], ALU.add, [sq_[i, 0][1], sq_[i, 1][1]])
                a = act(st[:, 28 + i:29 + i], st[:, 24 + i:25 + i], ACT.Sqrt, [a], bias=col("eps6"), scale=1.0 / 1024)
                go(g)
                a = rec(st[:, 32 + i:33 + i], st[:, 28 + i:29 + i], [a])
                go(g)
                o = tmp[i % 2]
                r = []
                for h in range(2):
                    bk = sq_[i, h][0]
                    t = stt(o[:, 512 * h:512 * h + 512], ps[bk][:, :], st[:, 32 + i:33 + i], rows[0][:, 512 * h:512 * h + 512],
                            ALU.mult, ALU.mult, [a, d_r] + free + (xt[i - 2] if i > 1 else []))
                    put(bk, t)
                    r.append(t)
                xt[i] = [tt(x[:, i, :], x[:, i, :], o[:, :], ALU.add, r)]
                go_all(g)
                more[0] = then(i, xt[i], m)

            tok_group(lH, lL, kt, ready, [0, 1, 2, 3], lambda i, b, m: square(i, 0, b, m))
            if middle is not None:
                middle()
            last = tok_group(lH, lL, kt, ready, [4, 5, 6, 7], use, True, between)
            return xt, last, more[0]

        R = Region(BIG, TOP)
        xn = R([128, 4, 1024])
        tmp = [R([128, 1024]) for _ in range(2)]
        junk = [R([128, 1024]) for _ in range(2)]
        oneh = R([32, 384])
        rb = R([32, 8])
        uu = R([8, 384])
        d_g = row(1, 11, gdn_end)
        d1 = dma(oneh[:, :], ins["oneh"], gdn_end)
        d2 = dma(rb[:, :], ins["rel_bias_2"], gdn_end)
        d_u = []

        def bias_table():
            m = mm(ps[7][0:8, 0:384], rb[:, :], oneh[:, :], True, True, take(7) + [d1, d2], True)
            a = cpa(uu[:, :], ps[7][0:8, 0:384], [m] + gdn_end)
            put(7, a)
            d_u.append(dma(u_dram, uu[:, :], [a]))

        hT, t_rms, done = {}, {}, {}

        def ffn_norm(i, t, m):
            done[i] = m
            return rms_scale(i, xn[:, i, :], x[:, i, :], t, (1, d_g), gdn_end + ([t_rms[i - 1]] if i else []), junk[0][:, :], 0, t_rms)

        def turn_xn(i):
            return lambda: turn(i, xn[:, i, :], [t_rms[i]], [done[i]], hT)

        def both(f, g):
            f()
            g()

        xt, last, rms_3 = rms_residual(8, hH, hL, mixed, 0, tmp, junk[1][:, 0:512], gdn_end, ffn_norm,
                                {(3, 0): turn_xn(0)}, bias_table, turn_xn(1))

        R = Region(BIG, TOP)
        aH = R([128, 22, 512], F32R)
        aL = R([128, 22, 512], F32R)
        TMP = R.at
        ft = [R([128, 512]) for _ in range(6)]
        f_free = [[] for _ in range(6)]
        a_free = list(d_u)
        atoks = []

        def ffn_pair(t, b, m, m_tile, hold={}):
            if t == 0:
                s = m_tile % 2
                a = act(ft[s][:, :], ps[b][:, :], ACT.Silu, [m] + f_free[s])
                put(b, a)
                hold["g"] = a
            else:
                s = m_tile % 2
                a = tt(ft[2 + s][:, :], ft[s][:, :], ps[b][:, :], ALU.mult, [m, hold["g"]] + f_free[2 + s])
                put(b, a)
                f_free[s] = [a]
                h = act(aH[:, m_tile, :], ft[2 + s][:, :], ACT.Copy, [a] + a_free)
                l = tt(aL[:, m_tile, :], ft[2 + s][:, :], aH[:, m_tile, :].bitcast(F32), ALU.subtract, [a, h] + a_free, q=GE)
                f_free[2 + s] = [h, l]
                atoks.append([h, l])

        def last_turn():
            turn_xn(2)()
            go_all(rms_3)
            turn_xn(3)()
            a_free.append((PE.sem, PE.n))
            a_free.extend(t_rms.values())
            a_free.extend(t for u in xt for t in u)
            for f in f_free:
                f.extend(a_free)

        feat_lead(hT, [0, 1, 2, 3], lambda n, t, b, m: ffn_pair(t, b, m, n), last_turn)
        for m_tile in range(2, 22):
            feat_chunk(hT, [2 * (m_tile % 2), 2 * (m_tile % 2) + 1], lambda t, b, m, mt=m_tile: ffn_pair(t, b, m, mt))
        ft_end = [t for f in f_free for t in f]
        tmp = [at(TMP + 4096 * j, [128, 1024]) for j in range(2)]
        junk = at(TMP + 8192, [128, 512])
        hT, done, xtk = {}, {}, {}

        def keep(i, t, m):
            xtk[i], done[i] = t, m

        def turn_x(i):
            return lambda: turn(i, x[:, i, :], xtk[i], [done[i]], hT)

        xt, last, _ = rms_residual(22, aH, aL, atoks, 1, tmp, junk[:, :], ft_end, keep,
                                {(3, 0): lambda: both(turn_x(0), turn_x(1)), (3, 1): turn_x(2)})
        x_end = [t for u in xt for t in u]

        prev = [last] + x_end
        R = Region(BIG, TOP)
        ckvT = R([128, 512])
        far = R([128, 8])
        widx = R([128, 4, 8])
        Q0 = R.at
        qiT = [R([128, 512]) for _ in range(4)]
        kiT = R([128, 512])
        qaT = [R([128, 512]) for _ in range(4)]
        B0 = R.at
        QB = R([66, 8, 512])
        KB = R([66, 8, 512])
        vb = R([128, 4, 512])
        near = R([128, 8, 256])
        CM = R([128, 512])
        selm = R([128, 1152])
        wuk = R([128, 4, 128])
        wuv = R([128, 8, 64])
        anti = R([128, 128])
        C0 = R.at
        cf = R([8, 2, 512])
        otb = R([128, 4, 512])
        sco = R([128, 512])
        Pt = [R([128, 512]) for _ in range(2)]
        m8 = R([128, 8])
        sx2 = R([128, 6, 4])
        d_1q = dma(QB[64:65, :, :], ins["ones"].rearrange("p (h n) -> p h n", h=8), prev)
        d_1k = dma(KB[65:66, :, :], ins["ones"].rearrange("p (h n) -> p h n", h=8), prev)
        d_CM = dma(CM[:, :], ins["causal"], prev)
        d_wuk = dma(wuk[:, :, :], ins["wuk"].rearrange("p (a r) -> p a r", a=4), prev)
        d_wuv = dma(wuv[:, :, :], ins["wuv"].rearrange("p (a r) -> p a r", a=8), prev)
        d_anti = dma(anti[:, :], ins["anti"], prev)
        d_far = dma(far[:, :], ins["rel_bias_2"][31:32, :].partition_broadcast(128).rearrange("p a n -> p (a n)"), prev)
        toep = bass.AP(u_dram.tensor, 0, [[1, 128], [384, 8], [1, 256]])
        d_near = dma(near[:, :, :], toep, prev + d_u)

        f0, f1 = cf[:, 0, :], cf[:, 1, :]
        w0, w1, w2, wxT = (rows[j // 2][0:8, 512 * (j % 2):512 * (j % 2) + 512] for j in range(4))

        def small2(t, b, m):
            tk["f"] = ts(f0, ps[b][0:8, :], cols[0:8, COLS["b_f"]:COLS["b_f"] + 1], -1.0, ALU.add, ALU.mult, [m, d_cols] + prev)
            tk["wx"] = ts(wxT, ps[b][32:40, :], 8.0 ** -0.5, None, ALU.mult, after=[m] + prev)
            put(b, tk["f"], tk["wx"])

        def gates():
            after = take(7) + [tk["wx"], d_id]
            for i in range(4):
                m = tr(ps[7][:, 8 * i:8 * i + 8], wxT[:, 128 * i:128 * i + 128], after, i == 3)
                after = []
            tk["widx"] = cpa(widx[:, :, :], ps[7][:, 0:32].rearrange("p (i h) -> p i h", h=8), [m] + prev)
            put(7, tk["widx"])
            t = tk["f"]
            a = stt(w0, f0, -1.0, f0, ALU.mult, ALU.max, [t] + prev)
            a = act(w0, w0, ACT.Exp, [a], scale=-1.0)
            b = ts(w1, w0, 1.0, None, ALU.add, after=[a])
            c = act(w2, w1, ACT.Ln, [b])
            yield
            b = ts(w1, w1, -1.0, 1e-30, ALU.add, ALU.max, [b, c])
            d = rec(f1, w1, [b])
            d = tt(f1, f1, w2, ALU.mult, [d, c])
            d = tt(f1, f1, w0, ALU.mult, [d])
            b = ts(w1, w1, 1e-30, None, ALU.is_equal, after=[d])
            b = tt(w1, w1, w0, ALU.mult, [b])
            d = tt(f1, f1, w1, ALU.add, [d, b])
            d = stt(f1, f0, 0.0, f1, ALU.max, ALU.add, [d])
            yield
            b = mset(w1, 1.0, [b])
            d = VE.add(lambda e: e.tensor_tensor_scan(f0, w1, f1, 0.0, ALU.mult, ALU.add), [d, b], True, 1100)
            d2 = ts(f1, f0, -1.0, None, ALU.mult, after=[d])
            tk["gates"] = [d2, c, m]
            tk["dq"] = dma(QB[65:66, :, :], f1, prev + [d2])
            tk["dk"] = dma(KB[64:65, :, :], f0, prev + [d])
            yield

        sel_at = [0, 0, 256, 640]
        t_sel = [d_CM, None, None, None]

        def index():
            while ("ki" not in tk) or ("dk" not in tk):
                yield
            rel = [at(C0 + 2048 * j, [128, 512]) for j in range(2)]
            rel_free = [[tk["dq"], tk["dk"]], [tk["dq"], tk["dk"]]]
            done = []
            n_r = 0
            for i in range(1, 4):
                n = 128 * (i + 1)
                acc = None
                for h in range(8):
                    r = n_r % 2
                    s = slice(64 * (h % 2), 64 * (h % 2) + 64)
                    m = mm(ps[7][:, 0:n], qiT[h // 2][s, 128 * i:128 * i + 128], kiT[s, 0:n], True, True,
                           take(7) + [tk["qi", h // 2], tk["ki"]], True)
                    a = act(rel[r][:, 0:n], ps[7][:, 0:n], ACT.Relu, [m] + rel_free[r])
                    put(7, a)
                    prior = CM[:, 512 - n:512] if h == 0 else sco[:, 0:n]
                    acc = stt(sco[:, 0:n], rel[r][:, 0:n], widx[:, i, h:h + 1], prior, ALU.mult, ALU.add,
                              [a, tk["widx"], d_CM] + (prev + done if h == 0 else [acc]))
                    rel_free[r] = [acc]
                    n_r += 1
                    yield
                t = acc
                for q in range(16):
                    t = VE.add(lambda e, n=n: e.max(m8[:, :], sco[:, 0:n]), [t], True, 70 + 1.05 * n)
                    t = VE.add(lambda e, n=n: e.match_replace(sco[:, 0:n], m8[:, :], sco[:, 0:n], TAKEN), [t], True, 70 + 1.05 * n)
                    yield
                t = ts(selm[:, sel_at[i]:sel_at[i] + n], sco[:, 0:n], TAKEN / 2, NEG, ALU.is_gt, ALU.mult, [t] + prev)
                done = [t]
                t_sel[i] = t
            tk["index"] = [t]
            yield

        Pt_free = [list(prev), list(prev)]
        masked = {}

        def units(todo, slots, slot_free, look, scores, product, out, there=lambda h: True):
            NS = len(slots)
            masked_at, soft, sums, turned = {}, {}, {}, {}
            outs = tk[out.name] = {}

            def first(n):
                h, i = todo[n]
                w = 128 * (i + 1)
                s, b = n % NS, 2 + n % 2
                m, mask, need = scores(h, i, b)
                mx = sx2[:, s, 0:1]
                t = VE.add(lambda e, o=slots[s][:, 0:w], a=ps[b][:, 0:w], k=mask, c=mx:
                           e.tensor_tensor_reduce(o, a, k, 1.0, 2 * NEG, ALU.add, ALU.max, c), [m] + need + slot_free[s], True, 70 + 1.05 * w)
                put(b, t)
                masked[h, i] = t
                masked_at[n] = ts(mx, mx, -1.0, None, ALU.mult, after=[t])

            def exps(n):
                h, i = todo[n]
                w = 128 * (i + 1)
                s = n % NS
                soft[n] = act(slots[s][:, 0:w], slots[s][:, 0:w], ACT.Exp, [masked_at[n]], bias=sx2[:, s, 0:1], accum=sx2[:, s, 1:2])

            def second(n):
                h, i = todo[n]
                w = 128 * (i + 1)
                s, p, b = n % NS, n % 2, 4 + n % 2
                after = take(b) + [soft[n]]
                for j in range(i + 1):
                    m = tr(ps[b][:, 128 * j:128 * j + 128], slots[s][:, 128 * j:128 * j + 128], after, j == i)
                    after = []
                slot_free[s] = [m]
                sums[n] = rec(sx2[:, s, 2:3], sx2[:, s, 1:2], [soft[n]])
                turned[n] = cpa(Pt[p][:, 0:w], ps[b][:, 0:w], [m] + Pt_free[p])
                put(b, turned[n])

            def third(n):
                h, i = todo[n]
                s, p = n % NS, n % 2
                b, v, need = product(h, n)
                after = [turned[n]] + need + take(b)
                for j in range(i + 1):
                    m = mm(ps[b][:, 0:64], Pt[p][:, 128 * j:128 * j + 128], v[:, j, 64 * h:64 * h + 64], j == 0, j == i, after, j == i)
                    after = []
                Pt_free[p] = [m]
                t = act(out[:, i, 64 * h:64 * h + 64], ps[b][:, 0:64], ACT.Copy, [m, sums[n]] + prev, scale=sx2[:, s, 2:3])
                put(b, t)
                slot_free[s] = slot_free[s] + [t]
                outs[i] = t

            N = len(todo)
            for n in range(-look, N):
                if n + look < N:
                    while not there(todo[n + look][0]):
                        yield
                    first(n + look)
                    yield
                if 0 <= n + look - 1 < N:
                    exps(n + look - 1)
                if 0 <= n + 1 < N:
                    second(n + 1)
                    yield
                if n >= 0:
                    third(n)
                    yield

        def scores_b(h, i, b):
            w = 128 * (i + 1)
            m = mm(ps[b][:, 0:w], QB[:, h, 128 * i:128 * i + 128], KB[:, h, 0:w], True, True,
                   take(b) + [tk["QB", h], tk["KB", h], tk["dq"], tk["dk"], d_1q, d_1k], True)
            return m, CM[:, 512 - w:512], [d_CM]

        def product_b(h, n):
            return 6 + n % 2, vb, [tk["vb", j, h // 4] for j in range(4)]

        rows4 = [rows[j // 2][:, 512 * (j % 2):512 * (j % 2) + 512] for j in range(4)]
        rows_free = [None] * 4

        def forget_attention():
            while "dk" not in tk:
                yield
            for j in range(4):
                rows_free[j] = prev + tk["gates"]
            todo = [(h, i) for h in range(8) for i in range(4)]
            for _ in units(todo, rows4, rows_free, 3, scores_b, product_b, otb,
                           lambda h: ("QB", h) in tk and ("KB", h) in tk and "dk" in tk):
                yield

        def evac2(name, dst, scale=None):
            def use(b, m):
                tk[name] = act(dst[:, :], ps[b][:, :], ACT.Copy, [m] + prev, scale=scale)
                put(b, tk[name])
            return use

        def evac_heads(name, dst, j, scale=None):
            def use(b, m):
                for h in range(2):
                    o, i = dst[0:64, 2 * j + h, :], ps[b][64 * h:64 * h + 64, :]
                    if h == 0:
                        t = act(o, i, ACT.Copy, [m] + prev, scale=scale)
                    else:
                        t = ts(o, i, 1.0 if scale is None else scale, None, ALU.mult, after=[m] + prev)
                    tk[name, 2 * j + h] = t
                    put(b, t)
            return use

        def two(a, b):
            feat_chunk(hT, [0, 1], lambda t, bk, m: (a, b)[t](bk, m))

        split_by[0] = GE
        for half in range(2):
            def vb_use(i, b, m, half=half):
                tk["vb", i, half] = cpa(vb[:, i, 256 * half:256 * half + 256], ps[b][:, 0:256], [m] + prev)
                put(b, tk["vb", i, half])

            tok_group(hH, hL, 8, hT, [0, 1, 0, 1], vb_use, True, {} if half else {(1, 0): turn_x(3)})
        feat_chunk(hT, [0], small2)
        bg.add(gates())
        bg.add(index())
        for j in range(2):
            two(evac2(("qi", 2 * j), qiT[2 * j], 0.125), evac2(("qi", 2 * j + 1), qiT[2 * j + 1], 0.125))
        two(evac2("ckvT", ckvT), evac2("ki", kiT))
        bg.add(forget_attention())
        for j in range(4):
            two(evac_heads("QB", QB, j, 0.125), evac_heads("KB", KB, j))
        for j in range(2):
            two(evac2(("qa", 2 * j), qaT[2 * j]), evac2(("qa", 2 * j + 1), qaT[2 * j + 1]))
        ht_free = [(PE.sem, PE.n)]
        bg.finish()
        split_by[0] = VE
        RQ = Region(Q0, Q0 + 8192)
        ql = [RQ([128, 512]) for _ in range(2)]
        ql_free = [list(tk["index"]) for _ in range(2)]
        ql_tok = {}
        RQ = Region(B0, B0 + 16384)
        mb = [RQ([128, 1280]) for _ in range(2)]
        RQ = Region(B0 + 16384, B0 + 32768)
        va = RQ([128, 4, 512])
        ota = RQ([128, 4, 512])
        mb_at = [0, 128, 384, 768]
        masked.clear()
        mb_tok = {}
        b_end = [(PE.sem, PE.n)]
        far_tok = [cpv(mb[r][:, mb_at[i]:mb_at[i] + 128 * (i - 1)], selm[:, sel_at[i]:sel_at[i] + 128 * (i - 1)],
                       [t_sel[i]] + b_end, q=GE) for r in range(2) for i in (2, 3)]

        def latent(h):
            r = slice(64 * (h % 2), 64 * (h % 2) + 64)
            m = mm(ps[0][:, :], wuk[r, h // 2, :], qaT[h // 2][r, :], True, True, take(0) + [d_wuk, tk["qa", h // 2]], True)
            ql_tok[h] = act(ql[h % 2][:, :], ps[0][:, :], ACT.Copy, [m] + ql_free[h % 2], scale=0.125)
            put(0, ql_tok[h])
            m = mm(ps[1][:, 0:256], anti[:, :], near[:, h, :], True, True, take(1) + [d_near, d_anti], True)
            for i in range(4):
                n = min(128 * (i + 1), 256)
                at_ = mb_at[i] + 128 * (i + 1) - n
                mask = CM[:, 384:512] if i == 0 else selm[:, sel_at[i] + 128 * (i + 1) - n:sel_at[i] + 128 * (i + 1)]
                mb_tok[h, i] = stt(mb[h % 2][:, at_:at_ + n], ps[1][:, 256 - n:256], far[:, h:h + 1], mask, ALU.subtract, ALU.add,
                                   [m, d_far, d_CM, t_sel[i]] + b_end + [masked.get((h - 2, i))])
            put(1, mb_tok[h, 3])

        def scores_a(h, i, b):
            w = 128 * (i + 1)
            if i == 0 and h == 0:
                latent(0)
            if i == 1 and h < 7:
                latent(h + 1)
            m = mm(ps[b][:, 0:w], ql[h % 2][:, 128 * i:128 * i + 128], ckvT[:, 0:w], True, True, take(b) + [ql_tok[h], tk["ckvT"]], True)
            if i == 3:
                ql_free[h % 2] = [m]
            return m, mb[h % 2][:, mb_at[i]:mb_at[i] + w], [mb_tok[h, i]] + far_tok

        def product_a(h, n):
            return 6 + n % 2, va, [tk["va", j] for j in range(4)]

        for j in range(4):
            m = mm(ps[7][:, :], ckvT[:, 128 * j:128 * j + 128], wuv[:, :, :], True, True, take(7) + [tk["ckvT"], d_wuv], True)
            tk["va", j] = cpa(va[:, j, :], ps[7][:, :], [m] + b_end)
            put(7, tk["va", j])
        todo = [(h, i) for h in range(8) for i in range(4)]
        slots = rows4 + [at(C0 + 2048 * j, [128, 512])[:, :] for j in range(2)]
        for _ in units(todo, slots, rows_free + [tk["index"], tk["index"]], 4, scores_a, product_a, ota):
            pass
        mixed = {}
        for j, o in ((1, otb), (0, ota)):
            for i in range(4):
                turn(i, o[:, i, :], [tk[o.name][i]], ht_free, mixed, (j,))
        att_end = [(PE.sem, PE.n), (VE.sem, VE.n), (SE.sem, SE.n)]
        x_end = x_end + att_end

        def ln_stage(n, kt, lH, lL, ready, want_ht=True, store=None):
            r_g, r_b = row(0, 2 + n, x_end), row(1, 6 + n, x_end)
            toks = [[] for _ in range(4)]
            xt, done, hT = [None] * 4, {}, {}

            def half(i, h, b, m):
                xv = x[:, i, 512 * h:512 * h + 512]
                t = stt(xv, xv, ALPHA, ps[b][:, :], ALU.mult, ALU.add, [m] + x_end)
                put(b, t)
                at_ = 12 * i + 6 * h
                toks[i].append(VE.add(lambda e: e.bn_stats(st[:, at_:at_ + 6], xv), [t], True, 600))

            def use(i, b, m):
                done[i] = m
                half(i, 1, b, m)
                mv, sd, rs = st[:, 48 + 2 * i:50 + 2 * i], st[:, 56 + i:57 + i], st[:, 60 + i:61 + i]
                sl = st[:, 12 * i:12 * i + 12].rearrange("p (h c) -> p h c", h=2)
                a = VE.add(lambda e: e.bn_aggr(mv, sl), toks[i])
                s = act(sd, mv[:, 1:2], ACT.Sqrt, [a, d_cols], bias=col("eps5"))
                a = stt(x[:, i, :], x[:, i, :], mv[:, 0:1], rows[0][:, :], ALU.subtract, ALU.mult, [a, r_g])
                s = rec(rs, sd, [s])
                xt[i] = [stt(x[:, i, :], x[:, i, :], rs, rows[1][:, :], ALU.mult, ALU.add, [a, s, r_b])]
                if store is not None:
                    store(i, xt[i])

            def turn_x(i):
                return lambda: turn(i, x[:, i, :], xt[i], [done[i]], hT)

            tok_group(lH, lL, kt, ready, [0, 1, 2, 3], lambda i, b, m: half(i, 0, b, m))
            between = {(3, 0): lambda: both(turn_x(0), turn_x(1)), (3, 1): turn_x(2)} if want_ht else {}
            last = tok_group(lH, lL, kt, ready, [4, 5, 6, 7], use, True, between)
            return hT, xt, last, turn_x(3)

        hT, xt, last, turn3 = ln_stage(0, 8, hH, hL, mixed)
        x_end = [t for u in xt for t in u]

        def conv_ffn(layer, hT, turn3, big_free):
            R = Region(BIG, TOP)
            aH = R([128, 22, 512], F32R)
            aL = R([128, 22, 512], F32R)
            ft = [R([128, 512]) for _ in range(6)]
            f_free = [list(big_free) for _ in range(6)]
            atoks = []
            hold = {}
            cw = COLS[f"fcw{layer}"]

            def pair(t, b, m, mt):
                s = 2 * (mt % 2) + t
                w = cw + 3 * (mt + 22 * t)
                y = ft[s]
                a = act(y[:, :], ps[b][:, :], ACT.Identity, [m, d_cols] + f_free[s], scale=cols[:, w + 2:w + 3])
                for d in range(1, 3):
                    a = stt(y[:, d:512], ps[b][:, 0:512 - d], cols[:, w + 2 - d:w + 3 - d], y[:, d:512], ALU.mult, ALU.add, [a])
                put(b, a)
                if t == 0:
                    hold["g"] = act(y[:, :], y[:, :], ACT.Silu, [a])
                else:
                    g = ft[s - 1]
                    o = ft[4 + mt % 2]
                    a = tt(o[:, :], g[:, :], y[:, :], ALU.mult, [a, hold["g"]] + f_free[4 + mt % 2])
                    f_free[s - 1], f_free[s] = [a], [a]
                    h = act(aH[:, mt, :], o[:, :], ACT.Copy, [a] + big_free)
                    l = tt(aL[:, mt, :], o[:, :], aH[:, mt, :].bitcast(F32), ALU.subtract, [a, h] + big_free, q=GE)
                    f_free[4 + mt % 2] = [h, l]
                    atoks.append([h, l])

            feat_lead(hT, [0, 1, 2, 3], lambda n, t, b, m: pair(t, b, m, n), turn3)
            for mt in range(2, 22):
                feat_chunk(hT, [2 * (mt % 2), 2 * (mt % 2) + 1], lambda t, b, m, mt=mt: pair(t, b, m, mt))
            return aH, aL, atoks

        aH, aL, atoks = conv_ffn(0, hT, turn3, att_end + [last])
        hT, xt, last, turn3 = ln_stage(1, 22, aH, aL, atoks)
        x_end = [t for u in xt for t in u]

        prev = [last]
        R = Region(BIG, TOP)
        v1 = R([128, 4, 512])
        vsq = R([128, 4, 512])
        sgg = R([128, 512])
        sgw = R([128, 8, 128])
        sgb = R([1, 1024])
        vst = R([128, 4, 32])
        gcT = [R([128, 516]) for _ in range(2)]
        yc = [R([128, 512]) for _ in range(4)]
        uT = [R([128, 512]) for _ in range(4)]
        od = [R([128, 512]) for _ in range(4)]
        d_sgg = dma(sgg[:, :], ins["sgg"].partition_broadcast(128).rearrange("p a n -> p (a n)"), prev)
        d_sgw = dma(sgw[:, :, :], ins["sgw"].rearrange("p (g t) -> p g t", g=8), prev)
        d_sgb = dma(sgb[:, :], ins["sgb"], prev)
        t_sgw = tt(sgw[:, :, :], sgw[:, :, :], U[:, :].unsqueeze(1).broadcast_to([128, 8, 128]), ALU.mult, [d_sgw, d_U], q=GE)

        def v_use(i, b, m):
            tk["v", i] = act(v1[:, i, :], ps[b][:, :], ACT.Gelu_apprx_tanh, [m] + prev)
            put(b, tk["v", i])

        tok_group(hH, hL, 8, hT, [0, 1, 2, 3], v_use, True, {(1, 1): turn3})

        t_v = []

        def v_norm():
            for i in range(4):
                v = h64(v1[:, i, :])
                mu, var = vst[:, i, 0:8], vst[:, i, 8:16]
                t = red(mu, v, ALU.add, [tk["v", i]] + prev)
                t = ts(mu, mu, 1.0 / 64, None, ALU.mult, after=[t])
                t = tt(v, v, bc64(mu), ALU.subtract, [t])
                u = tt(vsq[:, i, :], v1[:, i, :], v1[:, i, :], ALU.mult, [t] + prev, q=GE)
                yield
                tk["var", i] = red(var, h64(vsq[:, i, :]), ALU.add, [u])
                yield
            a = act(vst[:, :, 16:24], vst[:, :, 8:16], ACT.Sqrt, [tk["var", i] for i in range(4)], bias=col("eps5"), scale=1.0 / 64)
            a = rec(vst[:, :, 24:32], vst[:, :, 16:24], [a])
            for i in range(4):
                t = tt(h64(v1[:, i, :]), h64(v1[:, i, :]), bc64(vst[:, i, 24:32]), ALU.mult, [a])
                t_v.append(tt(v1[:, i, :], v1[:, i, :], sgg[:, :], ALU.mult, [t, d_sgg]))
                yield

        gc_free = [list(prev), list(prev)]
        hold = {}

        def gcz(j):
            def use(t, b, m):
                s = j % 2
                if t == 0:
                    hold["gc"] = cpa(gcT[s][:, 0:512], ps[b][:, :], [m] + gc_free[s])
                    put(b, hold["gc"])
                else:
                    g = gcT[s]
                    a = tt(g[:, 0:512], g[:, 0:512], ps[b][:, :], ALU.mult, [m, hold["gc"]])
                    put(b, a)
                    w = COLS["od_cw"] + 3 * j
                    y = yc[j]
                    c = act(y[:, :], g[:, 0:512], ACT.Identity, [a, d_cols] + prev, scale=cols[:, w + 2:w + 3])
                    for d in range(1, 3):
                        c = stt(y[:, d:512], g[:, 0:512 - d], cols[:, w + 2 - d:w + 3 - d], y[:, d:512], ALU.mult, ALU.add, [c])
                    gc_free[s] = [c]
                    tk["yc", j] = c
            return use

        bg.add(v_norm())
        for j in range(4):
            feat_chunk(hT, [4 + 2 * (j % 2), 5 + 2 * (j % 2)], gcz(j))

        def gb_use(jj):
            def use(t, b, m):
                j = jj + t
                tk["od", j] = tt(od[j][:, :], yc[j][:, :], ps[b][:, :], ALU.mult, [m, tk["yc", j]] + prev)
                put(b, tk["od", j])
            return use

        for j in range(0, 4, 2):
            feat_chunk(hT, [4 + j, 5 + j], gb_use(j))

        def u_use(jj):
            def use(t, b, m):
                j = jj + t
                tk["u", j] = act(uT[j][:, :], ps[b][:, :], ACT.Gelu_apprx_tanh, [m] + prev)
                put(b, tk["u", j])
            return use

        for j in range(0, 4, 2):
            e = feat_chunk(hT, [4 + j, 5 + j], u_use(j))
        bg.finish()
        ht_free = [e]
        mixed = [None] * 8
        for j in range(4):
            mixed[4 + j] = split_ht(4 + j, od[j][:, :], [tk["od", j]], ht_free)
            b = j
            after = take(b) + [t_sgw, d_sgb, t_ones] + t_v
            for n in range(4):
                for g in (2 * j, 2 * j + 1):
                    o = ps[b][64 * (g % 2):64 * (g % 2) + 64, 128 * n:128 * n + 128]
                    mm(o, v1[:, n, 64 * g:64 * g + 64], sgw[:, g, :], True, False, after)
                    after = []
                    m = mm(o, ones[0:1, 0:64], sgb[0:1, 128 * g:128 * g + 128], False, True, (), n == 3 and g % 2 == 1)
            t = tt(uT[j][:, :], uT[j][:, :], ps[b][:, :], ALU.mult, [m, tk["u", j]])
            put(b, t)
            mixed[j] = split_ht(j, uT[j][:, :], [t], ht_free)
        odd_end = [t for q in mixed for t in q] + [m]

        hT, xt, last, turn3 = ln_stage(2, 8, hH, hL, mixed)
        x_end = [t for u in xt for t in u]
        aH, aL, atoks = conv_ffn(1, hT, turn3, odd_end + [last])
        stores = []

        def store(i, t):
            stores.append(dma(out[0, 128 * i:128 * i + 128, :], x[:, i, :], t))

        ln_stage(3, 22, aH, aL, atoks, False, store)
        SP.items.append((stores + d_u, lambda e: None, False))

        block = ctx.enter_context(nc.Block())

        @block.sync
        def _(e):
            SP.emit(e)

        @block.gpsimd
        def _(e):
            GE.emit(e)

        @block.scalar
        def _(e):
            SE.emit(e)

        @block.vector
        def _(e):
            VE.emit(e)

        @block.tensor
        def _(e):
            PE.emit(e)


def shape_constants():
    f = np.float32
    i, j = np.arange(128)[:, None], np.arange(128)[None, :]
    out = {"ident": np.eye(128, dtype=f), "anti": np.eye(128, dtype=f)[::-1], "triu": (i <= j).astype(f)}
    r, c = np.arange(128)[:, None], np.arange(256)[None, :]
    ok = ((c // 64) >= (r // 64)) & ((c // 64) <= (r // 64) + 2)
    dist = np.abs(r + 128 - c)
    out["abias"] = np.concatenate([np.where(ok, -(2.0 ** (-8.0 * h / 4)) * dist, NEG) for h in range(1, 5)], axis=1).astype(f)
    levels = [((i // b) % 2 == 1) & ((j // b) == (i // b) - 1) for b in (1, 2, 4, 8, 16, 32, 64)]
    out["levels"] = np.concatenate([levels[0].T] + levels[1:], axis=1).astype(f)
    out["causal"] = np.where(384 + i - np.arange(512)[None, :] >= 0, 0.0, NEG).astype(f)
    n = np.maximum(255 - np.arange(384), 0)
    large = 16 + (np.log(np.maximum(n, 1) / 16) / math.log(128 / 16) * 16).astype(np.int64)
    bucket = np.where(n < 16, n, np.minimum(large, 31))
    out["oneh"] = (np.arange(32)[:, None] == bucket[None, :]).astype(f)
    out["ones"] = np.ones((1, 4096), f)
    return out


def kernel(**inputs):
    import concourse.bacc as bacc
    from concourse.bass_utils import run_bass_kernel_spmd

    a = {k: np.asarray(v) for k, v in inputs.items()}
    chunks = []
    for name, layer, k0, nk, cols in weight_plan():
        if name == "gate_up":
            w = np.concatenate([a[n][0][:, 128 * cols:128 * cols + 128] for n in ("ffn_w_gate", "ffn_w_up")], axis=1)
        else:
            w = a[name][layer][128 * k0:128 * (k0 + nk)]
            if cols == rng(cols[0], len(cols)):
                w = w[:, cols[0]:cols[0] + len(cols)]
            else:
                w = w[:, np.array(cols)]
        chunks.append(w.reshape(nk, 128, -1).transpose(1, 0, 2).reshape(-1))
    arrays = {"wbig": np.concatenate(chunks), "x": a["x"], "rel_bias_2": a["rel_bias_2"]}

    def tiles(v):
        return v.reshape(-1, 128).T

    def taps_(w):
        k, n = w.shape
        return w.reshape(k, n // 128, 128).transpose(2, 1, 0).reshape(128, -1)

    eps = np.full((128, 1), 1e-6, np.float32), np.full((128, 1), 1e-5, np.float32)
    bf = np.concatenate([a["ev_b_f_2"][0], np.zeros(120, np.float32)])[:, None]
    parts = [taps_(a["ssd_conv_w"][0]), tiles(a["ssd_conv_b"][0]),
             taps_(a["gdn_conv_w"][0]), np.concatenate([a["gdn_norm_w"][0]] * 2)[:, None],
             taps_(a["od_conv_w_2"][0]), bf, *eps,
             taps_(a["ffn_conv_w_2"][0]), taps_(a["ffn_conv_w_2"][1])]
    arrays["cols"] = np.ascontiguousarray(np.concatenate(parts, axis=1))
    arrays["rows"] = np.concatenate([a["post_mix_norm"], a["post_ffn_norm"], a["ln_g_2"].reshape(4, 1024), a["ln_b_2"].reshape(4, 1024),
                                     a["pre_mix_norm"], a["pre_ffn_norm"]], axis=0)
    arrays["brow"] = np.concatenate([a["ssd_dt_bias"][0], a["gdn_dt_bias"][0], a["ssd_A_log"][0], a["gdn_A_log"][0],
                                     a["attn_sinks"][0], a["ssd_D"][0], np.zeros(12, np.float32)])[None, :]
    arrays["ssd_nw"] = a["ssd_norm_w"]
    arrays["wuk"] = np.ascontiguousarray(a["ev_w_uk_2"][0].reshape(4, 2, 128, 64).transpose(1, 3, 0, 2).reshape(128, 512))
    arrays["wuv"] = np.ascontiguousarray(a["ev_w_uv_2"][0].transpose(1, 0, 2).reshape(128, 512))
    arrays["sgg"] = a["od_sgu_g_2"].reshape(1, 512)
    arrays["sgw"] = np.ascontiguousarray(a["od_sgu_w_2"][0].transpose(2, 0, 1).reshape(128, 1024))
    arrays["sgb"] = a["od_sgu_b_2"].reshape(1, 1024)
    arrays.update(shape_constants())
    arrays = {k: np.ascontiguousarray(v) for k, v in arrays.items()}

    nc = bacc.Bacc("TRN2", target_bir_lowering=False, num_devices=1)
    ins = {k: nc.dram_tensor("in_" + k, v.shape, mybir.dt.from_np(v.dtype), kind="ExternalInput").ap() for k, v in arrays.items()}
    out = nc.dram_tensor("out_0", (1, 512, 1024), F32, kind="ExternalOutput").ap()
    build(nc, ins, out)
    r = run_bass_kernel_spmd(nc, [{"in_" + k: v for k, v in arrays.items()}], core_ids=[0])
    return r.results[0]["out_0"]
```
